# Optimizing a Trainium2 kernel written in Bass

```python
import math
import jax
import jax.numpy as jnp
from jax import lax
import numpy as np

D_MODEL = 1024
BATCH = 1
SEQ = 128
DEPTH = 2
DEC_BATCH = 1
DEC_SEQ = 512
PAST_LEN = 128

GRID_W = 64
N_AB_LAYERS = (DEPTH + 1) // 2
N_CD_LAYERS = DEPTH // 2
MIX_WIDTH = D_MODEL
HEAD_DIM = 64
ROPE_THETA = 10000.0
RMS_EPS = 1e-6
Q_BLOCK = 128
CONV_W = 4
CONV_LEFT = 2
CONV_RIGHT = CONV_W - 1 - CONV_LEFT
LRU_WIDTH = MIX_WIDTH // 2
LRU_BLOCKS = 8
LRU_BW = LRU_WIDTH // LRU_BLOCKS
LRU_C = 8.0
DIFF_HEADS = (MIX_WIDTH // 2) // (2 * HEAD_DIM)
DIFF_QK = DIFF_HEADS * 2 * HEAD_DIM
DIFF_V = DIFF_HEADS * 2 * HEAD_DIM
IN_AB = 2 * LRU_WIDTH + 2 * DIFF_QK + DIFF_V
DELTA_HEADS = 4
DELTA_DK = (MIX_WIDTH // 2) // DELTA_HEADS
DELTA_DV = DELTA_DK
DELTA_WIDTH = DELTA_HEADS * DELTA_DV
DELTA_CONV_CH = 2 * DELTA_HEADS * DELTA_DK + DELTA_WIDTH
DELTA_CHUNK = 64
GQA_HEADS = (MIX_WIDTH // 2) // HEAD_DIM
GQA_KV_HEADS = 2
GQA_GROUP = GQA_HEADS // GQA_KV_HEADS
GQA_WIDTH = GQA_HEADS * HEAD_DIM
IN_CD = DELTA_CONV_CH + DELTA_WIDTH + 4 * DELTA_HEADS + GQA_WIDTH + 2 * GQA_KV_HEADS * HEAD_DIM
N_EXPERTS = 16
EC_CAPACITY_FACTOR = 2
EXPERT_FF = D_MODEL // 2

kernel_name = 'hybrid_diffusion_lru_diffattn_deltanet_gqa_ec'

def rms_norm(x, g):
    xf = x.astype(jnp.float32)
    y = xf * lax.rsqrt(jnp.mean(xf * xf, axis=-1, keepdims=True) + RMS_EPS)
    return (y * g.astype(jnp.float32)).astype(x.dtype)

def l2_normalize(x):
    return x * lax.rsqrt(jnp.sum(x * x, axis=-1, keepdims=True) + 1e-6)

def split_last(x, sizes):
    out, start = [], 0
    for s in sizes:
        out.append(x[..., start:start + s])
        start += s
    return out

def axial_rope_tables(n_tokens, head_dim):
    rows = n_tokens // GRID_W
    row = jnp.repeat(jnp.arange(rows, dtype=jnp.float32), GRID_W)
    col = jnp.tile(jnp.arange(GRID_W, dtype=jnp.float32), rows)
    quarter = head_dim // 4
    inv_freq = ROPE_THETA ** (-jnp.arange(quarter, dtype=jnp.float32) / quarter)
    ang = jnp.concatenate([row[:, None] * inv_freq, col[:, None] * inv_freq], axis=-1)
    return jnp.cos(ang), jnp.sin(ang)

def apply_rope(x, cos, sin):
    half = x.shape[-1] // 2
    shape = (1, cos.shape[0]) + (1,) * (x.ndim - 3) + (half,)
    c = cos.reshape(shape)
    s = sin.reshape(shape)
    x1, x2 = x[..., :half], x[..., half:]
    return jnp.concatenate([x1 * c - x2 * s, x2 * c + x1 * s], axis=-1)

def centred_depthwise_conv(x, w):
    T = x.shape[1]
    xp = jnp.pad(x, ((0, 0), (CONV_LEFT, CONV_RIGHT), (0, 0)))
    y = xp[:, 0:T] * w[0]
    for tap in range(1, CONV_W):
        y = y + xp[:, tap:tap + T] * w[tap]
    return y

def sweep_query_blocks(block_fn, q):
    B, T = q.shape[:2]
    qb_len = min(Q_BLOCK, T)
    nb = T // qb_len
    qb = jnp.moveaxis(q.reshape((B, nb, qb_len) + q.shape[2:]), 1, 0)
    out = jnp.moveaxis(lax.map(block_fn, qb), 0, 1)
    return out.reshape((B, T) + out.shape[3:])

def linear_recurrence(a, b, h0):
    def combine(left, right):
        return left[0] * right[0], right[0] * left[1] + right[1]
    a_cum, b_cum = lax.associative_scan(combine, (a, b), axis=1)
    return a_cum * h0[:, None, :] + b_cum

def rglru_coeffs(u, w_a, b_a, w_i, b_i, lam):
    B, T, W = u.shape
    ub = u.reshape(B, T, LRU_BLOCKS, LRU_BW)
    r = jax.nn.sigmoid(jnp.einsum('btnc,ncd->btnd', ub, w_a).reshape(B, T, W) + b_a)
    i = jax.nn.sigmoid(jnp.einsum('btnc,ncd->btnd', ub, w_i).reshape(B, T, W) + b_i)
    log_a = -LRU_C * r * jax.nn.softplus(-lam)
    a = jnp.exp(log_a)
    b = jnp.sqrt(-jnp.expm1(2.0 * log_a)) * (i * u)
    return a, b

def rglru_mixer(xa, ga, conv_w, conv_b, w_a, b_a, w_i, b_i, lam, h0):
    u = centred_depthwise_conv(xa, conv_w) + conv_b
    a_f, b_f = rglru_coeffs(u, w_a[0], b_a[0], w_i[0], b_i[0], lam[0])
    h_f = linear_recurrence(a_f, b_f, h0[:, 0])
    a_b, b_b = rglru_coeffs(u, w_a[1], b_a[1], w_i[1], b_i[1], lam[1])
    h_b = jnp.flip(linear_recurrence(jnp.flip(a_b, 1), jnp.flip(b_b, 1), h0[:, 1]), 1)
    y = (h_f + h_b) * jax.nn.gelu(ga)
    return y, jnp.stack([h_f[:, -1], h_b[:, 0]], axis=1)

def diff_attention_block(qb, k, v, lam):
    s = jnp.einsum('bqhcd,bkhcd->bhcqk', qb, k) * HEAD_DIM ** -0.5
    p = jax.nn.softmax(s, axis=-1)
    a = p[:, :, 0] - lam * p[:, :, 1]
    return jnp.einsum('bhqk,bkhe->bqhe', a, v)

def chunk_gated_delta_rule(q, k, v, beta, g, s0):
    B, T, H, dk = q.shape
    dv = v.shape[-1]
    C = DELTA_CHUNK
    n = T // C

    def chunks(x):
        x = x.reshape((B, n, C, H) + x.shape[3:])
        return jnp.moveaxis(jnp.swapaxes(x, 2, 3), 1, 0)

    q, k, v, beta, g = (chunks(t) for t in (q, k, v, beta, g))
    G = jnp.cumsum(g, axis=-1)
    incl = jnp.tril(jnp.ones((C, C), dtype=bool))
    strict = jnp.tril(jnp.ones((C, C), dtype=bool), -1)
    decay = jnp.exp(jnp.where(incl, G[..., :, None] - G[..., None, :], -jnp.inf))
    kb = k * beta[..., None]
    a = jnp.where(strict, jnp.einsum('nbhid,nbhjd->nbhij', kb, k) * decay, 0.0)
    m = a + jnp.eye(C, dtype=a.dtype)
    rhs = jnp.concatenate([kb * jnp.exp(G)[..., None], v * beta[..., None]], axis=-1)
    sol = lax.linalg.triangular_solve(m, rhs, left_side=True, lower=True, unit_diagonal=True)
    w, u = sol[..., :dk], sol[..., dk:]
    qk = jnp.where(incl, jnp.einsum('nbhid,nbhjd->nbhij', q, k) * decay, 0.0)
    q_dec = q * jnp.exp(G)[..., None]
    k_tail = k * jnp.exp(G[..., -1:] - G)[..., None]
    chunk_decay = jnp.exp(G[..., -1])

    def step(s, xs):
        w_c, u_c, qk_c, qd_c, kt_c, cd_c = xs
        v_new = u_c - jnp.einsum('bhcd,bhde->bhce', w_c, s)
        o = jnp.einsum('bhcd,bhde->bhce', qd_c, s) + jnp.einsum('bhij,bhje->bhie', qk_c, v_new)
        s = s * cd_c[..., None, None] + jnp.einsum('bhcd,bhce->bhde', kt_c, v_new)
        return s, o

    s_final, o = lax.scan(step, s0, (w, u, qk, q_dec, k_tail, chunk_decay))
    o = jnp.swapaxes(jnp.moveaxis(o, 0, 1), 2, 3).reshape(B, T, H, dv)
    return o, s_final

def gated_delta_mixer(qkv, gate, beta_logit, decay_logit, conv_w, a_log, dt_bias, norm_g, s0):
    B, T = qkv.shape[:2]
    qkv = jax.nn.silu(centred_depthwise_conv(qkv, conv_w))
    q, k, v = split_last(qkv, (DELTA_HEADS * DELTA_DK, DELTA_HEADS * DELTA_DK, DELTA_WIDTH))
    q = l2_normalize(q.reshape(B, T, DELTA_HEADS, DELTA_DK)) * DELTA_DK ** -0.5
    k = l2_normalize(k.reshape(B, T, DELTA_HEADS, DELTA_DK))
    v = v.reshape(B, T, DELTA_HEADS, DELTA_DV)
    beta = jax.nn.sigmoid(beta_logit)
    g = -jnp.exp(a_log) * jax.nn.softplus(decay_logit + dt_bias)
    o_f, s_f = chunk_gated_delta_rule(q, k, v, beta[:, :, 0], g[:, :, 0], s0[:, 0])
    rev = lambda t: jnp.flip(t, 1)
    o_b, s_b = chunk_gated_delta_rule(rev(q), rev(k), rev(v), rev(beta[:, :, 1]), rev(g[:, :, 1]), s0[:, 1])
    o = o_f + rev(o_b)
    o = rms_norm(o, norm_g) * jax.nn.silu(gate.reshape(B, T, DELTA_HEADS, DELTA_DV))
    return o.reshape(B, T, DELTA_WIDTH), jnp.stack([s_f, s_b], axis=1)

def gqa_block(qb, k, v):
    s = jnp.einsum('bqngd,bknd->bngqk', qb, k) * HEAD_DIM ** -0.5
    p = jax.nn.softmax(s, axis=-1)
    return jnp.einsum('bngqk,bknd->bqngd', p, v)

def expert_choice_ffn(h, router_w, w1, w3, w2):
    B, T, D = h.shape
    n = B * T
    cap = max(1, EC_CAPACITY_FACTOR * n // N_EXPERTS)
    xf = h.reshape(n, D)
    aff = jax.nn.softmax(jnp.dot(xf, router_w).astype(jnp.float32), axis=-1)
    gate, idx = lax.top_k(aff.T, cap)
    xe = xf[idx]
    hid = jax.nn.silu(jnp.einsum('ecd,edf->ecf', xe, w1)) * jnp.einsum('ecd,edf->ecf', xe, w3)
    ye = jnp.einsum('ecf,efd->ecd', hid, w2) * gate[..., None].astype(h.dtype)
    out = jnp.zeros_like(xf).at[idx.reshape(-1)].add(ye.reshape(-1, D).astype(xf.dtype))
    return out.reshape(B, T, D)

def even_mixer(h, l, P, rope, ctx):
    li = l // 2
    B, T = h.shape[:2]
    f32 = jnp.float32
    z = jnp.dot(h, P['w_in_ab'][li]).astype(f32)
    xa, ga, qd, kd, vd = split_last(z, (LRU_WIDTH, LRU_WIDTH, DIFF_QK, DIFF_QK, DIFF_V))
    h0 = jnp.zeros((B, 2, LRU_WIDTH), f32) if ctx is None else ctx[0].astype(f32)
    y_a, lru_state = rglru_mixer(
        xa, ga, P['lru_conv_w'][li], P['lru_conv_b'][li], P['lru_wa'][li], P['lru_ba'][li],
        P['lru_wi'][li], P['lru_bi'][li], P['lru_lam'][li], h0)
    q = rms_norm(qd.reshape(B, T, DIFF_HEADS, 2, HEAD_DIM), P['diff_q_gain'][li])
    k = rms_norm(kd.reshape(B, T, DIFF_HEADS, 2, HEAD_DIM), P['diff_k_gain'][li])
    v = vd.reshape(B, T, DIFF_HEADS, 2 * HEAD_DIM)
    new = (lru_state, k, v) if ctx is None else None
    if ctx is not None:
        q = apply_rope(q, rope[0], rope[1])
        k = jnp.concatenate([ctx[1].astype(f32), apply_rope(k, rope[0], rope[1])], axis=1)
        v = jnp.concatenate([ctx[2].astype(f32), v], axis=1)
    lam_init = 0.8 - 0.6 * math.exp(-0.3 * l)
    lv = P['diff_lam'][li].astype(f32)
    lam = jnp.exp(jnp.sum(lv[0] * lv[1])) - jnp.exp(jnp.sum(lv[2] * lv[3])) + lam_init
    o = sweep_query_blocks(lambda qb: diff_attention_block(qb, k, v, lam), q)
    y_b = rms_norm(o, P['diff_sub_gain'][li]) * (1.0 - lam_init)
    y = jnp.concatenate([y_a, y_b.reshape(B, T, DIFF_V)], axis=-1).astype(h.dtype)
    return jnp.dot(y, P['w_out'][l]), new

def odd_mixer(h, l, P, rope, ctx):
    li = l // 2
    B, T = h.shape[:2]
    f32 = jnp.float32
    z = jnp.dot(h, P['w_in_cd'][li]).astype(f32)
    qkv, gate, beta_logit, decay_logit, qg, kg, vg = split_last(
        z, (DELTA_CONV_CH, DELTA_WIDTH, 2 * DELTA_HEADS, 2 * DELTA_HEADS, GQA_WIDTH,
            GQA_KV_HEADS * HEAD_DIM, GQA_KV_HEADS * HEAD_DIM))
    s0 = jnp.zeros((B, 2, DELTA_HEADS, DELTA_DK, DELTA_DV), f32) if ctx is None else ctx[0].astype(f32)
    y_c, delta_state = gated_delta_mixer(
        qkv, gate, beta_logit.reshape(B, T, 2, DELTA_HEADS), decay_logit.reshape(B, T, 2, DELTA_HEADS),
        P['delta_conv_w'][li], P['delta_a_log'][li], P['delta_dt_bias'][li], P['delta_norm_g'][li], s0)
    q = rms_norm(qg.reshape(B, T, GQA_KV_HEADS, GQA_GROUP, HEAD_DIM), P['gqa_q_gain'][li])
    k = rms_norm(kg.reshape(B, T, GQA_KV_HEADS, HEAD_DIM), P['gqa_k_gain'][li])
    v = vg.reshape(B, T, GQA_KV_HEADS, HEAD_DIM)
    new = (delta_state, k, v) if ctx is None else None
    if ctx is not None:
        q = apply_rope(q, rope[0], rope[1])
        k = jnp.concatenate([ctx[1].astype(f32), apply_rope(k, rope[0], rope[1])], axis=1)
        v = jnp.concatenate([ctx[2].astype(f32), v], axis=1)
    o = sweep_query_blocks(lambda qb: gqa_block(qb, k, v), q)
    y = jnp.concatenate([y_c, o.reshape(B, T, GQA_WIDTH)], axis=-1).astype(h.dtype)
    return jnp.dot(y, P['w_out'][l]), new

def run_layer(x, mod, l, P, rope, ctx):
    shift1, scale1, gate1, shift2, scale2, gate2 = jnp.split(mod, 6, axis=-1)
    h = rms_norm(x, P['norm1_g'][l]) * (1 + scale1) + shift1
    if l % 2 == 0:
        y, new = even_mixer(h, l, P, rope, ctx)
    else:
        y, new = odd_mixer(h, l, P, rope, ctx)
    x = x + gate1 * y
    h = rms_norm(x, P['norm2_g'][l]) * (1 + scale2) + shift2
    x = x + gate2 * expert_choice_ffn(h, P['router_w'][l], P['exp_w1'][l], P['exp_w3'][l], P['exp_w2'][l])
    return x, new

def setup_inputs(seed: int = 0) -> dict:
    key = jax.random.key(seed)
    keys = jax.random.split(key, 48)
    counter = [0]
    f32 = jnp.float32

    def nk():
        counter[0] += 1
        return keys[counter[0] - 1]

    def nrm(shape, scale):
        return scale * jax.random.normal(nk(), shape, f32)

    def gain(shape):
        return 1.0 + nrm(shape, 0.01)

    a0 = jax.random.uniform(nk(), (N_AB_LAYERS, 2, LRU_WIDTH), f32, 0.9, 0.999)
    a_root = a0 ** (1.0 / LRU_C)
    lru_lam = jnp.log(a_root) - jnp.log1p(-a_root)
    a_log = jnp.log(jax.random.uniform(nk(), (N_CD_LAYERS, 2, DELTA_HEADS), f32, 1.0, 16.0))
    dt = jnp.exp(jax.random.uniform(nk(), (N_CD_LAYERS, 2, DELTA_HEADS), f32, math.log(0.001), math.log(0.1)))
    dt_bias = dt + jnp.log(-jnp.expm1(-dt))
    return {
        'x_prompt': nrm((BATCH, SEQ, D_MODEL), 1.0),
        'x_sample': nrm((DEC_BATCH, DEC_SEQ, D_MODEL), 1.0),
        'state_lru': nrm((DEC_BATCH, N_AB_LAYERS, 2, LRU_WIDTH), 0.5),
        'cache_diff_k': nrm((DEC_BATCH, N_AB_LAYERS, PAST_LEN, DIFF_HEADS, 2, HEAD_DIM), 1.0),
        'cache_diff_v': nrm((DEC_BATCH, N_AB_LAYERS, PAST_LEN, DIFF_HEADS, 2 * HEAD_DIM), 1.0),
        'state_delta': nrm((DEC_BATCH, N_CD_LAYERS, 2, DELTA_HEADS, DELTA_DK, DELTA_DV), DELTA_DK ** -0.5),
        'cache_gqa_k': nrm((DEC_BATCH, N_CD_LAYERS, PAST_LEN, GQA_KV_HEADS, HEAD_DIM), 1.0),
        'cache_gqa_v': nrm((DEC_BATCH, N_CD_LAYERS, PAST_LEN, GQA_KV_HEADS, HEAD_DIM), 1.0),
        'c': nrm((DEC_BATCH, D_MODEL), 1.0),
        'c_ctx': nrm((D_MODEL,), 1.0),
        'norm1_g': gain((DEPTH, D_MODEL)),
        'norm2_g': gain((DEPTH, D_MODEL)),
        'w_mod': nrm((DEPTH, D_MODEL, 6 * D_MODEL), 0.5 * D_MODEL ** -0.5),
        'b_mod': nrm((DEPTH, 6 * D_MODEL), 0.01),
        'w_in_ab': nrm((N_AB_LAYERS, D_MODEL, IN_AB), D_MODEL ** -0.5),
        'lru_conv_w': nrm((N_AB_LAYERS, CONV_W, LRU_WIDTH), 0.5),
        'lru_conv_b': nrm((N_AB_LAYERS, LRU_WIDTH), 0.01),
        'lru_wa': nrm((N_AB_LAYERS, 2, LRU_BLOCKS, LRU_BW, LRU_BW), LRU_BW ** -0.5),
        'lru_ba': nrm((N_AB_LAYERS, 2, LRU_WIDTH), 0.01),
        'lru_wi': nrm((N_AB_LAYERS, 2, LRU_BLOCKS, LRU_BW, LRU_BW), LRU_BW ** -0.5),
        'lru_bi': nrm((N_AB_LAYERS, 2, LRU_WIDTH), 0.01),
        'lru_lam': lru_lam,
        'diff_q_gain': gain((N_AB_LAYERS, HEAD_DIM)),
        'diff_k_gain': gain((N_AB_LAYERS, HEAD_DIM)),
        'diff_lam': nrm((N_AB_LAYERS, 4, HEAD_DIM), 0.1),
        'diff_sub_gain': gain((N_AB_LAYERS, 2 * HEAD_DIM)),
        'w_in_cd': nrm((N_CD_LAYERS, D_MODEL, IN_CD), D_MODEL ** -0.5),
        'delta_conv_w': nrm((N_CD_LAYERS, CONV_W, DELTA_CONV_CH), 0.5),
        'delta_a_log': a_log,
        'delta_dt_bias': dt_bias,
        'delta_norm_g': gain((N_CD_LAYERS, DELTA_DV)),
        'gqa_q_gain': gain((N_CD_LAYERS, HEAD_DIM)),
        'gqa_k_gain': gain((N_CD_LAYERS, HEAD_DIM)),
        'w_out': nrm((DEPTH, MIX_WIDTH, D_MODEL), MIX_WIDTH ** -0.5),
        'router_w': nrm((DEPTH, D_MODEL, N_EXPERTS), D_MODEL ** -0.5),
        'exp_w1': nrm((DEPTH, N_EXPERTS, D_MODEL, EXPERT_FF), D_MODEL ** -0.5),
        'exp_w3': nrm((DEPTH, N_EXPERTS, D_MODEL, EXPERT_FF), D_MODEL ** -0.5),
        'exp_w2': nrm((DEPTH, N_EXPERTS, EXPERT_FF, D_MODEL), EXPERT_FF ** -0.5),
    }

def reference(x_prompt, x_sample, state_lru, cache_diff_k, cache_diff_v, state_delta, cache_gqa_k, cache_gqa_v,
              c, c_ctx, norm1_g, norm2_g, w_mod, b_mod, w_in_ab, lru_conv_w, lru_conv_b, lru_wa, lru_ba,
              lru_wi, lru_bi, lru_lam, diff_q_gain, diff_k_gain, diff_lam, diff_sub_gain, w_in_cd,
              delta_conv_w, delta_a_log, delta_dt_bias, delta_norm_g, gqa_q_gain, gqa_k_gain, w_out,
              router_w, exp_w1, exp_w3, exp_w2):
    P = dict(
        norm1_g=norm1_g, norm2_g=norm2_g, w_in_ab=w_in_ab, lru_conv_w=lru_conv_w, lru_conv_b=lru_conv_b,
        lru_wa=lru_wa, lru_ba=lru_ba, lru_wi=lru_wi, lru_bi=lru_bi, lru_lam=lru_lam,
        diff_q_gain=diff_q_gain, diff_k_gain=diff_k_gain, diff_lam=diff_lam, diff_sub_gain=diff_sub_gain,
        w_in_cd=w_in_cd, delta_conv_w=delta_conv_w, delta_a_log=delta_a_log, delta_dt_bias=delta_dt_bias,
        delta_norm_g=delta_norm_g, gqa_q_gain=gqa_q_gain, gqa_k_gain=gqa_k_gain, w_out=w_out,
        router_w=router_w, exp_w1=exp_w1, exp_w3=exp_w3, exp_w2=exp_w2)
    dtype = x_prompt.dtype

    y_prompt = x_prompt
    lru_new, dk_new, dv_new, delta_new, gk_new, gv_new = [], [], [], [], [], []
    for l in range(DEPTH):
        mod = (jnp.dot(jax.nn.silu(c_ctx), w_mod[l]) + b_mod[l])[None, None, :]
        y_prompt, new = run_layer(y_prompt, mod, l, P, None, None)
        if l % 2 == 0:
            lru_new.append(new[0])
            dk_new.append(new[1])
            dv_new.append(new[2])
        else:
            delta_new.append(new[0])
            gk_new.append(new[1])
            gv_new.append(new[2])

    rope = axial_rope_tables(x_sample.shape[1], HEAD_DIM)
    y_sample = x_sample
    for l in range(DEPTH):
        li = l // 2
        mod = (jnp.dot(jax.nn.silu(c), w_mod[l]) + b_mod[l])[:, None, :]
        if l % 2 == 0:
            ctx = (state_lru[:, li], cache_diff_k[:, li], cache_diff_v[:, li])
        else:
            ctx = (state_delta[:, li], cache_gqa_k[:, li], cache_gqa_v[:, li])
        y_sample, _ = run_layer(y_sample, mod, l, P, rope, ctx)

    new_state_lru = jnp.stack(lru_new, axis=1).astype(dtype)
    new_cache_diff_k = jnp.stack(dk_new, axis=1).astype(dtype)
    new_cache_diff_v = jnp.stack(dv_new, axis=1).astype(dtype)
    new_state_delta = jnp.stack(delta_new, axis=1).astype(dtype)
    new_cache_gqa_k = jnp.stack(gk_new, axis=1).astype(dtype)
    new_cache_gqa_v = jnp.stack(gv_new, axis=1).astype(dtype)
    return (y_prompt, y_sample, new_state_lru, new_cache_diff_k, new_cache_diff_v, new_state_delta, new_cache_gqa_k, new_cache_gqa_v)


_drawn_inputs = setup_inputs


def setup_inputs(seed=0):
    import zlib

    import numpy as np

    out = dict(_drawn_inputs(seed))
    spreads = {}
    factors = {'cache_diff_k': 23.36,
     'state_delta': 5.451,
     'cache_gqa_k': 8.0,
     'cache_gqa_v': 8.0,
     'norm1_g': 3.548,
     'norm2_g': 6.947,
     'lru_ba': 8.0,
     'lru_bi': 8.0,
     'diff_q_gain': 8.0,
     'diff_k_gain': 5.725,
     'diff_lam': 2.844,
     'diff_sub_gain': 8.0,
     'delta_norm_g': 45.687,
     'gqa_q_gain': 26.197,
     'gqa_k_gain': 33.441,
     'cache_diff_v': 8.0}
    for name, (base, spread) in spreads.items():
        noise = np.random.default_rng([zlib.crc32(name.encode()), seed]).standard_normal(out[name].shape)
        drawn = base * np.exp(spread * noise) if base else spread * noise
        out[name] = jnp.asarray(drawn.astype(out[name].dtype))
    for name, factor in factors.items():
        out[name] = (out[name] * factor).astype(out[name].dtype)
    return out
```

```python
from contextlib import ExitStack

import concourse.bass as bass
from concourse import mybir

F32 = mybir.dt.float32
U32 = mybir.dt.uint32
ACT = mybir.ActivationFunctionType
ALU = mybir.AluOpType
AX_X = mybir.AxisListType.X

P = 128
D = 1024
KD = D // P
NS, NP = 512, 128
T = NS + NP
NT = T // P
ST = NS // P
HD = 64
PADW = NS + NP + 6
PS0, PP0 = 2, NS + 5
UW = PADW - 3
UP0 = NS + 3
NE, CAPS, CAPP = 16, 64, 16
CAP = CAPS + CAPP
FF = 512
FT = FF // P
NIN_AB, NIN_CD = 2560, 2832
CK = 64
NEG = -1.0e30
LAM_INIT = 0.2
CONSTS = ["ident", "ones", "lo_neg", "up_neg", "lo_one", "up_one", "block"] + [f"f{s}" for s in range(6)] + \
         [f"b{s}" for s in range(6)]


class Units:

    def __init__(self):
        self.uses = [0] * 4
        self.of = {}
        self.next = 0

    def add(self, name):
        pair = self.next % 4
        self.next += 1
        self.uses[pair] += 1
        self.of[name] = (pair, self.uses[pair])
        return self.of[name]


class Steps:

    def __init__(self, eng, sem):
        self.eng, self.sem, self.n = eng, sem, 0

    def __call__(self, ins):
        self.n += 1
        ins.then_inc(self.sem, 1)
        self.eng.wait_ge(self.sem, self.n)


def build(nc, io, outs, dbg=None, stop=None):
    with ExitStack() as ctx:
        def sb(name, shape, dt=F32):
            return ctx.enter_context(nc.sbuf_tensor(name, shape, dt))

        sems = {}

        def S(name):
            if name not in sems:
                sems[name] = ctx.enter_context(nc.semaphore("s_" + name))
            return sems[name]

        PSUM = ctx.enter_context(nc.psum_tensor("pairs", [P, 4, 1024], F32))
        pair_full = [S(f"pair_full{i}") for i in range(4)]
        pair_free = [S(f"pair_free{i}") for i in range(4)]
        units = Units()

        xT = sb("xT", [P, KD, T])
        hT = sb("hT", [P, KD, T])
        ring = sb("ring", [P, 3, 4096])
        cst = sb("cst", [P, len(CONSTS), P])
        rope = sb("rope", [P, ST, HD])
        cA = sb("cA", [P, P])
        cB = sb("cB", [P, P])
        par = sb("par", [P, 784])
        modt = sb("modt", [P, 2, 48, 2])
        gsc = sb("gsc", [P, 2, 2, KD, 2])
        csil = sb("csil", [P, KD, 2])
        dk_c = sb("dk_c", [P, 512])
        dv_c = sb("dv_c", [P, 512])
        gk_c = sb("gk_c", [P, 128])
        gv_c = sb("gv_c", [P, 128])
        sdel = sb("sdel", [P, 8, P])
        wr = sb("wr", [P, 2, KD, NE])
        sm = sb("sm", [P, 640])
        AR = 23400
        arena = sb("arena", [P, AR])

        C = {n: cst[:, i, :] for i, n in enumerate(CONSTS)}
        ident, ones = C["ident"], C["ones"]

        def ar(off, *shape):
            n = 1
            for x in shape:
                n *= x
            assert off + n <= AR, (off, n)
            v = arena[:, off:off + n]
            if len(shape) == 2:
                v = v.rearrange("p (a b) -> p a b", b=shape[1])
            elif len(shape) == 3:
                v = v.rearrange("p (a b c) -> p a b c", b=shape[1], c=shape[2])
            return v

        hflat = hT[:, :, :].rearrange("p k t -> p (k t)")
        rows = ar(0, NT, D)
        c_cols, cb_col, ba_col, bi_col, lam_col, st_col, lw_col, dw_col = \
            cB[:, 0:16], 16, 20, 28, 36, 44, 52, 68
        dqg, dkg, gqg, gkg = (par[:, 64 * i:64 * i + 64] for i in range(4))
        dsg, dng = par[:, 256:384], par[:, 384:512]
        alog, dtb = par[:, 512:520], par[:, 520:528]
        dlam = par[:, 528:784]
        hs = sm[:, 0:8]
        nlam = sm[:, 8:9]
        hba, hbi = sm[:, 16:24], sm[:, 24:32]
        spt = sm[:, 32:112]
        stl = sm[:, 112:120]
        smx = sm[:, 120:160]
        ssq = sm[:, 160:200]
        sps = sm[:, 200:208]
        anl = sm[:, 208:216]

        DR = {}
        for l in range(2):
            DR["h", l] = nc.dram_tensor(f"h_rows{l}", (T, D), F32, kind="Internal").ap()
            DR["m", l] = nc.dram_tensor(f"moe_rows{l}", (T, D), F32, kind="Internal").ap()

        def take(pe, name):
            pair, n = units.add(name)
            if n > 1:
                pe.wait_ge(pair_free[pair], n - 1)
            return PSUM[:, pair, :]

        def finish(ins, name):
            ins.then_inc(pair_full[units.of[name][0]], 1)

        def filled(eng, name):
            pair, n = units.of[name]
            eng.wait_ge(pair_full[pair], n)
            return PSUM[:, pair, :]

        def release(ins, name):
            ins.then_inc(pair_free[units.of[name][0]], 1)

        def emptied(eng, name):
            pair, n = units.of[name]
            eng.wait_ge(pair_free[pair], n)

        def mmk(pe, out, lhs, rhs):
            for k in range(KD):
                last = pe.matmul(out, lhs(k), rhs(k), start=(k == 0), stop=(k == KD - 1))
            return last

        chunks = []
        for l in range(2):
            lst = [("mod", l, m, h) for m in range(2) for h in range(2)]
            lst += [("in", l, c, 0) for c in range(5 + l)]
            lst += [("mod", l, m, h) for m in range(2, 6) for h in range(2)]
            lst += [("out", l, h, 0) for h in range(2)]
            chunks.append(lst)
        slot_of, slot_uses = {}, [0] * 6
        last_in_slot = {}
        loads = []
        for l in range(2):
            for i, c in enumerate(chunks[l]):
                s = i % 3
                slot_uses[s] += 1
                slot_of[c] = (s, slot_uses[s])
                loads.append((c, s, last_in_slot.get(s)))
                last_in_slot[s] = c
            base = list(slot_uses)
            for s in range(6):
                slot_uses[s] += NE // 2
                slot_of["exp", l, s] = base[s]
            loads.append((("experts", l), None, dict(last_in_slot)))
            for s in range(3):
                last_in_slot[s] = ("experts", l)
        slots = [ring[:, s, :] for s in range(3)] + [ar(4096 * s, 4096) for s in range(3)]
        w_here = [S(f"w_here{s}") for s in range(6)]

        def chunk_src(c):
            kind, l, a, b = c
            if kind == "mod":
                return io["w_mod"][l][:, 1024 * a + 512 * b:1024 * a + 512 * b + 512], 512
            if kind == "in":
                w = io["w_in_ab" if l == 0 else "w_in_cd"][0]
                n = min(512, w.shape[1] - 512 * a)
                return w[:, 512 * a:512 * a + n], n
            return io["w_out"][l][:, 512 * a:512 * a + 512], 512

        def chunk(c):
            n = chunk_src(c)[1]
            return slots[slot_of[c][0]][:, 0:KD * n].rearrange("p (k n) -> p k n", n=n)

        def arrived(pe, c):
            s, n = slot_of[c]
            pe.wait_ge(w_here[s], 16 * n)
            return chunk(c)

        chunk_last = {}

        W1 = [io["exp_w1"][l].rearrange("e (k p) f -> p (e k) f", p=P) for l in range(2)]
        W3 = [io["exp_w3"][l].rearrange("e (k p) f -> p (e k) f", p=P) for l in range(2)]
        W2 = [io["exp_w2"][l].rearrange("e (k p) d -> p (e k) d", p=P) for l in range(2)]
        moe_base = {}

        N_CONST = 17

        def setup_dma(act):
            q = S("const_here")
            act.dma_start(cst[:, :, :], io["consts"].rearrange("n p m -> p n m")).then_inc(q, 16)
            act.dma_start(rows[:, 0:ST, :], io["x_sample"][0].rearrange("(t p) d -> p t d", p=P)).then_inc(q, 16)
            act.dma_start(rows[:, ST, :], io["x_prompt"][0]).then_inc(q, 16)
            act.dma_start(ar(6000, 128), io["colsA"]).then_inc(q, 16)
            act.dma_start(ar(6200, 128)[0:116, :], io["colsB"]).then_inc(q, 16)
            act.dma_start(par[:, :], io["params"].to_broadcast((P, 784))).then_inc(q, 16)
            act.dma_start(rope[:, :, :], io["rope"].rearrange("(t p) n -> p t n", p=P)).then_inc(q, 16)
            act.dma_start(dk_c[:, :], io["cache_diff_k"][0, 0].rearrange("t h c d -> t (h c d)")).then_inc(q, 16)
            act.dma_start(dv_c[:, :], io["cache_diff_v"][0, 0].rearrange("t h d -> t (h d)")).then_inc(q, 16)
            act.dma_start(gk_c[:, :], io["cache_gqa_k"][0, 0].rearrange("t h d -> t (h d)")).then_inc(q, 16)
            act.dma_start(gv_c[:, :], io["cache_gqa_v"][0, 0].rearrange("t h d -> t (h d)")).then_inc(q, 16)
            act.dma_start(sdel[:, :, :], io["state_delta"][0, 0].rearrange("r h k v -> k (r h) v")).then_inc(q, 16)
            for l in range(2):
                act.dma_start(wr[:, l, :, :], io["router_w"][l].rearrange("(k p) e -> p k e", p=P)).then_inc(q, 16)

        wg = ar(10000, 16, P).rearrange("p (q c) m -> p q c m", c=4)

        def setup_gates_dma(act):
            q = S("const_here")
            for r in range(2):
                for i, w in enumerate(("lru_wa", "lru_wi")):
                    for half in range(2):
                        src = io[w][0, r].rearrange("(t h) c d -> h c t d", h=2)[half]
                        act.dma_start(wg[64 * half:64 * half + 64, 2 * r + i, :, 64 * half:64 * half + 64],
                                      src).then_inc(q, 16)
        CONST_ALL = 16 * (14 + 8)

        def setup_pe(pe):
            pe.wait_ge(S("const_here"), CONST_ALL)
            ps = take(pe, "cols")
            pe.transpose(ps[:, 0:P], ar(6000, 128), ident)
            finish(pe.transpose(ps[:, 512:628], ar(6200, 128)[0:116, :], ident[0:116, 0:116]), "cols")
            flip_in_pe(pe, "x_in")

        def flip_in_pe(pe, tag):
            for k in range(KD):
                ps = take(pe, (tag, k))
                for t in range(NT):
                    last = pe.transpose(ps[:, t * P:t * P + P], rows[:, t, k * P:k * P + P], ident)
                finish(last, (tag, k))

        def flip_out_pe(pe, tag, src):
            for t in range(NT):
                ps = take(pe, (tag, t))
                for k in range(KD):
                    last = pe.transpose(ps[:, k * P:k * P + P], src[:, k, t * P:t * P + P], ident)
                finish(last, (tag, t))

        def copy(eng, dst, src):
            return eng.activation(dst, src, ACT.Copy) if eng is nc.scalar else eng.tensor_copy(dst, src)

        def flip_in_read(eng, tag, part):
            for k in range(part, KD, 2):
                release(copy(eng, xT[:, k, :], filled(eng, (tag, k))[:, 0:T]), (tag, k))

        def flip_out_read(eng, tag, part):
            for t in range(part, NT, 2):
                release(copy(eng, rows[:, t, :], filled(eng, (tag, t))), (tag, t))

        def softplus_act(act, step, x, e):
            step(act.activation(e, x, ACT.Abs))
            return act.activation(e, e, ACT.Exp, scale=-1.0)

        def softplus_dve(v, step, x, e, z, z2, out):
            step(v.tensor_scalar(z, e, 2.0, None, ALU.add))
            step(v.reciprocal(z, z))
            step(v.tensor_tensor(z, e, z, ALU.mult))
            step(v.tensor_tensor(z2, z, z, ALU.mult))
            step(v.tensor_scalar(e, z2, 1.0 / 17, 1.0 / 15, ALU.mult, ALU.add))
            for n in (13, 11, 9, 7, 5, 3, 1):
                step(v.tensor_tensor(e, e, z2, ALU.mult))
                step(v.tensor_scalar(e, e, 1.0 / n, None, ALU.add))
            step(v.tensor_tensor(e, e, z, ALU.mult))
            step(v.tensor_scalar(z, x, 0.0, None, ALU.max))
            step(v.scalar_tensor_tensor(out=out, in0=e, scalar=2.0, in1=z, op0=ALU.mult, op1=ALU.add))

        negl = sm[:, 216:224]

        def setup_act(act, step):
            setup_dma(act)
            act.wait_ge(S("zeroed"), 2)
            setup_gates_dma(act)
            flip_in_read(act, "x_in", 0)
            act.wait_ge(S("cB"), 1)
            act.activation(csil[:, :, :].rearrange("p k g -> p g k"), c_cols.rearrange("p (g k) -> p g k", g=2),
                           ACT.Silu).then_inc(S("csil"), 1)
            act.wait_ge(S("negl"), 1)
            softplus_act(act, step, negl, spt[:, 0:8]).then_inc(S("sp_exp"), 1)
            act.wait_ge(S("lam_dot"), 1)
            act.activation(sps[:, 2:4], sps[:, 0:2], ACT.Exp).then_inc(S("lam_exp"), 1)

        def setup_dve(v, step):
            v.memset(hflat, 0.0).then_inc(S("zeroed"), 1)
            v.memset(ar(10000, 2048), 0.0).then_inc(S("zeroed"), 1)
            ps = filled(v, "cols")
            v.tensor_copy(cB[:, 0:116], ps[:, 512:628]).then_inc(S("cB"), 1)
            release(v.tensor_copy(cA[:, :], ps[:, 0:P]), "cols")
            flip_in_read(v, "x_in", 1)
            v.wait_ge(S("cB"), 1)
            v.tensor_scalar(negl, cB[:, lam_col:lam_col + 8], -1.0, None, ALU.mult).then_inc(S("negl"), 1)
            v.wait_ge(S("negl"), 1)
            v.wait_ge(S("sp_exp"), 1)
            softplus_dve(v, step, negl, spt[:, 0:8], spt[:, 8:16], spt[:, 16:24], spt[:, 24:32])
            step(v.tensor_scalar(hs, spt[:, 24:32], -4.0, None, ALU.mult))
            step(v.tensor_scalar(hba, cB[:, ba_col:ba_col + 8], 0.5, None, ALU.mult))
            step(v.tensor_scalar(hbi, cB[:, bi_col:bi_col + 8], 0.5, None, ALU.mult))
            v.wait_ge(S("const_here"), CONST_ALL)
            dl = dlam.rearrange("p (a b d) -> p a b d", a=2, b=2)
            step(v.tensor_tensor(ar(6400, 2, 64), dl[:, :, 0, :], dl[:, :, 1, :], ALU.mult))
            v.tensor_reduce(sps[:, 0:2], ar(6400, 2, 64), AX_X, ALU.add).then_inc(S("lam_dot"), 1)
            v.wait_ge(S("lam_exp"), 1)
            step(v.tensor_tensor(sps[:, 4:5], sps[:, 3:4], sps[:, 2:3], ALU.subtract))
            step(v.tensor_scalar(nlam, sps[:, 4:5], -LAM_INIT, None, ALU.add))
            step(v.tensor_scalar(dsg, dsg, 1.0 - LAM_INIT, None, ALU.mult))

        def setup_pool(g):
            g.wait_ge(S("zeroed"), 1)
            for l in range(2):
                g.dma_start(DR["m", l].rearrange("(t p) d -> p t d", p=P),
                            hflat.rearrange("p (t d) -> p t d", t=NT)).then_inc(S(f"y_room{l}"), 16)

        def mod_pe(pe, l, m):
            if l == 0 and m == 0:
                pe.wait_ge(S("csil"), 1)
            for h in range(2):
                w = arrived(pe, ("mod", l, m, h))
                u = ("mod", l, m, h)
                ps = take(pe, u)
                for f in range(4):
                    last = mmk(pe, ps[:, 2 * f:2 * f + 2], lambda k: w[:, k, f * P:f * P + P],
                               lambda k: csil[:, k, :])
                finish(last, u)
                chunk_last[u] = u

        def mod_dve(v, step, l, m):
            for h in range(2):
                u = ("mod", l, m, h)
                c0 = 8 * m + 4 * h
                ps = filled(v, u)[:, 0:8].rearrange("p (f g) -> p f g", g=2)
                b = cA[:, 32 + 48 * l + c0:32 + 48 * l + c0 + 4].unsqueeze(2).broadcast_to((P, 4, 2))
                if l == 0 and m == 0 and h == 0:
                    emptied(v, "cols")
                release(v.tensor_tensor(modt[:, l, c0:c0 + 4, :], ps, b, ALU.add), u)
                emptied(v, u)
            if m in (1, 4):
                n = m // 4
                g = cA[:, 16 * n + 8 * l:16 * n + 8 * l + 8].unsqueeze(2).broadcast_to((P, KD, 2))
                step(v.scalar_tensor_tensor(out=gsc[:, l, n, :, :], in0=modt[:, l, 8 * m:8 * m + 8, :], scalar=1.0,
                                            in1=g, op0=ALU.add, op1=ALU.mult))

        sq = ar(12800, KD, T)
        rstd = ar(18000, T)
        seg = ((0, NS), (NS, T))

        def norm_pe(pe, l, n):
            u = ("nrm", l, n)
            pe.wait_ge(S("sq_sum"), 2 * l + n + 1)
            ps = take(pe, u)
            pe.matmul(ps[:, 0:NS], ones, sq[:, 0, 0:NS], start=True, stop=True)
            finish(pe.matmul(ps[:, NS:T], ones, sq[:, 0, NS:T], start=True, stop=True), u)

        def norm_act(act, step, l, n):
            i = 2 * l + n
            if i:
                act.wait_ge(S("x_ready"), i)
            else:
                for k in range(4, KD):
                    emptied(act, ("x_in", k))
            if n == 1:
                act.wait_ge(S("caches"), (48, 96)[l])
            for h in range(2):
                act.activation(sq[:, 4 * h:4 * h + 4, :], xT[:, 4 * h:4 * h + 4, :], ACT.Square)\
                    .then_inc(S("sq"), 1)
            ps = filled(act, ("nrm", l, n))
            release(act.activation(rstd, ps[:, 0:T], ACT.Sqrt, scale=1.0 / D, bias=1e-6), ("nrm", l, n))
            for k in range(KD):
                for g in range(2):
                    a, b = seg[g]
                    act.wait_ge(S("h_scaled"), i * 16 + 2 * k + g + 1)
                    act.activation(hT[:, k, a:b], hT[:, k, a:b], ACT.Identity,
                                   bias=modt[:, l, 24 * n + k, g:g + 1]).then_inc(S("h_ready"), 1)

        def norm_dve(v, step, l, n):
            i = 2 * l + n
            v.wait_ge(S("sq"), 2 * i + 2)
            step(v.tensor_tensor(sq[:, 0:4, :], sq[:, 0:4, :], sq[:, 4:8, :], ALU.add))
            step(v.tensor_tensor(sq[:, 0:2, :], sq[:, 0:2, :], sq[:, 2:4, :], ALU.add))
            v.tensor_tensor(sq[:, 0, :], sq[:, 0, :], sq[:, 1, :], ALU.add).then_inc(S("sq_sum"), 1)
            emptied(v, ("nrm", l, n))
            step(v.reciprocal(rstd, rstd))
            if i == 0:
                v.wait_ge(S("y_room0"), 16)
                v.wait_ge(S("y_room1"), 16)
                for k in range(4, KD):
                    emptied(v, ("x_in", k))
            for k in range(KD):
                for g in range(2):
                    a, b = seg[g]
                    v.scalar_tensor_tensor(out=hT[:, k, a:b], in0=xT[:, k, a:b], scalar=gsc[:, l, n, k, g:g + 1],
                                           in1=rstd[:, a:b], op0=ALU.mult, op1=ALU.mult)\
                        .then_inc(S("h_scaled"), 1)

        def proj_T_pe(pe, l, c):
            w = arrived(pe, ("in", l, c, 0))
            for f in range(4):
                u = ("pT", l, c, f)
                ps = take(pe, u)
                lhs = lambda k: w[:, k, f * P:f * P + P]
                mmk(pe, ps[:, 0:NS], lhs, lambda k: hT[:, k, 0:NS])
                finish(mmk(pe, ps[:, NS:T], lhs, lambda k: hT[:, k, NS:T]), u)
            chunk_last["in", l, c, 0] = u

        def proj_R_pe(pe, l, c):
            w = arrived(pe, ("in", l, c, 0))
            n = chunk_src(("in", l, c, 0))[1]
            for tp in range(3):
                u = ("pR", l, c, tp)
                ps = take(pe, u)
                for t in range(2 * tp, min(2 * tp + 2, NT)):
                    o = 512 * (t % 2)
                    last = mmk(pe, ps[:, o:o + n], lambda k: hT[:, k, t * P:t * P + P], lambda k: w[:, k, 0:n])
                finish(last, u)
            chunk_last["in", l, c, 0] = u

        def read_T(eng, l, c, dst, part, padded):
            for f in range(part, 4, 2):
                u = ("pT", l, c, f)
                ps = filled(eng, u)
                if padded:
                    copy(eng, dst[:, f, PS0:PS0 + NS], ps[:, 0:NS]).then_inc(S("pad_evac" + str(part)), 1)
                    release(copy(eng, dst[:, f, PP0:PP0 + NP], ps[:, NS:T]), u)
                else:
                    release(copy(eng, dst[:, f, :], ps[:, 0:T]), u)

        def read_R(eng, l, c, dst, part):
            n = chunk_src(("in", l, c, 0))[1]
            for tp in range(3):
                if (tp + c) % 2 == part:
                    u = ("pR", l, c, tp)
                    ps = filled(eng, u)
                    m = 2 if tp < 2 else 1
                    release(copy(eng, dst[:, 2 * tp:2 * tp + m, :],
                                 ps.rearrange("p (a b) -> p a b", a=2)[:, 0:m, 0:n]), u)

        xap = ar(0, 4, PADW)
        ga = ar(2584, 4, T)
        qkv = ar(12048, NT, 1536)
        uT = ar(5144, 4, UW)
        gb = [ar(7716 + 2 * i * UW, 2, UW) for i in range(1)] + [None]
        lb = [[hflat[:, 2560 + 0 * UW:2560 + UW], hflat[:, 2560 + UW:2560 + 2 * UW],
               hflat[:, 2560 + 2 * UW:2560 + 3 * UW], ar(7716, UW)],
              [ar(7716 + UW, UW), ar(7716 + 2 * UW, UW), ar(19728 + 0 * UW, UW), ar(19728 + UW, UW)]]
        hfb = [ar(19728 + 2 * UW, UW), ar(19728 + 3 * UW, UW)]

        def pads_dve(v, step, pad):
            step(v.memset(pad[:, :, 0:2], 0.0))
            step(v.memset(pad[:, :, PS0 + NS:PP0], 0.0))
            step(v.memset(pad[:, :, PADW - 1:PADW], 0.0))

        def conv_dve(v, step, out, src, w, b):
            if b is None:
                step(v.tensor_scalar(out, src[:, 0:UW], w(0), None, ALU.mult))
            else:
                step(v.tensor_scalar(out, src[:, 0:UW], w(0), b, ALU.mult, ALU.add))
            for tap in range(1, 4):
                ins = v.scalar_tensor_tensor(out=out, in0=src[:, tap:tap + UW], scalar=w(tap), in1=out,
                                             op0=ALU.mult, op1=ALU.add)
                if tap < 3:
                    step(ins)
            return ins

        def lru_pe(pe):
            for ct in range(4):
                pe.wait_ge(S("u_ready"), ct + 1)
                for q in range(4):
                    u = ("gate", ct, q)
                    ps = take(pe, u)
                    pe.matmul(ps[:, 0:NS], wg[:, q, ct, :], uT[:, ct, 0:NS], start=True, stop=True)
                    finish(pe.matmul(ps[:, NS:UW], wg[:, q, ct, :], uT[:, ct, NS:UW], start=True, stop=True), u)

        def lru_act(act, step):
            for i in range(9):
                if i < 8:
                    ct, d = i // 2, i % 2
                    tr, ti, a, _ = lb[i % 2]
                    c8 = 4 * d + ct
                    if i == 0:
                        act.wait_ge(S("h_dead"), 1)
                    if i >= 2:
                        act.wait_ge(S("lru_scan"), i - 1)
                    release(act.activation(tr, filled(act, ("gate", ct, 2 * d))[:, 0:UW], ACT.Tanh, scale=0.5,
                                           bias=hba[:, c8:c8 + 1]), ("gate", ct, 2 * d))
                    release(act.activation(ti, filled(act, ("gate", ct, 2 * d + 1))[:, 0:UW], ACT.Tanh, scale=0.5,
                                           bias=hbi[:, c8:c8 + 1]), ("gate", ct, 2 * d + 1))
                    emptied(act, ("gate", ct, 2 * d))
                    step(act.activation(a, tr, ACT.Exp, scale=hs[:, c8:c8 + 1], bias=hs[:, c8:c8 + 1]))
                    act.activation(tr, tr, ACT.Tanh, scale=hs[:, c8:c8 + 1], bias=hs[:, c8:c8 + 1])\
                        .then_inc(S("lru_tanh"), 1)
                if i >= 1:
                    act.wait_ge(S("lru_q"), i)
                    tr = lb[(i - 1) % 2][0]
                    act.activation(tr, tr, ACT.Sqrt).then_inc(S("lru_root"), 1)
            for f in range(4):
                emptied(act, ("pT", 0, 1, f))
            act.activation(ga, ga, ACT.Gelu_apprx_tanh).then_inc(S("gelu"), 1)

        def lru_dve(v, step):
            for part in range(2):
                v.wait_ge(S("pad_evac" + str(part)), 2)
            for ct in range(4):
                emptied(v, ("pT", 0, 0, ct))
                conv_dve(v, step, uT[:, ct, :], xap[:, ct, :], lambda tap: cB[:, lw_col + 4 * tap + ct:lw_col + 4 * tap + ct + 1],
                         cB[:, cb_col + ct:cb_col + ct + 1]).then_inc(S("u_ready"), 1)
            v.wait_ge(S("h_dead"), 1)
            v.wait_ge(S("u_ready"), 4)
            for i in range(9):
                if i < 8:
                    tr, ti, a, w = lb[i % 2]
                    v.wait_ge(S("lru_tanh"), i + 1)
                    step(v.tensor_scalar(w, tr, -1.0, 1.0, ALU.mult, ALU.add))
                    step(v.reciprocal(w, w))
                    v.scalar_tensor_tensor(out=tr, in0=tr, scalar=-0.5, in1=w, op0=ALU.mult, op1=ALU.mult)\
                        .then_inc(S("lru_q"), 1)
                    step(v.scalar_tensor_tensor(out=ti, in0=ti, scalar=1.0, in1=uT[:, i // 2, :], op0=ALU.add,
                                                op1=ALU.mult))
                if i >= 1:
                    j = i - 1
                    ct, d = j // 2, j % 2
                    tr, ti, a, w = lb[j % 2]
                    c8 = 4 * d + ct
                    v.wait_ge(S("lru_root"), j + 1)
                    step(v.tensor_tensor(ti, ti, tr, ALU.mult))
                    h = hfb[d]
                    r = slice(None, None, 1 if d == 0 else -1)
                    step(v.tensor_tensor_scan(h[:, 0:NS][:, r], a[:, 0:NS][:, r], ti[:, 0:NS][:, r],
                                              cB[:, st_col + c8:st_col + c8 + 1], ALU.mult, ALU.add))
                    v.tensor_tensor_scan(h[:, UP0:UW][:, r], a[:, UP0:UW][:, r], ti[:, UP0:UW][:, r], 0.0,
                                         ALU.mult, ALU.add).then_inc(S("lru_scan"), 1)
                    v.wait_ge(S("lru_scan"), j + 1)
                    e = UW - 1 if d == 0 else UP0
                    step(v.tensor_copy(stl[:, c8:c8 + 1], h[:, e:e + 1]))
                    if d == 1:
                        step(v.tensor_tensor(hT[:, ct, 0:NS], hfb[0][:, 0:NS], hfb[1][:, 0:NS], ALU.add))
                        step(v.tensor_tensor(hT[:, ct, NS:T], hfb[0][:, UP0:UW], hfb[1][:, UP0:UW], ALU.add))
            v.wait_ge(S("gelu"), 1)
            v.tensor_tensor(hT[:, 0:4, :], hT[:, 0:4, :], ga, ALU.mult).then_inc(S("y_first"), 1)

        dscr = ar(0, NT * 8, HD)
        def rope_dve(v, step, x, nh, scr):
            cos = rope[:, :, 0:32].unsqueeze(2).broadcast_to((P, ST, nh, 32))
            sin = rope[:, :, 32:64].unsqueeze(2).broadcast_to((P, ST, nh, 32))
            x1, x2 = x[:, :, :, 0:32], x[:, :, :, 32:64]
            n = ST * nh * 32
            a, b, c, d = (scr[:, i * n:(i + 1) * n].rearrange("p (t h d) -> p t h d", h=nh, d=32) for i in range(4))
            for t in range(ST):
                v.tensor_tensor(a[:, t], x1[:, t], cos[:, t], ALU.mult)
                v.tensor_tensor(b[:, t], x2[:, t], sin[:, t], ALU.mult)
                v.tensor_tensor(c[:, t], x2[:, t], cos[:, t], ALU.mult)
                step(v.tensor_tensor(d[:, t], x1[:, t], sin[:, t], ALU.mult))
                v.tensor_tensor(x1[:, t], a[:, t], b[:, t], ALU.subtract)
                step(v.tensor_tensor(x2[:, t], c[:, t], d[:, t], ALU.add))

        qr = qkv[:, :, 0:512]
        kr = qkv[:, :, 512:1024]
        vr = qkv[:, :, 1024:1536]
        kT = ar(0, 4, 768)
        qT = ar(3072, 4, T)
        pb = [ar(5632 + 1280 * i, 2, T) for i in range(2)]
        aT = [ar(8192 + 640 * i, T) for i in range(2)]
        osb = qkv[:, :, 0:512]
        ITS = [(t, h) for t in range(NT) for h in range(4)]
        hn_count = [0]

        def hn_act(act, src, n_el, scr, eps_scale, ss):
            hn_count[0] += 1
            k = hn_count[0]
            act.activation(scr, src, ACT.Square).then_inc(S("hn_sq"), 1)
            act.wait_ge(S("hn_sum"), k)
            act.activation(ss, ss, ACT.Sqrt, scale=eps_scale, bias=1e-6).then_inc(S("hn_root"), 1)

        def hn_dve(v, step, k, x, scr, ss, nh, w, gain, out=None, mul=None):
            v.wait_ge(S("hn_sq"), k)
            v.tensor_reduce(ss, scr, AX_X, ALU.add).then_inc(S("hn_sum"), 1)
            v.wait_ge(S("hn_root"), k)
            step(v.reciprocal(ss, ss))
            if mul is not None:
                step(v.tensor_scalar(ss, ss, mul, None, ALU.mult))
            s4 = ss.rearrange("p (t h) -> p t h", h=nh).unsqueeze(3).broadcast_to((P, NT, nh, w))
            for t in range(NT):
                step(v.tensor_tensor(x[:, t], x[:, t], s4[:, t], ALU.mult))
                if gain is not None:
                    o = x if out is None else out
                    step(v.tensor_tensor(o[:, t], x[:, t], gain.unsqueeze(1).broadcast_to((P, nh, w)), ALU.mult))

        def diff_act(act, step):
            act.wait_ge(S("y_first"), 1)
            q4 = qr.rearrange("p t (h d) -> p t h d", d=HD)
            for c in (2, 3, 4):
                for tp in range(3):
                    emptied(act, ("pR", 0, c, tp))
            sc = dscr.rearrange("p (t h) d -> p t h d", h=8)
            hn_act(act, q4, 0, sc, 1.0 / HD, ssq)
            act.wait_ge(S("dq_done"), 1)
            hn_act(act, kr.rearrange("p t (h d) -> p t h d", d=HD), 0, sc, 1.0 / HD, ssq)
            for h in range(4):
                for j, tag in enumerate(("kT", "qT")):
                    u = (tag, h)
                    dst = kT[:, h, :] if j == 0 else qT[:, h, :]
                    release(copy(act, dst, filled(act, u)[:, 0:(768 if j == 0 else T)]), u)

            def exps(i):
                t, h = ITS[i]
                n = T if t < ST else P
                act.wait_ge(S("d_max"), i + 1)
                if i >= 2:
                    act.wait_ge(S("d_comb"), i - 1)
                for c in range(2):
                    u = ("ds", i, c)
                    release(act.activation(pb[i % 2][:, c, 0:n], filled(act, u)[:, 0:n], ACT.Exp, scale=HD ** -0.5,
                                           bias=smx[:, 2 * (i % 2) + c:2 * (i % 2) + c + 1],
                                           accum_out=smx[:, 8 + 2 * (i % 2) + c:9 + 2 * (i % 2) + c]), u)

            exps(0)
            for i in range(len(ITS)):
                if i + 1 < len(ITS):
                    exps(i + 1)
                n = T if ITS[i][0] < ST else P
                u = ("daT", i)
                if i >= 2:
                    filled(act, ("do", i - 2))
                release(copy(act, aT[i % 2][:, 0:n], filled(act, u)[:, 0:n]), u)
            act.wait_ge(S("d_rows"), 1)
            hn_act(act, osb.rearrange("p t (h d) -> p t h d", d=P), 0,
                   dscr.rearrange("p a b -> p (a b)").rearrange("p (t h d) -> p t h d", h=4, d=P), 1.0 / P, ssq[:, 0:20])
            for h in range(4):
                u = ("dyT", h)
                release(copy(act, hT[:, 4 + h, :], filled(act, u)[:, 0:T]), u)

        def diff_dve(v, step):
            for c in (2, 3, 4):
                for tp in range(3):
                    emptied(v, ("pR", 0, c, tp))
            q4 = qr.rearrange("p t (h d) -> p t h d", d=HD)
            k4 = kr.rearrange("p t (h d) -> p t h d", d=HD)
            v.wait_ge(S("y_first"), 1)
            hn_dve(v, step, 1, q4, dscr, ssq, 8, HD, dqg)
            v.memset(smx[:, 20:21], 0.0).then_inc(S("dq_done"), 1)
            hn_dve(v, step, 2, k4, dscr, ssq, 8, HD, dkg)
            v.memset(smx[:, 21:22], 0.0).then_inc(S("cache_k_ready"), 1)
            rs = ar(0, 4096)
            rope_dve(v, step, q4[:, 0:ST], 8, rs)
            rope_dve(v, step, k4[:, 0:ST], 8, rs)
            v.memset(smx[:, 22:23], 0.0).then_inc(S("qk_rows"), 1)

            def maxes(i):
                n = T if ITS[i][0] < ST else P
                if i >= 2:
                    emptied(v, ("ds", i - 2, 1))
                for c in range(2):
                    v.tensor_reduce(smx[:, 4 + c:5 + c], filled(v, ("ds", i, c))[:, 0:n], AX_X, ALU.max)\
                        .then_inc(S("d_mx1"), 1)
                v.wait_ge(S("d_mx1"), 2 * i + 2)
                v.tensor_scalar(smx[:, 2 * (i % 2):2 * (i % 2) + 2], smx[:, 4:6], -HD ** -0.5, None, ALU.mult)\
                    .then_inc(S("d_max"), 1)

            def rows_out(i):
                t, h = ITS[i]
                release(v.tensor_copy(osb[:, t, h * P:h * P + P], filled(v, ("do", i))[:, 0:P]), ("do", i))

            maxes(0)
            for i in range(len(ITS)):
                if i + 1 < len(ITS):
                    v.wait_ge(S("d_max"), i + 1)
                    maxes(i + 1)
                n = T if ITS[i][0] < ST else P
                r = smx[:, 8 + 2 * (i % 2):10 + 2 * (i % 2)]
                emptied(v, ("ds", i, 1))
                emptied(v, ("ds", i, 0))
                if i >= 2:
                    filled(v, ("daT", i - 2))
                step(v.reciprocal(smx[:, 12:14], r))
                step(v.tensor_tensor(smx[:, 14:15], smx[:, 13:14], nlam, ALU.mult))
                step(v.tensor_scalar(pb[i % 2][:, 0, 0:n], pb[i % 2][:, 0, 0:n], smx[:, 12:13], None, ALU.mult))
                v.scalar_tensor_tensor(out=pb[i % 2][:, 0, 0:n], in0=pb[i % 2][:, 1, 0:n], scalar=smx[:, 14:15],
                                       in1=pb[i % 2][:, 0, 0:n], op0=ALU.mult, op1=ALU.add).then_inc(S("d_comb"), 1)
                v.wait_ge(S("d_comb"), i + 1)
                if i >= 1:
                    rows_out(i - 1)
            rows_out(len(ITS) - 1)
            emptied(v, ("do", len(ITS) - 1))
            emptied(v, ("do", len(ITS) - 2))
            v.memset(smx[:, 23:24], 0.0).then_inc(S("d_rows"), 1)
            o4 = osb.rearrange("p t (h d) -> p t h d", d=P)
            hn_dve(v, step, 3, o4, dscr.rearrange("p a b -> p (a b)").rearrange("p (g d) -> p g d", d=P), ssq[:, 0:20], 4, P, dsg)
            v.memset(smx[:, 24:25], 0.0).then_inc(S("dy_rows"), 1)

        def diff_pe(pe):
            pe.wait_ge(S("qk_rows"), 1)
            pe.wait_ge(S("const_here"), CONST_ALL)
            for h in range(4):
                u = ("kT", h)
                ps = take(pe, u)
                c = slice(h * P, h * P + P)
                pe.transpose(ps[:, 0:P], dk_c[:, c], ident)
                for t in range(NT):
                    last = pe.transpose(ps[:, (t + 1) * P:(t + 2) * P], kr[:, t, c], ident)
                finish(last, u)
                u = ("qT", h)
                ps = take(pe, u)
                for t in range(NT):
                    last = pe.transpose(ps[:, t * P:t * P + P], qr[:, t, c], ident)
                finish(last, u)
            for h in range(4):
                emptied(pe, ("kT", h))
                emptied(pe, ("qT", h))

            def scores(i):
                t, h = ITS[i]
                for c in range(2):
                    u = ("ds", i, c)
                    ps = take(pe, u)
                    q = qT[64 * c:64 * c + 64, h, t * P:t * P + P]
                    k = kT[64 * c:64 * c + 64, h, :]
                    if t < ST:
                        pe.matmul(ps[:, 0:512], q, k[:, 0:512], start=True, stop=True)
                        last = pe.matmul(ps[:, 512:T], q, k[:, 512:T], start=True, stop=True)
                    else:
                        last = pe.matmul(ps[:, 0:P], q, k[:, T:768], start=True, stop=True)
                    finish(last, u)

            scores(0)
            for i, (t, h) in enumerate(ITS):
                if i + 1 < len(ITS):
                    scores(i + 1)
                nk = NT if t < ST else 1
                pe.wait_ge(S("d_comb"), i + 1)
                u = ("daT", i)
                ps = take(pe, u)
                for j in range(nk):
                    last = pe.transpose(ps[:, j * P:j * P + P], pb[i % 2][:, 0, j * P:j * P + P], ident)
                finish(last, u)
                u = ("do", i)
                ps = take(pe, u)
                emptied(pe, ("daT", i))
                for j in range(nk):
                    vals = vr[:, ST, h * P:h * P + P] if t == ST else \
                        dv_c[:, h * P:h * P + P] if j == 0 else vr[:, j - 1, h * P:h * P + P]
                    last = pe.matmul(ps[:, 0:P], aT[i % 2][:, j * P:j * P + P], vals, start=(j == 0), stop=(j == nk - 1))
                finish(last, u)
            pe.wait_ge(S("dy_rows"), 1)
            for h in range(4):
                u = ("dyT", h)
                ps = take(pe, u)
                for t in range(NT):
                    last = pe.transpose(ps[:, t * P:t * P + P], osb[:, t, h * P:h * P + P], ident)
                finish(last, u)

        def layer0_outputs(g):
            g.wait_ge(S("cache_k_ready"), 1)
            g.dma_start(outs["new_cache_diff_k"].rearrange("a b t h c d -> t (a b h c d)"), kr[:, ST, :])\
                .then_inc(S("caches"), 16)
            for tp in range(3):
                emptied(g, ("pR", 0, 4, tp))
            g.dma_start(outs["new_cache_diff_v"].rearrange("a b t h d -> t (a b h d)"), vr[:, ST, :])\
                .then_inc(S("caches"), 16)
            g.wait_ge(S("y_first"), 1)
            with nc.allow_non_contiguous_dma(reason="a small state"):
                g.dma_start(outs["new_state_lru"][0, 0].rearrange("r (c p) -> p (r c)", p=P), stl)\
                    .then_inc(S("caches"), 16)

        def out_pe(pe, l):
            if l == 0:
                pe.wait_ge(S("y_first"), 1)
                for h in range(4):
                    emptied(pe, ("dyT", h))
            else:
                layer1_ready(pe)
            for c in range(2):
                w = arrived(pe, ("out", l, c, 0))
                for f in range(4):
                    u = ("out", l, 4 * c + f)
                    ps = take(pe, u)
                    lhs = lambda k: w[:, k, f * P:f * P + P]
                    mmk(pe, ps[:, 0:NS], lhs, lambda k: hT[:, k, 0:NS])
                    finish(mmk(pe, ps[:, NS:T], lhs, lambda k: hT[:, k, NS:T]), u)
                chunk_last["out", l, c, 0] = u

        def add_gated(v, l, m, k, ps, u, last):
            a, b = seg[0]
            v.scalar_tensor_tensor(out=xT[:, k, a:b], in0=ps[:, a:b], scalar=modt[:, l, 8 * m + k, 0:1],
                                   in1=xT[:, k, a:b], op0=ALU.mult, op1=ALU.add).then_inc(S("x_half"), 1)
            xh[0] += 1
            a, b = seg[1]
            release(v.scalar_tensor_tensor(out=xT[:, k, a:b], in0=ps[:, a:b], scalar=modt[:, l, 8 * m + k, 1:2],
                                           in1=xT[:, k, a:b], op0=ALU.mult, op1=ALU.add), u)
        xh = [0]

        def out_dve(v, step, l):
            for k in range(KD):
                u = ("out", l, k)
                add_gated(v, l, 2, k, filled(v, u), u, k == KD - 1)
            v.wait_ge(S("x_half"), xh[0])
            for k in range(4, KD):
                emptied(v, ("out", l, k))
            v.memset(sm[:, 250:251], 0.0).then_inc(S("x_ready"), 1)

        lg = ar(18700, NT, NE)
        affT = ar(18800, T)[0:NE, :]
        g16 = ar(19500, CAP)[0:NE, :]
        i16 = ar(19600, CAP)[0:NE, :].bitcast(U32)
        i16f = ar(19700, CAP)[0:NE, :]
        gateT = ar(19800, NE)[0:CAP, :]
        idxT = ar(19820, NE)[0:CAP, :].bitcast(U32)
        hrow = ar(12800, NT, D)
        rows_m = ar(12800, NT, D)

        def flip_h_pe(pe, l):
            flip_out_pe(pe, ("hr", l), hT)

        def route_pe(pe, l):
            pe.wait_ge(S("h_ready"), 16 * (2 * l + 2))
            u = ("logit", l)
            ps = take(pe, u)
            for t in range(NT):
                last = mmk(pe, ps[:, 16 * t:16 * t + 16], lambda k: hT[:, k, t * P:t * P + P], lambda k: wr[:, l, k, :])
            finish(last, u)
            for t in range(NT):
                u = ("hr", l, t)
                ps = take(pe, u)
                for k in range(KD):
                    last = pe.transpose(ps[:, k * P:k * P + P], hT[:, k, t * P:t * P + P], ident)
                finish(last, u)
            pe.wait_ge(S("aff"), l + 1)
            u = ("affT", l)
            ps = take(pe, u)
            for t in range(NT):
                last = pe.transpose(ps[0:NE, t * P:t * P + P], lg[:, t, :], ident)
            finish(last, u)
            pe.wait_ge(S("top"), l + 1)
            u = ("gi", l)
            ps = take(pe, u)
            pe.transpose(ps[0:CAP, 0:16], g16, ident[0:NE, 0:NE])
            finish(pe.transpose(ps[0:CAP, 16:32], i16f, ident[0:NE, 0:NE]), u)

        def route_act(act, step, l):
            for t in range(NT):
                u = ("hr", l, t)
                release(copy(act, hrow[:, t, :], filled(act, u)), u)
            act.wait_ge(S("lg_sub"), l + 1)
            act.activation(lg, lg, ACT.Exp).then_inc(S("lg_exp"), 1)

        def route_dve(v, step, l):
            u = ("logit", l)
            ps = filled(v, u)[:, 0:80].rearrange("p (t e) -> p t e", e=NE)
            step(v.tensor_reduce(smx[:, 0:5], ps, AX_X, ALU.max))
            release(v.tensor_tensor(lg, ps, smx[:, 0:5].unsqueeze(2).broadcast_to((P, NT, NE)), ALU.subtract), u)
            emptied(v, u)
            v.memset(sm[:, 251:252], 0.0).then_inc(S("lg_sub"), 1)
            v.wait_ge(S("lg_exp"), l + 1)
            step(v.tensor_reduce(smx[:, 5:10], lg, AX_X, ALU.add))
            step(v.reciprocal(smx[:, 5:10], smx[:, 5:10]))
            v.tensor_tensor(lg, lg, smx[:, 5:10].unsqueeze(2).broadcast_to((P, NT, NE)), ALU.mult)\
                .then_inc(S("aff"), 1)
            u = ("affT", l)
            release(v.tensor_copy(affT, filled(v, u)[0:NE, 0:T]), u)
            emptied(v, u)
            for (a, b), c0, rounds in ((seg[0], 0, CAPS // 8), (seg[1], CAPS, CAPP // 8)):
                for r in range(rounds):
                    c = slice(c0 + 8 * r, c0 + 8 * r + 8)
                    step(v.max(g16[:, c], affT[:, a:b]))
                    step(v.max_index(i16[:, c], g16[:, c], affT[:, a:b]))
                    step(v.match_replace(affT[:, a:b], g16[:, c], affT[:, a:b], -1.0))
            step(v.tensor_copy(i16f, i16))
            v.tensor_scalar(i16f[:, CAPS:CAP], i16f[:, CAPS:CAP], float(NS), None, ALU.add).then_inc(S("top"), 1)
            u = ("gi", l)
            ps = filled(v, u)
            step(v.tensor_copy(gateT, ps[0:CAP, 0:16]))
            release(v.tensor_copy(idxT, ps[0:CAP, 16:32]), u)

        def route_pool(g, l):
            for t in range(NT):
                emptied(g, ("hr", l, t))
            g.dma_start(DR["h", l].rearrange("(t p) d -> p t d", p=P), hrow).then_inc(S("h_stored"), 16)

        xe = [hflat[0:CAP, 1024 * i:1024 * i + 1024] for i in range(2)]
        ye = [hflat[0:CAP, 2048 + 1024 * i:3072 + 1024 * i] for i in range(2)]
        xeT = [ar(20000 + 640 * i, 2, 4 * CAP) for i in range(2)]
        hid = [ar(21280 + 320 * i, FT, CAP) for i in range(2)]
        slu = [hflat[:, 4096 + 80 * i:4176 + 80 * i] for i in range(2)]
        PER = (1, 2, 2, 1)

        def moe_pe(pe, l):
            while units.next % 4:
                u = ("skip", l, units.next)
                take(pe, u)
                units.uses[units.of[u][0]] -= 1
            base = list(units.uses)
            moe_base[l] = base

            def take_at(pair, i, n):
                pe.wait_ge(pair_free[pair], i * PER[pair] + (base[pair] + n))

            def gather_T(i, par):
                pe.wait_ge(S(f"gathered{par}"), (i - par) * 8 + (16 + 128 * l))
                take_at(0, i, 0)
                ps = PSUM[:, 0, :]
                for k in range(KD):
                    o = 512 * (k // 4) + CAP * (k % 4)
                    last = pe.transpose(ps[:, o:o + CAP], xe[par][:, k * P:k * P + P], ident[0:CAP, 0:CAP])
                last.then_inc(pair_full[0], 1)

            def expert(i, par, nxt):
                s = 3 * par
                w1, w3 = (slots[s + j].rearrange("p (k n) -> p k n", n=FF) for j in range(2))
                w2 = slots[s + 2].rearrange("p (k n) -> p k n", n=D)
                pe.wait_ge(pair_free[0], i + (base[0] + 1))
                for j in range(2):
                    pe.wait_ge(w_here[s + j], (i - par) * 8 + 16 * (slot_of["exp", l, s + j] + 1))
                for f in range(FT):
                    pair = 1 + f % 2
                    take_at(pair, i, f // 2)
                    ps = PSUM[:, pair, :]
                    for w, o in ((w1, 0), (w3, 512)):
                        last = mmk(pe, ps[:, o:o + CAP], lambda k: w[:, k, f * P:f * P + P],
                                   lambda k: xeT[par][:, k // 4, CAP * (k % 4):CAP * (k % 4) + CAP])
                    last.then_inc(pair_full[pair], 1)
                if nxt is not None:
                    gather_T(nxt, 1 - par)
                pe.wait_ge(w_here[s + 2], (i - par) * 8 + 16 * (slot_of["exp", l, s + 2] + 1))
                take_at(3, i, 0)
                for f0, f1 in ((0, FT - 1), (FT - 1, FT)):
                    if f0 == 0:
                        pe.wait_ge(pair_free[1], i * 2 + (base[1] + 2))
                        pe.wait_ge(pair_free[2], i * 2 + (base[2] + 1))
                    else:
                        pe.wait_ge(pair_free[2], i * 2 + (base[2] + 2))
                    for half in range(2):
                        for f in range(f0, f1):
                            last = pe.matmul(PSUM[0:CAP, 3, 512 * half:512 * half + 512], hid[par][:, f, :],
                                             w2[:, f, 512 * half:512 * half + 512], start=(f == 0), stop=(f == FT - 1))
                last.then_inc(pair_full[3], 1)

            gather_T(0, 0)
            with pe.Fori(0, NE // 2 - 1) as i:
                expert(i * 2, 0, i * 2 + 1)
                expert(i * 2 + 1, 1, i * 2 + 2)
            expert(NE - 2, 0, NE - 1)
            expert(NE - 1, 1, None)
            for pair in range(4):
                units.uses[pair] = base[pair] + NE * PER[pair]

        def moe_act_run(act, l):
            base = moe_base[l]

            def xt(i, par):
                act.wait_ge(pair_full[0], i + (base[0] + 1))
                ps = PSUM[:, 0, :].rearrange("p (a b) -> p a b", a=2)[:, :, 0:4 * CAP]
                act.activation(xeT[par], ps, ACT.Copy).then_inc(pair_free[0], 1)

            def expert(i, par, nxt):
                for f in range(FT):
                    pair = 1 + f % 2
                    act.wait_ge(pair_full[pair], i * 2 + (base[pair] + f // 2 + 1))
                    act.wait_ge(pair_free[pair], i * 2 + (base[pair] + f // 2))
                    act.activation(slu[f % 2], PSUM[:, pair, 0:CAP], ACT.Silu).then_inc(S("silu"), 1)
                if nxt is not None:
                    xt(nxt, 1 - par)
                act.wait_ge(pair_full[3], i + (base[3] + 1))
                act.wait_ge(S(f"y_room{par}"), (i - par) * 8 + (16 + 128 * l))
                act.activation(ye[par][:, 0:512], PSUM[0:CAP, 3, 0:512], ACT.Copy, scale=gateT[:, bass.ds(i, 1)])\
                    .then_inc(S("y_low"), 1)

            emptied(act, ("gi", l))
            xt(0, 0)
            with act.Fori(0, NE // 2 - 1) as i:
                expert(i * 2, 0, i * 2 + 1)
                expert(i * 2 + 1, 1, i * 2 + 2)
            expert(NE - 2, 0, NE - 1)
            expert(NE - 1, 1, None)

        def moe_dve(v, l):
            base = moe_base[l]

            def expert(i, par):
                for f in range(FT):
                    pair = 1 + f % 2
                    v.wait_ge(S("silu"), i * 4 + (64 * l + f + 1))
                    v.tensor_tensor(hid[par][:, f, :], slu[f % 2], PSUM[:, pair, 512:512 + CAP], ALU.mult)\
                        .then_inc(pair_free[pair], 1)
                v.wait_ge(pair_full[3], i + (base[3] + 1))
                v.wait_ge(S("y_low"), i + (16 * l + 1))
                v.tensor_scalar(ye[par][:, 512:1024], PSUM[0:CAP, 3, 512:1024], gateT[:, bass.ds(i, 1)], None,
                                ALU.mult).then_inc(pair_free[3], 1)

            emptied(v, ("gi", l))
            with v.Fori(0, NE // 2) as i:
                expert(i * 2, 0)
                expert(i * 2 + 1, 1)

        def moe_pool(g, l):
            base = moe_base[l]
            emptied(g, ("gi", l))
            g.wait_ge(S("h_stored"), 16 * (l + 1))
            off = lambda e: bass.IndirectOffsetOnAxis(ap=idxT[:, e:e + 1], axis=0)

            def gather(e):
                if e >= 2:
                    g.wait_ge(pair_full[0], base[0] + e - 1)
                g.indirect_dma_start(xe[e % 2], None, DR["h", l], off(e)).then_inc(S(f"gathered{e % 2}"), 16)

            gather(0)
            for e in range(NE):
                if e + 1 < NE:
                    gather(e + 1)
                g.wait_ge(pair_free[3], base[3] + e + 1)
                if e:
                    g.wait_ge(S(f"y_room{(e - 1) % 2}"), 16 * ((e - 1) // 2 + 1) + 16 + 128 * l)
                g.indirect_dma_start(DR["m", l], off(e), ye[e % 2], None, compute_op=ALU.add)\
                    .then_inc(S(f"y_room{e % 2}"), 16)

        def load_stream(sp):
            for c, s, prev in loads:
                if c[0] != "experts":
                    if prev is not None:
                        if prev[0] == "experts":
                            l = prev[1]
                            pair, n = (2, 2 * (NE - 1)) if s < 2 else (3, NE - 1)
                            sp.wait_ge(pair_full[pair], moe_base[l][pair] + n)
                        else:
                            filled(sp, chunk_last[prev])
                    src, n = chunk_src(c)
                    sp.dma_start(chunk(c), src.rearrange("(k p) n -> p k n", p=P)).then_inc(w_here[s], 16)
                else:
                    experts_stream(sp, c[1], prev)

        def experts_stream(sp, l, prev):
            base = moe_base[l]

            def load(i, par, j, wait):
                s = 3 * par + j
                if wait:
                    pair = 3 if j == 2 else 2
                    sp.wait_ge(pair_full[pair], i * PER[pair] + (base[pair] - PER[pair]))
                w = (W1, W3, W2)[j][l]
                kk = FT if j == 2 else KD
                n = D if j == 2 else FF
                src = w[:, bass.ds(i * kk, kk), :]
                sp.dma_start(slots[s].rearrange("p (k n) -> p k n", n=n), src).then_inc(w_here[s], 16)

            for j in range(3):
                filled(sp, chunk_last[prev[j]])
                load(0, 0, j, False)
            sp.wait_ge(S("arena_free"), l + 1)
            for j in range(3):
                load(1, 1, j, False)
            with sp.Fori(1, NE // 2) as i:
                for par in range(2):
                    for j in range(3):
                        load(i * 2 + par, par, j, True)

        def gather_sum_act(act, l):
            for par in range(2):
                act.wait_ge(S(f"y_room{par}"), 16 + 128 + 128 * l)
            for pair in range(4):
                act.wait_ge(pair_free[pair], moe_base[l][pair] + NE * PER[pair])
            act.dma_start(rows_m, DR["m", l].rearrange("(t p) d -> p t d", p=P)).then_inc(S("m_rows"), 16)

        def sum_pe(pe, l):
            pe.wait_ge(S("m_rows"), 16 * (l + 1))
            for k in range(KD):
                u = ("ms", l, k)
                ps = take(pe, u)
                for t in range(NT):
                    last = pe.transpose(ps[:, t * P:t * P + P], rows_m[:, t, k * P:k * P + P], ident)
                finish(last, u)

        def sum_dve(v, step, l):
            for k in range(KD):
                u = ("ms", l, k)
                add_gated(v, l, 5, k, filled(v, u), u, k == KD - 1)
            v.wait_ge(S("x_half"), xh[0])
            for k in range(4, KD):
                emptied(v, ("ms", l, k))
            v.memset(sm[:, 250:251], 0.0).then_inc(S("x_ready"), 1)

        def store_pe(pe):
            pe.wait_ge(S("x_ready"), 4)
            for t in range(NT):
                u = ("xr", t)
                ps = take(pe, u)
                for k in range(KD):
                    last = pe.transpose(ps[:, k * P:k * P + P], xT[:, k, t * P:t * P + P], ident)
                finish(last, u)

        def store_read(eng, part):
            for t in range(part, NT, 2):
                u = ("xr", t)
                release(copy(eng, rows[:, t, :], filled(eng, u)), u)

        def store_sp(sp, n_out):
            for t in range(NT):
                emptied(sp, ("xr", t))
                dst = outs["y_sample"][0, t * P:t * P + P, :] if t < ST else outs["y_prompt"][0]
                sp.dma_start(dst, rows[:, t, :]).then_inc(S("outputs"), 16)
            sp.wait_ge(S("outputs"), 16 * NT)
            sp.wait_ge(S("caches"), 16 * n_out)

        pad = ar(0, 12, PADW)
        gate = ar(7752, NT, 512)
        z2 = ar(10312, NT, 784)
        zq = z2[:, :, 16:528].rearrange("p t (h d) -> p t h d", d=HD)
        zk = z2[:, :, 528:656].rearrange("p t (h d) -> p t h d", d=HD)
        zo = z2[:, :, 16:528]
        gqT = ar(14232, 4, T)
        gkT = ar(16792, 2, 768)
        gp = [ar(18328 + 640 * i, T) for i in range(2)]
        gaT = [ar(19608 + 640 * i, T) for i in range(2)]
        gscr = ar(18328, NT * 8, HD)
        kdup = ar(20888, NT, 256)
        cdup = ar(22168, 256)
        GI = [(t, h) for t in range(NT) for h in range(8)]
        beta = sm[:, 256:296]
        gdec = sm[:, 296:336]
        gsm = sm[:, 336:496]
        eG = sm[:, 496:536]
        eGL = sm[:, 536:576]
        bG = sm[:, 576:616]
        dx, de, dz, dz2, do_ = (ar(22700 + 40 * i, 40) for i in range(5))
        t8 = lambda x: x.rearrange("p (t q) -> p t q", q=8)

        def gqa_act(act, step):
            for c in (4, 5):
                for tp in range(3):
                    emptied(act, ("pR", 1, c, tp))
            act.activation(t8(beta), z2[:, :, 0:8], ACT.Tanh, scale=0.5).then_inc(S("dl_tanh"), 1)
            act.activation(anl, alog, ACT.Exp).then_inc(S("dl_tanh"), 1)
            act.wait_ge(S("dl_x"), 1)
            softplus_act(act, step, dx, de).then_inc(S("sp_exp"), 1)
            hn_act(act, zq, 0, gscr.rearrange("p (t h) d -> p t h d", h=8), 1.0 / HD, ssq)
            act.wait_ge(S("gq_done"), 1)
            hn_act(act, zk, 0, gscr[:, 0:10, :].rearrange("p (t h) d -> p t h d", h=2), 1.0 / HD, ssq[:, 0:10])
            for g in range(4):
                release(copy(act, gqT[:, g, :], filled(act, ("gqT", g))[:, 0:T]), ("gqT", g))
            for n in range(2):
                release(copy(act, gkT[:, n, :], filled(act, ("gkT", n))[:, 0:768]), ("gkT", n))

            def exps(i):
                t, h = GI[i]
                n = T if t < ST else P
                act.wait_ge(S("g_max"), i + 1)
                if i >= 2:
                    emptied(act, ("go", i - 2))
                u = ("gs", i)
                release(act.activation(gp[i % 2][:, 0:n], filled(act, u)[:, 0:n], ACT.Exp, scale=HD ** -0.5,
                                       bias=smx[:, i % 2:i % 2 + 1], accum_out=smx[:, 8 + i % 2:9 + i % 2]), u)

            for i in range(len(GI)):
                exps(i)
            for b in range(4):
                release(copy(act, hT[:, 4 + b, :], filled(act, ("gyT", b))[:, 0:T]), ("gyT", b))

        def gqa_dve(v, step):
            for c in (4, 5):
                for tp in range(3):
                    emptied(v, ("pR", 1, c, tp))
            v.tensor_tensor(t8(dx), z2[:, :, 8:16], dtb.unsqueeze(1).broadcast_to((P, NT, 8)), ALU.add)\
                .then_inc(S("dl_x"), 1)
            v.wait_ge(S("dl_x"), 1)
            v.wait_ge(S("dl_tanh"), 2)
            step(v.tensor_scalar(beta, beta, 0.5, 0.5, ALU.mult, ALU.add))
            v.wait_ge(S("sp_exp"), 2)
            softplus_dve(v, step, dx, de, dz, dz2, do_)
            step(v.scalar_tensor_tensor(out=t8(gdec), in0=t8(do_), scalar=-1.0,
                                        in1=anl.unsqueeze(1).broadcast_to((P, NT, 8)), op0=ALU.mult, op1=ALU.mult))
            hn_dve(v, step, 4, zq, gscr, ssq, 8, HD, gqg)
            v.memset(smx[:, 20:21], 0.0).then_inc(S("gq_done"), 1)
            hn_dve(v, step, 5, zk, gscr[:, 0:10, :], ssq[:, 0:10], 2, HD, gkg)
            v.memset(smx[:, 21:22], 0.0).then_inc(S("cache_k_ready"), 1)
            rs = ar(18328, 4096)
            rope_dve(v, step, zq[:, 0:ST], 8, rs)
            rope_dve(v, step, zk[:, 0:ST], 2, rs)
            for r in range(2):
                step(v.tensor_copy(kdup.rearrange("p t (n r d) -> p t n r d", n=2, r=2)[:, :, :, r, :], zk))
                step(v.tensor_copy(cdup.rearrange("p (n r d) -> p n r d", n=2, r=2)[:, :, r, :],
                                   gk_c[:, :].rearrange("p (n d) -> p n d", n=2)))
            v.memset(smx[:, 22:23], 0.0).then_inc(S("qk_rows"), 1)

            def maxes(i):
                n = T if GI[i][0] < ST else P
                if i >= 2:
                    emptied(v, ("gs", i - 2))
                v.tensor_reduce(smx[:, 4 + i % 2:5 + i % 2], filled(v, ("gs", i))[:, 0:n], AX_X, ALU.max)\
                    .then_inc(S("g_mx1"), 1)
                v.wait_ge(S("g_mx1"), i + 1)
                v.tensor_scalar(smx[:, i % 2:i % 2 + 1], smx[:, 4 + i % 2:5 + i % 2], -HD ** -0.5, None, ALU.mult)\
                    .then_inc(S("g_max"), 1)

            def rows_out(i):
                t, h = GI[i]
                emptied(v, ("gs", i))
                step(v.reciprocal(smx[:, 12 + i % 2:13 + i % 2], smx[:, 8 + i % 2:9 + i % 2]))
                release(v.tensor_scalar(zo[:, t, h * HD:h * HD + HD], filled(v, ("go", i))[:, 0:HD],
                                    smx[:, 12 + i % 2:13 + i % 2], None,
                                        ALU.mult), ("go", i))

            maxes(0)
            for i in range(len(GI)):
                if i + 1 < len(GI):
                    maxes(i + 1)
                n = T if GI[i][0] < ST else P
                if i >= 2:
                    filled(v, ("go", i - 2))
                release(v.tensor_copy(gaT[i % 2][:, 0:n], filled(v, ("gaT", i))[:, 0:n]), ("gaT", i))
                if i >= 1:
                    rows_out(i - 1)
            rows_out(len(GI) - 1)

        def gqa_pe(pe):
            pe.wait_ge(S("qk_rows"), 2)
            for g in range(4):
                u = ("gqT", g)
                ps = take(pe, u)
                for t in range(NT):
                    last = pe.transpose(ps[:, t * P:t * P + P], zo[:, t, g * P:g * P + P], ident)
                finish(last, u)
            for n in range(2):
                u = ("gkT", n)
                ps = take(pe, u)
                pe.transpose(ps[:, 0:P], cdup[:, n * P:n * P + P], ident)
                for t in range(NT):
                    last = pe.transpose(ps[:, (t + 1) * P:(t + 2) * P], kdup[:, t, n * P:n * P + P], ident)
                finish(last, u)
            for g in range(4):
                emptied(pe, ("gqT", g))
            emptied(pe, ("gkT", 0))
            emptied(pe, ("gkT", 1))

            def scores(i):
                t, h = GI[i]
                r = slice(64 * (h % 2), 64 * (h % 2) + 64)
                u = ("gs", i)
                ps = take(pe, u)
                q = gqT[r, h // 2, t * P:t * P + P]
                k = gkT[r, h // 4, :]
                if t < ST:
                    pe.matmul(ps[:, 0:512], q, k[:, 0:512], start=True, stop=True)
                    last = pe.matmul(ps[:, 512:T], q, k[:, 512:T], start=True, stop=True)
                else:
                    last = pe.matmul(ps[:, 0:P], q, k[:, T:768], start=True, stop=True)
                finish(last, u)

            scores(0)
            for i, (t, h) in enumerate(GI):
                if i + 1 < len(GI):
                    scores(i + 1)
                nk = NT if t < ST else 1
                emptied(pe, ("gs", i))
                u = ("gaT", i)
                ps = take(pe, u)
                for j in range(nk):
                    last = pe.transpose(ps[:, j * P:j * P + P], gp[i % 2][:, j * P:j * P + P], ident)
                finish(last, u)
                u = ("go", i)
                ps = take(pe, u)
                emptied(pe, ("gaT", i))
                o = 64 * (h // 4)
                for j in range(nk):
                    vals = z2[:, ST, 656 + o:720 + o] if t == ST else \
                        gv_c[:, o:o + HD] if j == 0 else z2[:, j - 1, 656 + o:720 + o]
                    last = pe.matmul(ps[:, 0:HD], gaT[i % 2][:, j * P:j * P + P], vals, start=(j == 0), stop=(j == nk - 1))
                finish(last, u)
            for i in range(len(GI) - 3, len(GI)):
                emptied(pe, ("go", i))
            for b in range(4):
                u = ("gyT", b)
                ps = take(pe, u)
                for t in range(NT):
                    last = pe.transpose(ps[:, t * P:t * P + P], zo[:, t, b * P:b * P + P], ident)
                finish(last, u)

        cv = [ar(15432 + UW * i, UW) for i in range(3)]
        dq, dk, dv = ar(10312, NT, 512), ar(12872, NT, 512), ar(0, NT, 512)
        dqkv = (dq, dk, dv)
        oacc = ar(15432, NT, 512)
        dscr2 = ar(18040, NT * 4, P)
        dbase = (18040, 2560)
        slot = lambda d, i, n=1: ar(dbase[d] + 512 * i, 4 * n, P)
        KT_U, QT_W, DA_KB, DB_QK, A_VB, AM_KT, X_, XT_, WT_VN, QD_ = range(10)
        sdec = [hflat[:, 512 * d:512 * d + 512].rearrange("p (h v) -> p h v", h=4) for d in range(2)]
        tile_of = lambda n, d: 4 if n == 4 else n if d == 0 else 3 - n
        chunk_at = lambda ci, d: ci if d == 0 else 1 - ci
        LEV = ["f", "b"]

        def over_heads(x):
            return x.unsqueeze(1).broadcast_to((P, 4, P))

        def per_head(x, t, d):
            return x[:, 8 * t + 4 * d:8 * t + 4 * d + 4].unsqueeze(2).broadcast_to((P, 4, P))

        def conv_pe(pe):
            for ct in range(12):
                pe.wait_ge(S("cv_silu"), ct + 1)
                u = ("cvT", ct)
                ps = take(pe, u)
                c = cv[ct % 3]
                for t in range(NT):
                    o = t * P if t < ST else UP0
                    last = pe.transpose(ps[:, t * P:t * P + P], c[:, o:o + P], ident)
                finish(last, u)

        def conv_read(eng, ct):
            u = ("cvT", ct)
            dst = dqkv[ct // 4][:, :, (ct % 4) * P:(ct % 4) * P + P]
            release(copy(eng, dst, filled(eng, u)[:, 0:T].rearrange("p (t c) -> p t c", c=P)), u)

        def heads4(x):
            return x.rearrange("p t (h d) -> p t h d", d=P)

        def delta_pe(pe):
            pe.wait_ge(S("dl_g"), 1)
            ps = take(pe, "G")
            gv = gdec.rearrange("p (t d h) -> p t d h", d=2, h=4)
            pv = ps[:, 0:40].rearrange("p (t d h) -> p t d h", d=2, h=4)
            for d in range(2):
                pe.matmul(pv[:, :, d, :], C[("up_one", "lo_one")[d]], gv[:, :, d, :], start=True, stop=True)
            pe.matmul(ps[:, 40:80], C["block"], gdec, start=True, stop=True)
            for c in range(2):
                last = pe.matmul(ps[:, 80 + 512 * c:120 + 512 * c], ones[64 * c:64 * c + 64, :], gdec[64 * c:64 * c + 64, :],
                                 start=True, stop=True)
            finish(last, "G")
            conv_pe(pe)
            pe.wait_ge(S("dn_rows"), 1)
            for n in range(5):
                for d in range(2):
                    t = tile_of(n, d)
                    u = ("kq", n, d)
                    ps = take(pe, u)
                    for h in range(4):
                        pe.transpose(ps[:, h * P:h * P + P], dk[:, t, h * P:h * P + P], ident)
                        last = pe.transpose(ps[:, 512 + h * P:640 + h * P], dq[:, t, h * P:h * P + P], ident)
                    finish(last, u)
                for d in range(2):
                    pe.wait_ge(S("dl_diag"), 2 * n + d + 1)
                    u = ("dec", n, d)
                    ps = take(pe, u)
                    pe.matmul(ps[:, 0:512], ones, slot(d, XT_), start=True, stop=False)
                    for h in range(4):
                        last = pe.matmul(ps[:, h * P:h * P + P], slot(d, X_)[:, h, :], ones, start=False, stop=(h == 3))
                    finish(last, u)
                for d in range(2):
                    u = ("kk", n, d)
                    emptied(pe, ("kq", n, d))
                    ps = take(pe, u)
                    for h in range(4):
                        k = slot(d, KT_U)[:, h, :]
                        pe.matmul(ps[:, h * P:h * P + P], k, k, start=True, stop=True)
                        last = pe.matmul(ps[:, 512 + h * P:640 + h * P], k, slot(d, QT_W)[:, h, :], start=True, stop=True)
                    finish(last, u)
                for d in range(2):
                    pe.wait_ge(S("dl_qd"), 2 * n + d + 1)
                    u = ("qd", n, d)
                    ps = take(pe, u)
                    for h in range(4):
                        last = pe.transpose(ps[:, h * P:h * P + P], slot(d, WT_VN)[:, h, :], ident)
                    finish(last, u)
                for d in range(2):
                    pe.wait_ge(S(f"dl_am{d}"), 6 * n + 1)
                    u = ("am", n, d)
                    ps = take(pe, u)
                    for h in range(4):
                        last = pe.transpose(ps[:, h * P:h * P + P], slot(d, AM_KT)[:, h, :], ident)
                    finish(last, u)
                for s in range(1, 6):
                    for d in range(2):
                        pe.wait_ge(S(f"dl_am{d}"), 6 * n + s + 1)
                        if s == 1:
                            pe.wait_ge(S(f"dl_x0{d}"), n + 1)
                        else:
                            emptied(pe, ("x", n, d, s - 1))
                        u = ("w", n, d, s)
                        ps = take(pe, u)
                        for h in range(4):
                            last = pe.matmul(ps[:, h * P:h * P + P], slot(d, AM_KT)[:, h, :], slot(d, XT_)[:, h, :],
                                             start=True, stop=True)
                        finish(last, u)
                    for d in range(2):
                        emptied(pe, ("w", n, d, s))
                        u = ("x", n, d, s)
                        ps = take(pe, u)
                        for h in range(4):
                            if s < 5:
                                pe.matmul(ps[:, h * P:h * P + P], slot(d, WT_VN)[:, h, :], slot(d, X_)[:, h, :],
                                          start=True, stop=True)
                            last = pe.matmul(ps[:, 512 + h * P:640 + h * P], slot(d, X_)[:, h, :],
                                             slot(d, WT_VN)[:, h, :], start=True, stop=True)
                        finish(last, u)
                for d in range(2):
                    emptied(pe, ("x", n, d, 5))
                    pe.wait_ge(S(f"dl_kv{d}"), n + 1)
                    u = ("wu", n, d)
                    ps = take(pe, u)
                    for h in range(4):
                        xt = slot(d, XT_)[:, h, :]
                        pe.matmul(ps[:, h * P:h * P + P], xt, slot(d, A_VB)[:, h, :], start=True, stop=True)
                        last = pe.matmul(ps[:, 512 + h * P:640 + h * P], slot(d, DA_KB)[:, h, :], xt,
                                         start=True, stop=True)
                    finish(last, u)
                for ci in range(2):
                    for d in range(2):
                        c = chunk_at(ci, d)
                        r = slice(64 * c, 64 * c + 64)
                        if ci == 0:
                            emptied(pe, ("wu", n, d))
                            if n == 4:
                                pe.wait_ge(S("dl_zero"), 2)
                            elif n:
                                emptied(pe, ("os", n - 1, d, 1))
                        else:
                            emptied(pe, ("os", n, d, 0))
                        u = ("vs", n, d, ci)
                        ps = take(pe, u)
                        for h in range(4):
                            last = pe.matmul(ps[r, h * P:h * P + P], slot(d, QT_W)[:, h, r], sdel[:, 4 * d + h, :],
                                             start=True, stop=True)
                        finish(last, u)
                    for d in range(2):
                        c = chunk_at(ci, d)
                        r = slice(64 * c, 64 * c + 64)
                        emptied(pe, ("vs", n, d, ci))
                        u = ("os", n, d, ci)
                        ps = take(pe, u)
                        for h in range(4):
                            pe.matmul(ps[r, h * P:h * P + P], slot(d, QD_)[:, h, r], sdel[:, 4 * d + h, :],
                                      start=True, stop=False)
                            pe.matmul(ps[r, h * P:h * P + P], slot(d, DB_QK)[r, h, r], slot(d, WT_VN)[r, h, :],
                                      start=False, stop=True)
                        for h in range(4):
                            last = pe.matmul(ps[:, 512 + h * P:640 + h * P], slot(d, AM_KT)[r, h, :],
                                             slot(d, WT_VN)[r, h, :], start=True, stop=True)
                        finish(last, u)
            pe.wait_ge(S("dy_rows"), 2)
            for b in range(4):
                u = ("cyT", b)
                ps = take(pe, u)
                for t in range(NT):
                    last = pe.transpose(ps[:, t * P:t * P + P], oacc[:, t, b * P:b * P + P], ident)
                finish(last, u)

        def delta_act(act, step):
            act.wait_ge(S("dl_gsm"), 1)
            act.activation(eG, gsm[:, 0:40], ACT.Exp).then_inc(S("dl_eg"), 1)
            act.activation(eGL, eGL, ACT.Exp).then_inc(S("dl_eg"), 1)
            act.activation(gsm[:, 80:160], gsm[:, 80:160], ACT.Exp).then_inc(S("dl_eg"), 1)
            for tp in range(3):
                emptied(act, ("pR", 1, 3, tp))
            act.activation(gate, gate, ACT.Silu).then_inc(S("gate_silu"), 1)
            for ct in range(12):
                act.wait_ge(S("cv_done"), ct + 1)
                act.activation(cv[ct % 3], cv[ct % 3], ACT.Silu).then_inc(S("cv_silu"), 1)
                if ct >= 1 and (ct - 1) % 2 == 0:
                    conv_read(act, ct - 1)
            scr = dscr2.rearrange("p (t h) d -> p t h d", h=4)
            for c in range(8):
                emptied(act, ("cvT", c))
            hn_act(act, heads4(dq), 0, scr, 1.0, ssq[:, 0:20])
            act.wait_ge(S("dq2_done"), 1)
            hn_act(act, heads4(dk), 0, scr, 1.0, ssq[:, 0:20])
            for n in range(5):
                for d in range(2):
                    if n:
                        emptied(act, ("vs", n - 1, d, 1))
                    if n == 0:
                        act.wait_ge(S("dn_rows"), 1)
                    u = ("kq", n, d)
                    release(copy(act, slot(d, KT_U, 2), filled(act, u).rearrange("p (h c) -> p h c", c=P)), u)
                for d in range(2):
                    emptied(act, ("dec", n, d))
                    act.activation(slot(d, DA_KB, 2), slot(d, DA_KB, 2), ACT.Exp).then_inc(S("dl_exp"), 1)
                for d in range(2):
                    if n:
                        filled(act, ("os", n - 1, d, 1))
                    u = ("qd", n, d)
                    release(copy(act, slot(d, QD_), filled(act, u)[:, 0:512].rearrange("p (h c) -> p h c", c=P)), u)
                for s in range(1, 6):
                    for d in range(2):
                        if s > 1:
                            filled(act, ("x", n, d, s - 1))
                        u = ("w", n, d, s)
                        release(copy(act, slot(d, WT_VN), filled(act, u)[:, 0:512].rearrange("p (h c) -> p h c", c=P)), u)
                for d in range(2):
                    u = ("wu", n, d)
                    release(copy(act, slot(d, KT_U, 2), filled(act, u).rearrange("p (h c) -> p h c", c=P)), u)
            act.wait_ge(S("d_rows"), 2)
            hn_act(act, heads4(oacc), 0, scr, 1.0 / P, ssq[:, 0:20])
            for b in range(4):
                release(copy(act, hT[:, b, :], filled(act, ("cyT", b))[:, 0:T]), ("cyT", b))

        def delta_dve(v, step):
            v.memset(smx[:, 20:21], 0.0).then_inc(S("dl_g"), 1)
            ps = filled(v, "G")
            step(v.tensor_copy(gsm[:, 0:120], ps[:, 0:120]))
            release(v.tensor_copy(gsm[:, 120:160], ps[:, 592:632]), "G")
            emptied(v, "G")
            v.tensor_tensor(eGL, gsm[:, 40:80], gsm[:, 0:40], ALU.subtract).then_inc(S("dl_gsm"), 1)
            v.wait_ge(S("dl_eg"), 3)
            step(v.tensor_tensor(bG, beta, eG, ALU.mult))
            for b in range(4):
                filled(v, ("gyT", b))
            v.wait_ge(S("pad_evac0"), 8)
            v.wait_ge(S("pad_evac1"), 8)
            v.wait_ge(S("caches"), 80)
            for ct in range(12):
                emptied(v, ("pT", 1, ct // 4, ct % 4))
                if ct >= 3:
                    filled(v, ("cvT", ct - 3))
                conv_dve(v, step, cv[ct % 3], pad[:, ct, :],
                         lambda tap: cB[:, dw_col + 12 * tap + ct:dw_col + 12 * tap + ct + 1], None)\
                    .then_inc(S("cv_done"), 1)
                if ct >= 2 and ct % 2 == 0:
                    conv_read(v, ct - 1)
            conv_read(v, 11)
            for c in range(12):
                emptied(v, ("cvT", c))
            hn_dve(v, step, 6, heads4(dq), dscr2, ssq[:, 0:20], 4, P, None, mul=P ** -0.5)
            v.memset(smx[:, 20:21], 0.0).then_inc(S("dq2_done"), 1)
            hn_dve(v, step, 7, heads4(dk), dscr2, ssq[:, 0:20], 4, P, None)
            v.memset(smx[:, 21:22], 0.0).then_inc(S("dn_rows"), 1)
            neg = ("lo_neg", "up_neg")
            for n in range(5):
                for d in range(2):
                    t = tile_of(n, d)
                    step(v.tensor_tensor(slot(d, X_), over_heads(ident), per_head(gsm, t, d), ALU.mult))
                    v.tensor_scalar(slot(d, XT_), slot(d, X_), -1.0, None, ALU.mult).then_inc(S("dl_diag"), 1)
                for d in range(2):
                    u = ("dec", n, d)
                    ps = filled(v, u)[:, 0:512].rearrange("p (h c) -> p h c", c=P)
                    step(v.tensor_tensor(slot(d, DA_KB), ps, over_heads(C[neg[d]]), ALU.add))
                    release(v.tensor_tensor(slot(d, DB_QK), over_heads(C[neg[1 - d]]), ps, ALU.subtract), u)
                for d in range(2):
                    t = tile_of(n, d)
                    v.wait_ge(S("dl_exp"), 2 * n + d + 1)
                    u = ("kk", n, d)
                    ps = filled(v, u).rearrange("p (h c) -> p h c", c=P)
                    step(v.tensor_tensor(slot(d, A_VB), ps[:, 0:4], slot(d, DA_KB), ALU.mult))
                    release(v.tensor_tensor(slot(d, DB_QK), ps[:, 4:8], slot(d, DB_QK), ALU.mult), u)
                    v.tensor_tensor(slot(d, A_VB), slot(d, A_VB), per_head(beta, t, d), ALU.mult)\
                        .then_inc(S(f"dl_A{d}"), 1)
                for d in range(2):
                    v.wait_ge(S(f"dl_am{d}"), 6 * n + 1)
                    u = ("am", n, d)
                    ps = filled(v, u)[:, 0:512].rearrange("p (h c) -> p h c", c=P)
                    release(v.tensor_tensor(slot(d, XT_), over_heads(ident), ps, ALU.subtract), u)
                    emptied(v, u)
                    v.tensor_tensor(slot(d, X_), over_heads(ident), slot(d, AM_KT), ALU.subtract)\
                        .then_inc(S(f"dl_x0{d}"), 1)
                    v.wait_ge(S(f"dl_x0{d}"), n + 1)
                for s in range(1, 6):
                    for d in range(2):
                        u = ("x", n, d, s)
                        ps = filled(v, u).rearrange("p (h c) -> p h c", c=P)
                        if s < 5:
                            release(v.tensor_tensor(slot(d, X_, 2), slot(d, X_, 2), ps, ALU.subtract), u)
                        else:
                            release(v.tensor_tensor(slot(d, XT_), slot(d, XT_), ps[:, 4:8], ALU.subtract), u)
                        emptied(v, u)
                for ci in range(2):
                    for d in range(2):
                        c = chunk_at(ci, d)
                        r = slice(64 * c, 64 * c + 64)
                        emptied(v, ("wu", n, d))
                        u = ("vs", n, d, ci)
                        ps = filled(v, u)[r, 0:512].rearrange("p (h c) -> p h c", c=P)
                        release(v.tensor_tensor(slot(d, WT_VN)[r], slot(d, KT_U)[r], ps, ALU.subtract), u)
                    for d in range(2):
                        c = chunk_at(ci, d)
                        r = slice(64 * c, 64 * c + 64)
                        t = tile_of(n, d)
                        u = ("os", n, d, ci)
                        ps = filled(v, u)
                        first = n < 2 if n < 4 else ci == 0
                        if first:
                            step(v.tensor_copy(oacc[r, t, :], ps[r, 0:512]))
                        else:
                            step(v.tensor_tensor(oacc[r, t, :], oacc[r, t, :], ps[r, 0:512], ALU.add))
                        v.wait_ge(S(f"dl_sd{d}"), 2 * n + ci + 1)
                        release(v.tensor_tensor(sdel[:, 4 * d:4 * d + 4, :], sdec[d],
                                                ps[:, 512:1024].rearrange("p (h c) -> p h c", c=P), ALU.add), u)
                        emptied(v, u)
                        if n == 3 and ci == 1:
                            v.memset(sdel[:, 4 * d:4 * d + 4, :], 0.0).then_inc(S("dl_zero"), 1)
            v.memset(smx[:, 23:24], 0.0).then_inc(S("d_rows"), 1)
            hn_dve(v, step, 8, heads4(oacc), dscr2, ssq[:, 0:20], 4, P, dng)
            v.wait_ge(S("gate_silu"), 1)
            v.tensor_tensor(oacc, oacc, gate, ALU.mult).then_inc(S("dy_rows"), 1)

        def delta_pool(g, step):
            g.wait_ge(S("dn_rows"), 1)
            r4 = lambda x: x.rearrange("p (h d) -> p h d", d=P)
            for n in range(5):
                for d in range(2):
                    t = tile_of(n, d)
                    if n:
                        filled(g, ("os", n - 1, d, 1))
                    g.tensor_tensor(slot(d, WT_VN), r4(dq[:, t, :]), per_head(eG, t, d), ALU.mult)\
                        .then_inc(S("dl_qd"), 1)
                for s in range(6):
                    for d in range(2):
                        if s == 0:
                            g.wait_ge(S(f"dl_A{d}"), n + 1)
                        elif s == 1:
                            g.wait_ge(S(f"dl_x0{d}"), n + 1)
                        else:
                            filled(g, ("w", n, d, s - 1))
                        g.tensor_tensor(slot(d, AM_KT), slot(d, A_VB), over_heads(C[f"{LEV[d]}{s}"]), ALU.mult)\
                            .then_inc(S(f"dl_am{d}"), 1)
                for d in range(2):
                    t = tile_of(n, d)
                    filled(g, ("w", n, d, 5))
                    g.wait_ge(S(f"dl_am{d}"), 6 * n + 6)
                    step(g.tensor_tensor(slot(d, DA_KB), r4(dk[:, t, :]), per_head(bG, t, d), ALU.mult))
                    step(g.tensor_tensor(slot(d, A_VB), r4(dv[:, t, :]), per_head(beta, t, d), ALU.mult))
                    g.tensor_tensor(slot(d, AM_KT), r4(dk[:, t, :]), per_head(eGL, t, d), ALU.mult)\
                        .then_inc(S(f"dl_kv{d}"), 1)
                for ci in range(2):
                    for d in range(2):
                        t = tile_of(n, d)
                        if ci:
                            emptied(g, ("os", n, d, 0))
                        elif n == 4:
                            g.wait_ge(S("dl_zero"), 2)
                        elif n:
                            emptied(g, ("os", n - 1, d, 1))
                        cd = gsm[:, 80 + 40 * chunk_at(ci, d):]
                        g.tensor_tensor(sdec[d], sdel[:, 4 * d:4 * d + 4, :], per_head(cd, t, d), ALU.mult)\
                            .then_inc(S(f"dl_sd{d}"), 1)
            for d in range(2):
                emptied(g, ("os", 4, d, 1))
            g.dma_start(outs["new_state_delta"][0, 0].rearrange("r h k v -> k (r h) v"), sdel[:, :, :])\
                .then_inc(S("caches"), 16)

        def layer1_outputs(g):
            g.wait_ge(S("cache_k_ready"), 2)
            g.dma_start(outs["new_cache_gqa_k"].rearrange("a b t h d -> t (a b h d)"), z2[:, ST, 528:656])\
                .then_inc(S("caches"), 16)
            g.dma_start(outs["new_cache_gqa_v"].rearrange("a b t h d -> t (a b h d)"), z2[:, ST, 656:784])\
                .then_inc(S("caches"), 16)

        def layer1_ready(pe):
            for b in range(4):
                emptied(pe, ("gyT", b))
                emptied(pe, ("cyT", b))

        ctx.enter_context(nc.allow_non_contiguous_dma(reason="weights' column chunks"))
        block = ctx.enter_context(nc.Block())

        @block.tensor
        def _(pe):
            setup_pe(pe)
            for l in range(2):
                mod_pe(pe, l, 0)
                mod_pe(pe, l, 1)
                norm_pe(pe, l, 0)
                pe.wait_ge(S("h_ready"), 32 * l + 16)
                for c in range(2 + l):
                    proj_T_pe(pe, l, c)
                for c in range(2 + l, 5 + l):
                    proj_R_pe(pe, l, c)
                for m in range(2, 6):
                    mod_pe(pe, l, m)
                if l == 0:
                    lru_pe(pe)
                    diff_pe(pe)
                else:
                    gqa_pe(pe)
                    delta_pe(pe)
                out_pe(pe, l)
                norm_pe(pe, l, 1)
                route_pe(pe, l)
                moe_pe(pe, l)
                sum_pe(pe, l)
            store_pe(pe)

        @block.scalar
        def _(act):
            step = Steps(act, S("act_step"))
            setup_act(act, step)
            for l in range(2):
                norm_act(act, step, l, 0)
                if l == 0:
                    read_T(act, 0, 0, xap, 0, True)
                    read_T(act, 0, 1, ga, 0, False)
                    for c in (2, 3, 4):
                        read_R(act, 0, c, qkv[:, :, 512 * (c - 2):512 * (c - 1)], 0)
                    lru_act(act, step)
                    diff_act(act, step)
                else:
                    for c in range(3):
                        read_T(act, 1, c, pad[:, 4 * c:4 * c + 4, :], 0, True)
                    read_R(act, 1, 3, gate, 0)
                    read_R(act, 1, 4, z2[:, :, 0:512], 0)
                    read_R(act, 1, 5, z2[:, :, 512:784], 0)
                    act.wait_ge(S("h_dead"), 2)
                    gqa_act(act, step)
                    delta_act(act, step)
                norm_act(act, step, l, 1)
                route_act(act, step, l)
                moe_act_run(act, l)
                gather_sum_act(act, l)
            store_read(act, 0)

        @block.vector
        def _(v):
            step = Steps(v, S("dve_step"))
            setup_dve(v, step)
            for l in range(2):
                mod_dve(v, step, l, 0)
                mod_dve(v, step, l, 1)
                norm_dve(v, step, l, 0)
                if l == 0:
                    pads_dve(v, step, xap)
                    read_T(v, 0, 0, xap, 1, True)
                    read_T(v, 0, 1, ga, 1, False)
                    for c in (2, 3, 4):
                        read_R(v, 0, c, qkv[:, :, 512 * (c - 2):512 * (c - 1)], 1)
                else:
                    pads_dve(v, step, pad)
                    for c in range(3):
                        read_T(v, 1, c, pad[:, 4 * c:4 * c + 4, :], 1, True)
                    read_R(v, 1, 3, gate, 1)
                    read_R(v, 1, 4, z2[:, :, 0:512], 1)
                    read_R(v, 1, 5, z2[:, :, 512:784], 1)
                for m in range(2, 6):
                    mod_dve(v, step, l, m)
                v.memset(sm[:, 252:253], 0.0).then_inc(S("h_dead"), 1)
                if l == 0:
                    lru_dve(v, step)
                    diff_dve(v, step)
                else:
                    gqa_dve(v, step)
                    delta_dve(v, step)
                out_dve(v, step, l)
                norm_dve(v, step, l, 1)
                v.memset(sm[:, 253:254], 0.0).then_inc(S("arena_free"), 1)
                route_dve(v, step, l)
                moe_dve(v, l)
                sum_dve(v, step, l)
            store_read(v, 1)

        @block.gpsimd
        def _(g):
            step = Steps(g, S("pool_step"))
            setup_pool(g)
            layer0_outputs(g)
            route_pool(g, 0)
            moe_pool(g, 0)
            layer1_outputs(g)
            delta_pool(g, step)
            route_pool(g, 1)
            moe_pool(g, 1)

        @block.sync
        def _(sp):
            load_stream(sp)
            store_sp(sp, 6)


_PLAIN = ["x_prompt", "x_sample", "cache_diff_k", "cache_diff_v", "state_delta", "cache_gqa_k", "cache_gqa_v",
          "w_mod", "w_in_ab", "lru_wa", "lru_wi", "w_in_cd", "w_out", "router_w", "exp_w1", "exp_w3", "exp_w2"]
_OUTS = {"y_prompt": (1, 128, 1024), "y_sample": (1, 512, 1024), "new_state_lru": (1, 1, 2, 512),
         "new_cache_diff_k": (1, 1, 128, 4, 2, 64), "new_cache_diff_v": (1, 1, 128, 4, 128),
         "new_state_delta": (1, 1, 2, 4, 128, 128), "new_cache_gqa_k": (1, 1, 128, 2, 64),
         "new_cache_gqa_v": (1, 1, 128, 2, 64)}


def layout(inputs):
    import numpy as np
    a = {k: np.ascontiguousarray(inputs[k]) for k in _PLAIN}
    r = lambda k: np.asarray(inputs[k]).reshape(-1, P)
    a["colsA"] = np.concatenate([r(k) for k in ("norm1_g", "norm2_g", "b_mod")])
    a["colsB"] = np.concatenate([r(k) for k in ("c", "c_ctx", "lru_conv_b", "lru_ba", "lru_bi", "lru_lam", "state_lru",
                                                "lru_conv_w", "delta_conv_w")])
    a["params"] = np.concatenate([np.asarray(inputs[k]).reshape(1, -1) for k in
                                  ("diff_q_gain", "diff_k_gain", "gqa_q_gain", "gqa_k_gain", "diff_sub_gain",
                                   "delta_norm_g", "delta_a_log", "delta_dt_bias", "diff_lam")], axis=1)
    t = np.arange(NS)
    inv = (10000.0 ** (-np.arange(16, dtype=np.float32) / 16)).astype(np.float32)
    ang = np.concatenate([(t // 64).astype(np.float32)[:, None] * inv, (t % 64).astype(np.float32)[:, None] * inv], 1)
    a["rope"] = np.concatenate([np.cos(ang), np.sin(ang)], 1).astype(np.float32)
    i, j = np.arange(P)[:, None], np.arange(P)[None, :]
    same = i // CK == j // CK
    lo, up = same & (j <= i), same & (j >= i)
    c = [i == j, i >= 0 * j, np.where(lo, 0.0, NEG), np.where(up, 0.0, NEG), lo, up, same]
    lev = [(i // (2 << s) == j // (2 << s)) & (i // (1 << s) > j // (1 << s)) for s in range(6)]
    c += lev + [m.T for m in lev]
    a["consts"] = np.stack([np.broadcast_to(m, (P, P)).astype(np.float32) for m in c])
    return a


def program(nc, arrays):
    io = {k: nc.dram_tensor("in_" + k, v.shape, F32, kind="ExternalInput").ap() for k, v in arrays.items()}
    outs = {k: nc.dram_tensor("out_" + k, s, F32, kind="ExternalOutput").ap() for k, s in _OUTS.items()}
    build(nc, io, outs)


def kernel(**inputs):
    import concourse.bacc as _bacc
    from concourse.bass_utils import run_bass_kernel_spmd as _run
    arrays = layout(inputs)
    nc = _bacc.Bacc("TRN2", target_bir_lowering=False, num_devices=1)
    program(nc, arrays)
    r = _run(nc, [{"in_" + k: v for k, v in arrays.items()}], core_ids=[0])
    return tuple(r.results[0]["out_" + k] for k in _OUTS)
```

```python
from contextlib import ExitStack

import concourse.bass as bass
from concourse import mybir

F32 = mybir.dt.float32
U32 = mybir.dt.uint32
ACT = mybir.ActivationFunctionType
ALU = mybir.AluOpType
AX_X = mybir.AxisListType.X

P = 128
D = 1024
KD = D // P
NS, NP = 512, 128
T = NS + NP
NT = T // P
ST = NS // P
HD = 64
PADW = NS + NP + 6
PS0, PP0 = 2, NS + 5
UW = PADW - 3
UP0 = NS + 3
NE, CAPS, CAPP = 16, 64, 16
CAP = CAPS + CAPP
FF = 512
FT = FF // P
NIN_AB, NIN_CD = 2560, 2832
CK = 64
NEG = -1.0e30
LAM_INIT = 0.2
CONSTS = ["ident", "ones", "lo_neg", "up_neg", "lo_one", "up_one", "block"] + [f"f{s}" for s in range(6)] + \
         [f"b{s}" for s in range(6)]


class Units:

    def __init__(self):
        self.uses = [0] * 4
        self.of = {}
        self.next = 0

    def add(self, name, pair=None):
        if pair is None:
            pair = self.next % 4
            self.next += 1
        self.uses[pair] += 1
        self.of[name] = (pair, self.uses[pair])
        return self.of[name]


class Steps:

    def __init__(self, eng, sem):
        self.eng, self.sem, self.n = eng, sem, 0

    def __call__(self, ins):
        self.n += 1
        ins.then_inc(self.sem, 1)
        self.eng.wait_ge(self.sem, self.n)


def build(nc, io, outs, dbg=None, stop=None):
    with ExitStack() as ctx:
        def sb(name, shape, dt=F32):
            return ctx.enter_context(nc.sbuf_tensor(name, shape, dt))

        sems = {}

        def S(name):
            if name not in sems:
                sems[name] = ctx.enter_context(nc.semaphore("s_" + name))
            return sems[name]

        PSUM = ctx.enter_context(nc.psum_tensor("pairs", [P, 4, 1024], F32))
        pair_full = [S(f"pair_full{i}") for i in range(4)]
        pair_free = [S(f"pair_free{i}") for i in range(4)]
        units = Units()

        xT = sb("xT", [P, KD, T])
        hT = sb("hT", [P, KD, T])
        ring = sb("ring", [P, 3, 4096])
        cst = sb("cst", [P, len(CONSTS), P])
        rope = sb("rope", [P, ST, HD])
        cA = sb("cA", [P, P])
        cB = sb("cB", [P, P])
        par = sb("par", [P, 784])
        modt = sb("modt", [P, 2, 48, 2])
        gsc = sb("gsc", [P, 2, 2, KD, 2])
        csil = sb("csil", [P, KD, 2])
        dk_c = sb("dk_c", [P, 512])
        dv_c = sb("dv_c", [P, 512])
        gk_c = sb("gk_c", [P, 128])
        gv_c = sb("gv_c", [P, 128])
        sdel = sb("sdel", [P, 8, P])
        wr = sb("wr", [P, 2, KD, NE])
        sm = sb("sm", [P, 640])
        AR = 23400
        arena = sb("arena", [P, AR])

        C = {n: cst[:, i, :] for i, n in enumerate(CONSTS)}
        ident, ones = C["ident"], C["ones"]

        def ar(off, *shape):
            n = 1
            for x in shape:
                n *= x
            assert off + n <= AR, (off, n)
            v = arena[:, off:off + n]
            if len(shape) == 2:
                v = v.rearrange("p (a b) -> p a b", b=shape[1])
            elif len(shape) == 3:
                v = v.rearrange("p (a b c) -> p a b c", b=shape[1], c=shape[2])
            return v

        hflat = hT[:, :, :].rearrange("p k t -> p (k t)")
        rows = ar(0, NT, D)
        c_cols, cb_col, ba_col, bi_col, lam_col, st_col, lw_col, dw_col = \
            cB[:, 0:16], 16, 20, 28, 36, 44, 52, 68
        dqg, dkg, gqg, gkg = (par[:, 64 * i:64 * i + 64] for i in range(4))
        dsg, dng = par[:, 256:384], par[:, 384:512]
        alog, dtb = par[:, 512:520], par[:, 520:528]
        dlam = par[:, 528:784]
        hs = sm[:, 0:8]
        nlam = sm[:, 8:9]
        hba, hbi = sm[:, 16:24], sm[:, 24:32]
        spt = sm[:, 32:112]
        stl = sm[:, 112:120]
        smx = sm[:, 120:160]
        nmax = lambda i, c=0: smx[:, 2 * (i % 4) + c:2 * (i % 4) + c + 1]
        psum_of = lambda i, c=0, n=1: smx[:, 8 + 2 * (i % 4) + c:8 + 2 * (i % 4) + c + n]
        rsum = lambda i, c=0, n=1: smx[:, 16 + 2 * (i % 4) + c:16 + 2 * (i % 4) + c + n]
        ratio = lambda i: smx[:, 24 + i % 4:25 + i % 4]
        ssq = sm[:, 160:200]
        sps = sm[:, 200:208]
        anl = sm[:, 208:216]

        DR = {}
        for l in range(2):
            DR["h", l] = nc.dram_tensor(f"h_rows{l}", (T, D), F32, kind="Internal").ap()
            DR["m", l] = nc.dram_tensor(f"moe_rows{l}", (T, D), F32, kind="Internal").ap()

        def take(pe, name, pair=None):
            pair, n = units.add(name, pair)
            if n > 1:
                pe.wait_ge(pair_free[pair], n - 1)
            return PSUM[:, pair, :]

        def finish(ins, name):
            ins.then_inc(pair_full[units.of[name][0]], 1)

        def filled(eng, name):
            pair, n = units.of[name]
            eng.wait_ge(pair_full[pair], n)
            return PSUM[:, pair, :]

        def release(ins, name):
            ins.then_inc(pair_free[units.of[name][0]], 1)

        def emptied(eng, name):
            pair, n = units.of[name]
            eng.wait_ge(pair_free[pair], n)

        def mmk(pe, out, lhs, rhs):
            for k in range(KD):
                last = pe.matmul(out, lhs(k), rhs(k), start=(k == 0), stop=(k == KD - 1))
            return last

        mods = [[("mod", l, m, h) for m in range(6) for h in range(2)] for l in range(2)]
        ins = [[("in", l, c, 0) for c in range(5 + l)] for l in range(2)]
        wouts = [[("out", l, h, 0) for h in range(2)] for l in range(2)]
        N_DIFF_MODS = 7
        chunks = [mods[0][:4] + ins[0] + mods[0][4:] + mods[1][:N_DIFF_MODS] + wouts[0] + mods[1][N_DIFF_MODS:],
                  ins[1] + wouts[1]]
        slot_of, slot_uses = {}, [0] * 6
        last_in_slot = {}
        loads = []
        for l in range(2):
            for i, c in enumerate(chunks[l]):
                s = i % 3
                slot_uses[s] += 1
                slot_of[c] = (s, slot_uses[s])
                loads.append((c, s, last_in_slot.get(s)))
                last_in_slot[s] = c
            base = list(slot_uses)
            for s in range(6):
                slot_uses[s] += NE // 2
                slot_of["exp", l, s] = base[s]
            loads.append((("experts", l), None, dict(last_in_slot)))
            for s in range(3):
                last_in_slot[s] = ("experts", l)
        slots = [ring[:, s, :] for s in range(3)] + [ar(4096 * s, 4096) for s in range(3)]
        w_here = [S(f"w_here{s}") for s in range(6)]

        def chunk_src(c):
            kind, l, a, b = c
            if kind == "mod":
                return io["w_mod"][l][:, 1024 * a + 512 * b:1024 * a + 512 * b + 512], 512
            if kind == "in":
                w = io["w_in_ab" if l == 0 else "w_in_cd"][0]
                n = min(512, w.shape[1] - 512 * a)
                return w[:, 512 * a:512 * a + n], n
            return io["w_out"][l][:, 512 * a:512 * a + 512], 512

        def chunk(c):
            n = chunk_src(c)[1]
            return slots[slot_of[c][0]][:, 0:KD * n].rearrange("p (k n) -> p k n", n=n)

        def arrived(pe, c):
            s, n = slot_of[c]
            pe.wait_ge(w_here[s], 16 * n)
            return chunk(c)

        chunk_last = {}

        W1 = [io["exp_w1"][l].rearrange("e (k p) f -> p (e k) f", p=P) for l in range(2)]
        W3 = [io["exp_w3"][l].rearrange("e (k p) f -> p (e k) f", p=P) for l in range(2)]
        W2 = [io["exp_w2"][l].rearrange("e (k p) d -> p (e k) d", p=P) for l in range(2)]
        moe_base = {}

        N_CONST = 17

        def setup_dma(act):
            q = S("const_here")
            act.dma_start(cst[:, :, :], io["consts"].rearrange("n p m -> p n m")).then_inc(q, 16)
            act.dma_start(rows[:, 0:ST, :], io["x_sample"][0].rearrange("(t p) d -> p t d", p=P)).then_inc(q, 16)
            act.dma_start(rows[:, ST, :], io["x_prompt"][0]).then_inc(q, 16)
            act.dma_start(ar(6000, 128), io["colsA"]).then_inc(q, 16)
            act.dma_start(ar(6200, 128)[0:116, :], io["colsB"]).then_inc(q, 16)
            act.dma_start(par[:, :], io["params"].to_broadcast((P, 784))).then_inc(q, 16)
            act.dma_start(rope[:, :, :], io["rope"].rearrange("(t p) n -> p t n", p=P)).then_inc(q, 16)
            act.dma_start(dk_c[:, :], io["cache_diff_k"][0, 0].rearrange("t h c d -> t (h c d)")).then_inc(q, 16)
            act.dma_start(dv_c[:, :], io["cache_diff_v"][0, 0].rearrange("t h d -> t (h d)")).then_inc(q, 16)
            act.dma_start(gk_c[:, :], io["cache_gqa_k"][0, 0].rearrange("t h d -> t (h d)")).then_inc(q, 16)
            act.dma_start(gv_c[:, :], io["cache_gqa_v"][0, 0].rearrange("t h d -> t (h d)")).then_inc(q, 16)
            act.dma_start(sdel[:, :, :], io["state_delta"][0, 0].rearrange("r h k v -> k (r h) v")).then_inc(q, 16)
            for l in range(2):
                act.dma_start(wr[:, l, :, :], io["router_w"][l].rearrange("(k p) e -> p k e", p=P)).then_inc(q, 16)

        wg = ar(10000, 16, P).rearrange("p (q c) m -> p q c m", c=4)

        def setup_gates_dma(act):
            q = S("const_here")
            for r in range(2):
                for i, w in enumerate(("lru_wa", "lru_wi")):
                    for half in range(2):
                        src = io[w][0, r].rearrange("(t h) c d -> h c t d", h=2)[half]
                        act.dma_start(wg[64 * half:64 * half + 64, 2 * r + i, :, 64 * half:64 * half + 64],
                                      src).then_inc(q, 16)
        CONST_ALL = 16 * (14 + 8)

        def setup_pe(pe):
            pe.wait_ge(S("const_here"), CONST_ALL)
            ps = take(pe, "cols")
            pe.transpose(ps[:, 0:P], ar(6000, 128), ident)
            finish(pe.transpose(ps[:, 512:628], ar(6200, 128)[0:116, :], ident[0:116, 0:116]), "cols")
            flip_in_pe(pe, "x_in")

        def flip_in_pe(pe, tag):
            for k in range(KD):
                ps = take(pe, (tag, k))
                for t in range(NT):
                    last = pe.transpose(ps[:, t * P:t * P + P], rows[:, t, k * P:k * P + P], ident)
                finish(last, (tag, k))

        def flip_out_pe(pe, tag, src):
            for t in range(NT):
                ps = take(pe, (tag, t))
                for k in range(KD):
                    last = pe.transpose(ps[:, k * P:k * P + P], src[:, k, t * P:t * P + P], ident)
                finish(last, (tag, t))

        def copy(eng, dst, src):
            return eng.activation(dst, src, ACT.Copy) if eng is nc.scalar else eng.tensor_copy(dst, src)

        def flip_in_read(eng, tag, part):
            for k in range(part, KD, 2):
                release(copy(eng, xT[:, k, :], filled(eng, (tag, k))[:, 0:T]), (tag, k))

        def flip_out_read(eng, tag, part):
            for t in range(part, NT, 2):
                release(copy(eng, rows[:, t, :], filled(eng, (tag, t))), (tag, t))

        def softplus_act(act, step, x, e):
            step(act.activation(e, x, ACT.Abs))
            return act.activation(e, e, ACT.Exp, scale=-1.0)

        def softplus_dve(v, step, x, e, z, z2, out):
            step(v.tensor_scalar(z, e, 2.0, None, ALU.add))
            step(v.reciprocal(z, z))
            step(v.tensor_tensor(z, e, z, ALU.mult))
            step(v.tensor_tensor(z2, z, z, ALU.mult))
            step(v.tensor_scalar(e, z2, 1.0 / 17, 1.0 / 15, ALU.mult, ALU.add))
            for n in (13, 11, 9, 7, 5, 3, 1):
                step(v.tensor_tensor(e, e, z2, ALU.mult))
                step(v.tensor_scalar(e, e, 1.0 / n, None, ALU.add))
            step(v.tensor_tensor(e, e, z, ALU.mult))
            step(v.tensor_scalar(z, x, 0.0, None, ALU.max))
            step(v.scalar_tensor_tensor(out=out, in0=e, scalar=2.0, in1=z, op0=ALU.mult, op1=ALU.add))

        negl = sm[:, 216:224]

        def setup_act(act, step):
            setup_dma(act)
            act.wait_ge(S("zeroed"), 2)
            setup_gates_dma(act)
            flip_in_read(act, "x_in", 0)
            act.wait_ge(S("cB"), 1)
            act.activation(csil[:, :, :].rearrange("p k g -> p g k"), c_cols.rearrange("p (g k) -> p g k", g=2),
                           ACT.Silu).then_inc(S("csil"), 1)
            act.wait_ge(S("negl"), 1)
            softplus_act(act, step, negl, spt[:, 0:8]).then_inc(S("sp_exp"), 1)
            act.wait_ge(S("lam_dot"), 1)
            act.activation(sps[:, 2:4], sps[:, 0:2], ACT.Exp).then_inc(S("lam_exp"), 1)

        def setup_dve(v, step):
            v.memset(hflat, 0.0).then_inc(S("zeroed"), 1)
            v.memset(ar(10000, 2048), 0.0).then_inc(S("zeroed"), 1)
            ps = filled(v, "cols")
            v.tensor_copy(cB[:, 0:116], ps[:, 512:628]).then_inc(S("cB"), 1)
            release(v.tensor_copy(cA[:, :], ps[:, 0:P]), "cols")
            flip_in_read(v, "x_in", 1)
            v.wait_ge(S("cB"), 1)
            v.tensor_scalar(negl, cB[:, lam_col:lam_col + 8], -1.0, None, ALU.mult).then_inc(S("negl"), 1)
            v.wait_ge(S("negl"), 1)
            v.wait_ge(S("sp_exp"), 1)
            softplus_dve(v, step, negl, spt[:, 0:8], spt[:, 8:16], spt[:, 16:24], spt[:, 24:32])
            step(v.tensor_scalar(hs, spt[:, 24:32], -4.0, None, ALU.mult))
            step(v.tensor_scalar(hba, cB[:, ba_col:ba_col + 8], 0.5, None, ALU.mult))
            step(v.tensor_scalar(hbi, cB[:, bi_col:bi_col + 8], 0.5, None, ALU.mult))
            v.wait_ge(S("const_here"), CONST_ALL)
            dl = dlam.rearrange("p (a b d) -> p a b d", a=2, b=2)
            step(v.tensor_tensor(ar(6400, 2, 64), dl[:, :, 0, :], dl[:, :, 1, :], ALU.mult))
            v.tensor_reduce(sps[:, 0:2], ar(6400, 2, 64), AX_X, ALU.add).then_inc(S("lam_dot"), 1)
            v.wait_ge(S("lam_exp"), 1)
            step(v.tensor_tensor(sps[:, 4:5], sps[:, 3:4], sps[:, 2:3], ALU.subtract))
            step(v.tensor_scalar(nlam, sps[:, 4:5], -LAM_INIT, None, ALU.add))
            step(v.tensor_scalar(dsg, dsg, 1.0 - LAM_INIT, None, ALU.mult))
            step(v.tensor_scalar(dqg, dqg, HD ** -0.5, None, ALU.mult))
            step(v.tensor_scalar(gqg, gqg, HD ** -0.5, None, ALU.mult))

        def setup_pool(g):
            g.wait_ge(S("zeroed"), 1)
            for l in range(2):
                g.dma_start(DR["m", l].rearrange("(t p) d -> p t d", p=P),
                            hflat.rearrange("p (t d) -> p t d", t=NT)).then_inc(S(f"y_room{l}"), 16)

        mrow = [ar(22360 + 512 * i, 512)[0:2, :] for i in range(2)]
        all_mods = mods[0] + mods[1]

        def mod_rows_pe(pe, i, pair=None):
            c = all_mods[i]
            if i == 0:
                pe.wait_ge(S("csil"), 1)
            w = arrived(pe, c)
            u = ("mod_rows", i)
            ps = take(pe, u, pair)
            finish(mmk(pe, ps[0:2, 0:512], lambda k: csil[:, k, :], lambda k: w[:, k, :]), u)
            chunk_last[c] = u

        def mod_turn_pe(pe, i, pair=None):
            emptied(pe, ("mod_rows", i))
            u = ("mod", i)
            ps = take(pe, u, pair)
            for f in range(4):
                last = pe.transpose(ps[:, 2 * f:2 * f + 2], mrow[i % 2][:, f * P:f * P + P], ident[0:2, 0:2])
            finish(last, u)

        def mod_act(act, i):
            if i >= 2:
                filled(act, ("mod", i - 2))
            u = ("mod_rows", i)
            release(copy(act, mrow[i % 2], filled(act, u)[0:2, 0:512]), u)

        def mod_dve(v, step, i):
            _, l, m, h = all_mods[i]
            u = ("mod", i)
            c0 = 8 * m + 4 * h
            ps = filled(v, u)[:, 0:8].rearrange("p (f g) -> p f g", g=2)
            b = cA[:, 32 + 48 * l + c0:32 + 48 * l + c0 + 4].unsqueeze(2).broadcast_to((P, 4, 2))
            if i == 0:
                emptied(v, "cols")
            release(v.tensor_tensor(modt[:, l, c0:c0 + 4, :], ps, b, ALU.add), u)
            if m in (1, 4) and h == 1:
                emptied(v, u)
                emptied(v, ("mod", i - 1))
                n = m // 4
                g = cA[:, 16 * n + 8 * l:16 * n + 8 * l + 8].unsqueeze(2).broadcast_to((P, KD, 2))
                step(v.scalar_tensor_tensor(out=gsc[:, l, n, :, :], in0=modt[:, l, 8 * m:8 * m + 8, :], scalar=1.0,
                                            in1=g, op0=ALU.add, op1=ALU.mult))

        def mods_done(eng, i):
            for j in range(max(0, i - 3), i + 1):
                emptied(eng, ("mod", j))

        sq = ar(20000, 2, T)
        ssum = ar(21280, T)
        rstd = ar(19300, T)
        seg = ((0, NS), (NS, T))

        def norm_pe(pe, l, n):
            u = ("nrm", l, n)
            pe.wait_ge(S("sq_add"), 7 * (2 * l + n) + 7)
            ps = take(pe, u)
            pe.matmul(ps[:, 0:NS], ones, ssum[:, 0:NS], start=True, stop=True)
            finish(pe.matmul(ps[:, NS:T], ones, ssum[:, NS:T], start=True, stop=True), u)

        def x_unit(l, n, k):
            return ("x_in", k) if (l, n) == (0, 0) else ("out", l, k) if n else ("ms", l - 1, k)

        def norm_squares_act(act, l, n):
            i = 2 * l + n
            if n == 1:
                act.wait_ge(S("caches"), (48, 96)[l])
            for k in range(KD):
                emptied(act, x_unit(l, n, k))
                if i:
                    act.wait_ge(S("x_half"), 8 * (i - 1) + k + 1)
                if k >= 2:
                    act.wait_ge(S("sq_add"), 7 * i + max(1, k - 2))
                act.activation(sq[:, k % 2, :], xT[:, k, :], ACT.Square).then_inc(S("sq"), 1)

        def norm_root_act(act, l, n):
            ps = filled(act, ("nrm", l, n))
            release(act.activation(rstd, ps[:, 0:T], ACT.Sqrt, scale=1.0 / D, bias=1e-6), ("nrm", l, n))

        def norm_shift_act(act, l, n):
            i = 2 * l + n
            for k in range(KD):
                for g in range(2):
                    a, b = seg[g]
                    act.wait_ge(S("h_scaled"), i * 16 + 2 * k + g + 1)
                    act.activation(hT[:, k, a:b], hT[:, k, a:b], ACT.Identity,
                                   bias=modt[:, l, 24 * n + k, g:g + 1]).then_inc(S("h_ready"), 1)

        def norm_add_dve(v, l, n, k):
            i = 2 * l + n
            v.wait_ge(S("sq"), 8 * i + k + 1)
            if k > 1:
                v.wait_ge(S("sq_add"), 7 * i + k - 1)
            v.tensor_tensor(ssum, sq[:, 0, :] if k == 1 else ssum, sq[:, k % 2, :], ALU.add).then_inc(S("sq_add"), 1)

        def norm_dve(v, step, l, n):
            i = 2 * l + n
            emptied(v, ("nrm", l, n))
            step(v.reciprocal(rstd, rstd))
            if i == 0:
                v.wait_ge(S("y_room0"), 16)
                v.wait_ge(S("y_room1"), 16)
            for k in range(KD):
                emptied(v, x_unit(l, n, k))
                for g in range(2):
                    a, b = seg[g]
                    v.scalar_tensor_tensor(out=hT[:, k, a:b], in0=xT[:, k, a:b], scalar=gsc[:, l, n, k, g:g + 1],
                                           in1=rstd[:, a:b], op0=ALU.mult, op1=ALU.mult)\
                        .then_inc(S("h_scaled"), 1)

        def proj_T_pe(pe, l, c):
            w = arrived(pe, ("in", l, c, 0))
            for f in range(4):
                u = ("pT", l, c, f)
                ps = take(pe, u)
                lhs = lambda k: w[:, k, f * P:f * P + P]
                if c == 0 and f == 0:
                    for k in range(KD):
                        pe.wait_ge(S("h_ready"), 32 * l + 2 * k + 2)
                        pe.matmul(ps[:, 0:NS], lhs(k), hT[:, k, 0:NS], start=(k == 0), stop=(k == KD - 1))
                        last = pe.matmul(ps[:, NS:T], lhs(k), hT[:, k, NS:T], start=(k == 0), stop=(k == KD - 1))
                    finish(last, u)
                    continue
                mmk(pe, ps[:, 0:NS], lhs, lambda k: hT[:, k, 0:NS])
                finish(mmk(pe, ps[:, NS:T], lhs, lambda k: hT[:, k, NS:T]), u)
            chunk_last["in", l, c, 0] = u

        def proj_R_pe(pe, l, c):
            w = arrived(pe, ("in", l, c, 0))
            n = chunk_src(("in", l, c, 0))[1]
            for tp in range(3):
                u = ("pR", l, c, tp)
                ps = take(pe, u)
                for t in range(2 * tp, min(2 * tp + 2, NT)):
                    o = 512 * (t % 2)
                    last = mmk(pe, ps[:, o:o + n], lambda k: hT[:, k, t * P:t * P + P], lambda k: w[:, k, 0:n])
                finish(last, u)
            chunk_last["in", l, c, 0] = u

        def read_T(eng, l, c, dst, part, padded):
            for f in range(part, 4, 2):
                u = ("pT", l, c, f)
                ps = filled(eng, u)
                if padded:
                    copy(eng, dst[:, f, PS0:PS0 + NS], ps[:, 0:NS]).then_inc(S("pad_evac" + str(part)), 1)
                    release(copy(eng, dst[:, f, PP0:PP0 + NP], ps[:, NS:T]), u)
                else:
                    release(copy(eng, dst[:, f, :], ps[:, 0:T]), u)

        def read_R(eng, l, c, dst, part):
            n = chunk_src(("in", l, c, 0))[1]
            for tp in range(3):
                if (tp + c) % 2 == part:
                    u = ("pR", l, c, tp)
                    ps = filled(eng, u)
                    m = 2 if tp < 2 else 1
                    release(copy(eng, dst[:, 2 * tp:2 * tp + m, :],
                                 ps.rearrange("p (a b) -> p a b", a=2)[:, 0:m, 0:n]), u)

        xap = ar(0, 4, PADW)
        ga = ar(2584, 4, T)
        qkv = ar(12048, NT, 1536)
        uT = ar(5144, 4, UW)
        gb = [ar(7716 + 2 * i * UW, 2, UW) for i in range(1)] + [None]
        lb = [[hflat[:, 2560 + 0 * UW:2560 + UW], hflat[:, 2560 + UW:2560 + 2 * UW],
               hflat[:, 2560 + 2 * UW:2560 + 3 * UW], ar(7716, UW)],
              [ar(7716 + UW, UW), ar(7716 + 2 * UW, UW), ar(19728 + 0 * UW, UW), ar(19728 + UW, UW)]]
        hfb = [ar(19728 + 2 * UW, UW), ar(19728 + 3 * UW, UW)]

        def pads_dve(v, step, pad):
            step(v.memset(pad[:, :, 0:2], 0.0))
            step(v.memset(pad[:, :, PS0 + NS:PP0], 0.0))
            step(v.memset(pad[:, :, PADW - 1:PADW], 0.0))

        def conv_dve(v, step, out, src, w, b):
            if b is None:
                step(v.tensor_scalar(out, src[:, 0:UW], w(0), None, ALU.mult))
            else:
                step(v.tensor_scalar(out, src[:, 0:UW], w(0), b, ALU.mult, ALU.add))
            for tap in range(1, 4):
                ins = v.scalar_tensor_tensor(out=out, in0=src[:, tap:tap + UW], scalar=w(tap), in1=out,
                                             op0=ALU.mult, op1=ALU.add)
                if tap < 3:
                    step(ins)
            return ins

        def lru_pe(pe):
            for ct in range(4):
                pe.wait_ge(S("u_ready"), ct + 1)
                for q in range(4):
                    u = ("gate", ct, q)
                    ps = take(pe, u)
                    pe.matmul(ps[:, 0:NS], wg[:, q, ct, :], uT[:, ct, 0:NS], start=True, stop=True)
                    finish(pe.matmul(ps[:, NS:UW], wg[:, q, ct, :], uT[:, ct, NS:UW], start=True, stop=True), u)
                    if q % 2 == 1:
                        i = 2 * ct + q // 2
                        mod_rows_pe(pe, 4 + i)
                        if i:
                            mod_turn_pe(pe, 3 + i)
            mod_turn_pe(pe, 11)

        def lru_act(act, step):
            for i in range(9):
                if i < 8:
                    ct, d = i // 2, i % 2
                    tr, ti, a, _ = lb[i % 2]
                    c8 = 4 * d + ct
                    if i == 0:
                        filled(act, ("pR", 0, 4, 2))
                    if i >= 2:
                        act.wait_ge(S("lru_scan"), i - 1)
                    release(act.activation(tr, filled(act, ("gate", ct, 2 * d))[:, 0:UW], ACT.Tanh, scale=0.5,
                                           bias=hba[:, c8:c8 + 1]), ("gate", ct, 2 * d))
                    release(act.activation(ti, filled(act, ("gate", ct, 2 * d + 1))[:, 0:UW], ACT.Tanh, scale=0.5,
                                           bias=hbi[:, c8:c8 + 1]), ("gate", ct, 2 * d + 1))
                    emptied(act, ("gate", ct, 2 * d))
                    step(act.activation(a, tr, ACT.Exp, scale=hs[:, c8:c8 + 1], bias=hs[:, c8:c8 + 1]))
                    act.activation(tr, tr, ACT.Tanh, scale=hs[:, c8:c8 + 1], bias=hs[:, c8:c8 + 1])\
                        .then_inc(S("lru_tanh"), 1)
                if i >= 1:
                    act.wait_ge(S("lru_q"), i)
                    tr = lb[(i - 1) % 2][0]
                    act.activation(tr, tr, ACT.Sqrt).then_inc(S("lru_root"), 1)
                if i < 8:
                    mod_act(act, 4 + i)
            for f in range(4):
                emptied(act, ("pT", 0, 1, f))
            act.activation(ga, ga, ACT.Gelu_apprx_tanh).then_inc(S("gelu"), 1)

        def lru_dve(v, step):
            for part in range(2):
                v.wait_ge(S("pad_evac" + str(part)), 2)
            for ct in range(4):
                emptied(v, ("pT", 0, 0, ct))
                conv_dve(v, step, uT[:, ct, :], xap[:, ct, :], lambda tap: cB[:, lw_col + 4 * tap + ct:lw_col + 4 * tap + ct + 1],
                         cB[:, cb_col + ct:cb_col + ct + 1]).then_inc(S("u_ready"), 1)
            filled(v, ("pR", 0, 4, 2))
            v.wait_ge(S("u_ready"), 4)
            for i in range(9):
                if i < 8:
                    tr, ti, a, w = lb[i % 2]
                    v.wait_ge(S("lru_tanh"), i + 1)
                    step(v.tensor_scalar(w, tr, -1.0, 1.0, ALU.mult, ALU.add))
                    step(v.reciprocal(w, w))
                    v.scalar_tensor_tensor(out=tr, in0=tr, scalar=-0.5, in1=w, op0=ALU.mult, op1=ALU.mult)\
                        .then_inc(S("lru_q"), 1)
                    step(v.scalar_tensor_tensor(out=ti, in0=ti, scalar=1.0, in1=uT[:, i // 2, :], op0=ALU.add,
                                                op1=ALU.mult))
                if i >= 1:
                    j = i - 1
                    ct, d = j // 2, j % 2
                    tr, ti, a, w = lb[j % 2]
                    c8 = 4 * d + ct
                    v.wait_ge(S("lru_root"), j + 1)
                    step(v.tensor_tensor(ti, ti, tr, ALU.mult))
                    h = hfb[d]
                    r = slice(None, None, 1 if d == 0 else -1)
                    step(v.tensor_tensor_scan(h[:, 0:NS][:, r], a[:, 0:NS][:, r], ti[:, 0:NS][:, r],
                                              cB[:, st_col + c8:st_col + c8 + 1], ALU.mult, ALU.add))
                    v.tensor_tensor_scan(h[:, UP0:UW][:, r], a[:, UP0:UW][:, r], ti[:, UP0:UW][:, r], 0.0,
                                         ALU.mult, ALU.add).then_inc(S("lru_scan"), 1)
                    v.wait_ge(S("lru_scan"), j + 1)
                    e = UW - 1 if d == 0 else UP0
                    step(v.tensor_copy(stl[:, c8:c8 + 1], h[:, e:e + 1]))
                    if d == 1:
                        step(v.tensor_tensor(hT[:, ct, 0:NS], hfb[0][:, 0:NS], hfb[1][:, 0:NS], ALU.add))
                        step(v.tensor_tensor(hT[:, ct, NS:T], hfb[0][:, UP0:UW], hfb[1][:, UP0:UW], ALU.add))
                    mod_dve(v, step, 4 + j)
            v.wait_ge(S("gelu"), 1)
            v.tensor_tensor(hT[:, 0:4, :], hT[:, 0:4, :], ga, ALU.mult).then_inc(S("y_first"), 1)

        dscr = ar(0, NT * 8, HD)
        def rope_dve(v, step, x, nh, scr):
            cos = rope[:, :, 0:32].unsqueeze(2).broadcast_to((P, ST, nh, 32))
            sin = rope[:, :, 32:64].unsqueeze(2).broadcast_to((P, ST, nh, 32))
            x1, x2 = x[:, :, :, 0:32], x[:, :, :, 32:64]
            n = ST * nh * 32
            a, b, c, d = (scr[:, i * n:(i + 1) * n].rearrange("p (t h d) -> p t h d", h=nh, d=32) for i in range(4))
            for t in range(ST):
                v.tensor_tensor(a[:, t], x1[:, t], cos[:, t], ALU.mult)
                v.tensor_tensor(b[:, t], x2[:, t], sin[:, t], ALU.mult)
                v.tensor_tensor(c[:, t], x2[:, t], cos[:, t], ALU.mult)
                step(v.tensor_tensor(d[:, t], x1[:, t], sin[:, t], ALU.mult))
                v.tensor_tensor(x1[:, t], a[:, t], b[:, t], ALU.subtract)
                step(v.tensor_tensor(x2[:, t], c[:, t], d[:, t], ALU.add))

        qr = qkv[:, :, 0:512]
        kr = qkv[:, :, 512:1024]
        vr = qkv[:, :, 1024:1536]
        kT = ar(0, 4, 768)
        qT = ar(3072, 4, T)
        pb = [ar(5632 + 1280 * i, 2, T) for i in range(2)]
        aT = [ar(8192 + 640 * i, T) for i in range(2)]
        osb = qkv[:, :, 0:512]
        ITS = [(t, h) for t in range(NT) for h in range(4)]
        MOD_AT = {2 * j + 1: 12 + j for j in range(N_DIFF_MODS)}
        hn_count = [0]

        def hn_act(act, src, n_el, scr, eps_scale, ss):
            hn_count[0] += 1
            k = hn_count[0]
            act.activation(scr, src, ACT.Square).then_inc(S("hn_sq"), 1)
            act.wait_ge(S("hn_sum"), k)
            act.activation(ss, ss, ACT.Sqrt, scale=eps_scale, bias=1e-6).then_inc(S("hn_root"), 1)

        def hn_dve(v, step, k, x, scr, ss, nh, w, gain, out=None, mul=None):
            v.wait_ge(S("hn_sq"), k)
            v.tensor_reduce(ss, scr, AX_X, ALU.add).then_inc(S("hn_sum"), 1)
            v.wait_ge(S("hn_root"), k)
            step(v.reciprocal(ss, ss))
            if mul is not None:
                step(v.tensor_scalar(ss, ss, mul, None, ALU.mult))
            s4 = ss.rearrange("p (t h) -> p t h", h=nh).unsqueeze(3).broadcast_to((P, NT, nh, w))
            for t in range(NT):
                step(v.tensor_tensor(x[:, t], x[:, t], s4[:, t], ALU.mult))
                if gain is not None:
                    o = x if out is None else out
                    step(v.tensor_tensor(o[:, t], x[:, t], gain.unsqueeze(1).broadcast_to((P, nh, w)), ALU.mult))

        def diff_act(act, step):
            act.wait_ge(S("y_first"), 1)
            q4 = qr.rearrange("p t (h d) -> p t h d", d=HD)
            for c in (2, 3, 4):
                for tp in range(3):
                    emptied(act, ("pR", 0, c, tp))
            sc = dscr.rearrange("p (t h) d -> p t h d", h=8)
            hn_act(act, q4, 0, sc, 1.0 / HD, ssq)
            act.wait_ge(S("dq_done"), 1)
            hn_act(act, kr.rearrange("p t (h d) -> p t h d", d=HD), 0, sc, 1.0 / HD, ssq)
            for h in range(4):
                for j, tag in enumerate(("kT", "qT")):
                    u = (tag, h)
                    dst = kT[:, h, :] if j == 0 else qT[:, h, :]
                    release(copy(act, dst, filled(act, u)[:, 0:(768 if j == 0 else T)]), u)

            def exps(i):
                n = T if ITS[i][0] < ST else P
                for c in range(2):
                    act.wait_ge(S("d_max"), 2 * i + c + 1)
                    if i >= 2:
                        filled(act, ("daT", i - 2))
                    u = ("ds", i, c)
                    release(act.activation(pb[i % 2][:, c, 0:n], filled(act, u)[:, 0:n], ACT.Exp,
                                           bias=nmax(i, c), accum_out=psum_of(i, c)), u)

            exps(0)
            for i in range(len(ITS)):
                if i + 1 < len(ITS):
                    exps(i + 1)
                n = T if ITS[i][0] < ST else P
                u = ("daT", i)
                if i >= 2:
                    filled(act, ("do", i - 2))
                release(copy(act, aT[i % 2][:, 0:n], filled(act, u)[:, 0:n]), u)
                if i in MOD_AT:
                    mod_act(act, MOD_AT[i])
            act.wait_ge(S("d_rows"), 1)
            hn_act(act, osb.rearrange("p t (h d) -> p t h d", d=P), 0,
                   dscr.rearrange("p a b -> p (a b)").rearrange("p (t h d) -> p t h d", h=4, d=P), 1.0 / P, ssq[:, 0:20])
            for h in range(4):
                u = ("dyT", h)
                release(copy(act, hT[:, 4 + h, :], filled(act, u)[:, 0:T]), u)

        def diff_dve(v, step):
            for c in (2, 3, 4):
                for tp in range(3):
                    emptied(v, ("pR", 0, c, tp))
            q4 = qr.rearrange("p t (h d) -> p t h d", d=HD)
            k4 = kr.rearrange("p t (h d) -> p t h d", d=HD)
            v.wait_ge(S("y_first"), 1)
            hn_dve(v, step, 1, q4, dscr, ssq, 8, HD, dqg)
            v.memset(smx[:, 36:37], 0.0).then_inc(S("dq_done"), 1)
            hn_dve(v, step, 2, k4, dscr, ssq, 8, HD, dkg)
            v.memset(smx[:, 36:37], 0.0).then_inc(S("cache_k_ready"), 1)
            rs = ar(0, 4096)
            rope_dve(v, step, q4[:, 0:ST], 8, rs)
            rope_dve(v, step, k4[:, 0:ST], 8, rs)
            v.memset(smx[:, 36:37], 0.0).then_inc(S("qk_rows"), 1)

            def maxes(i):
                n = T if ITS[i][0] < ST else P
                if i >= 4:
                    emptied(v, ("ds", i - 4, 1))
                for c in range(2):
                    v.tensor_reduce(nmax(i, c), filled(v, ("ds", i, c))[:, 0:n], AX_X, ALU.max, negate=True)\
                        .then_inc(S("d_max"), 1)

            def combine(i):
                n = T if ITS[i][0] < ST else P
                emptied(v, ("ds", i, 0))
                emptied(v, ("ds", i, 1))
                step(v.reciprocal(rsum(i, 0, 2), psum_of(i, 0, 2)))
                step(v.scalar_tensor_tensor(out=ratio(i), in0=rsum(i, 1), scalar=nlam, in1=psum_of(i),
                                            op0=ALU.mult, op1=ALU.mult))
                v.scalar_tensor_tensor(out=pb[i % 2][:, 0, 0:n], in0=pb[i % 2][:, 1, 0:n], scalar=ratio(i),
                                       in1=pb[i % 2][:, 0, 0:n], op0=ALU.mult, op1=ALU.add).then_inc(S("d_comb"), 1)

            def rows_out(i):
                t, h = ITS[i]
                release(v.tensor_scalar(osb[:, t, h * P:h * P + P], filled(v, ("do", i))[:, 0:P], rsum(i), None,
                                        ALU.mult), ("do", i))

            maxes(0)
            for i in range(len(ITS)):
                if i + 1 < len(ITS):
                    maxes(i + 1)
                combine(i)
                if i >= 1:
                    rows_out(i - 1)
                if i - 2 in MOD_AT:
                    mod_dve(v, step, MOD_AT[i - 2])
            rows_out(len(ITS) - 1)
            emptied(v, ("do", len(ITS) - 1))
            emptied(v, ("do", len(ITS) - 2))
            v.memset(smx[:, 36:37], 0.0).then_inc(S("d_rows"), 1)
            o4 = osb.rearrange("p t (h d) -> p t h d", d=P)
            hn_dve(v, step, 3, o4, dscr.rearrange("p a b -> p (a b)").rearrange("p (g d) -> p g d", d=P), ssq[:, 0:20], 4, P, dsg)
            v.memset(smx[:, 36:37], 0.0).then_inc(S("dy_rows"), 1)

        def diff_pe(pe):
            pe.wait_ge(S("qk_rows"), 1)
            pe.wait_ge(S("const_here"), CONST_ALL)
            for h in range(4):
                u = ("kT", h)
                ps = take(pe, u)
                c = slice(h * P, h * P + P)
                pe.transpose(ps[:, 0:P], dk_c[:, c], ident)
                for t in range(NT):
                    last = pe.transpose(ps[:, (t + 1) * P:(t + 2) * P], kr[:, t, c], ident)
                finish(last, u)
                u = ("qT", h)
                ps = take(pe, u)
                for t in range(NT):
                    last = pe.transpose(ps[:, t * P:t * P + P], qr[:, t, c], ident)
                finish(last, u)
            for h in range(4):
                emptied(pe, ("kT", h))
                emptied(pe, ("qT", h))

            def scores(i):
                t, h = ITS[i]
                for c in range(2):
                    u = ("ds", i, c)
                    ps = take(pe, u, c)
                    q = qT[64 * c:64 * c + 64, h, t * P:t * P + P]
                    k = kT[64 * c:64 * c + 64, h, :]
                    if t < ST:
                        pe.matmul(ps[:, 0:512], q, k[:, 0:512], start=True, stop=True)
                        last = pe.matmul(ps[:, 512:T], q, k[:, 512:T], start=True, stop=True)
                    else:
                        last = pe.matmul(ps[:, 0:P], q, k[:, T:768], start=True, stop=True)
                    finish(last, u)

            def rows(i):
                t, h = ITS[i]
                nk = NT if t < ST else 1
                u = ("do", i)
                ps = take(pe, u, 3)
                emptied(pe, ("daT", i))
                for j in range(nk):
                    vals = vr[:, ST, h * P:h * P + P] if t == ST else \
                        dv_c[:, h * P:h * P + P] if j == 0 else vr[:, j - 1, h * P:h * P + P]
                    last = pe.matmul(ps[:, 0:P], aT[i % 2][:, j * P:j * P + P], vals, start=(j == 0), stop=(j == nk - 1))
                finish(last, u)

            scores(0)
            for i, (t, h) in enumerate(ITS):
                if i + 1 < len(ITS):
                    scores(i + 1)
                if i >= 1:
                    rows(i - 1)
                if i - 1 in MOD_AT:
                    mod_rows_pe(pe, MOD_AT[i - 1], 2)
                if i - 2 in MOD_AT:
                    mod_turn_pe(pe, MOD_AT[i - 2], 3)
                pe.wait_ge(S("d_comb"), i + 1)
                u = ("daT", i)
                ps = take(pe, u, 2)
                for j in range(NT if t < ST else 1):
                    last = pe.transpose(ps[:, j * P:j * P + P], pb[i % 2][:, 0, j * P:j * P + P], ident)
                finish(last, u)
            rows(len(ITS) - 1)
            pe.wait_ge(S("dy_rows"), 1)
            for h in range(4):
                u = ("dyT", h)
                ps = take(pe, u)
                for t in range(NT):
                    last = pe.transpose(ps[:, t * P:t * P + P], osb[:, t, h * P:h * P + P], ident)
                finish(last, u)

        def layer0_outputs(g):
            g.wait_ge(S("cache_k_ready"), 1)
            g.dma_start(outs["new_cache_diff_k"].rearrange("a b t h c d -> t (a b h c d)"), kr[:, ST, :])\
                .then_inc(S("caches"), 16)
            for tp in range(3):
                emptied(g, ("pR", 0, 4, tp))
            g.dma_start(outs["new_cache_diff_v"].rearrange("a b t h d -> t (a b h d)"), vr[:, ST, :])\
                .then_inc(S("caches"), 16)
            g.wait_ge(S("y_first"), 1)
            with nc.allow_non_contiguous_dma(reason="a small state"):
                g.dma_start(outs["new_state_lru"][0, 0].rearrange("r (c p) -> p (r c)", p=P), stl)\
                    .then_inc(S("caches"), 16)

        def out_pe(pe, l):
            if l == 0:
                pe.wait_ge(S("y_first"), 1)
                for h in range(4):
                    emptied(pe, ("dyT", h))
            else:
                layer1_ready(pe)
            for c in range(2):
                w = arrived(pe, ("out", l, c, 0))
                for f in range(4):
                    u = ("out", l, 4 * c + f)
                    ps = take(pe, u)
                    lhs = lambda k: w[:, k, f * P:f * P + P]
                    mmk(pe, ps[:, 0:NS], lhs, lambda k: hT[:, k, 0:NS])
                    finish(mmk(pe, ps[:, NS:T], lhs, lambda k: hT[:, k, NS:T]), u)
                chunk_last["out", l, c, 0] = u

        def add_gated(v, l, m, k, ps, u):
            a, b = seg[0]
            v.scalar_tensor_tensor(out=xT[:, k, a:b], in0=ps[:, a:b], scalar=modt[:, l, 8 * m + k, 0:1],
                                   in1=xT[:, k, a:b], op0=ALU.mult, op1=ALU.add).then_inc(S("x_half"), 1)
            a, b = seg[1]
            release(v.scalar_tensor_tensor(out=xT[:, k, a:b], in0=ps[:, a:b], scalar=modt[:, l, 8 * m + k, 1:2],
                                           in1=xT[:, k, a:b], op0=ALU.mult, op1=ALU.add), u)

        def residual_dve(v, step, l, kind):
            nl, nn = (l, 1) if kind == "out" else (l + 1, 0)
            for k in range(KD):
                u = (kind, l, k)
                add_gated(v, l, 2 if kind == "out" else 5, k, filled(v, u), u)
                if k >= 2 and nl < 2:
                    norm_add_dve(v, nl, nn, k - 1)
            if nl < 2:
                norm_add_dve(v, nl, nn, KD - 1)
            v.wait_ge(S("x_half"), 8 * (2 * l + (1 if kind == "out" else 2)))

        lg = ar(18700, NT, NE)
        affT = ar(18800, T)[0:NE, :]
        g16 = ar(19500, CAP)[0:NE, :]
        i16 = ar(19600, CAP)[0:NE, :].bitcast(U32)
        i16f = ar(19700, CAP)[0:NE, :]
        gateT = ar(19800, NE)[0:CAP, :]
        idxT = ar(19820, NE)[0:CAP, :].bitcast(U32)
        hrow = ar(12800, NT, D)
        rows_m = ar(12800, NT, D)

        def flip_h_pe(pe, l):
            flip_out_pe(pe, ("hr", l), hT)

        def route_pe(pe, l):
            pe.wait_ge(S("h_ready"), 16 * (2 * l + 2))
            u = ("logit", l)
            ps = take(pe, u)
            for t in range(NT):
                last = mmk(pe, ps[:, 16 * t:16 * t + 16], lambda k: hT[:, k, t * P:t * P + P], lambda k: wr[:, l, k, :])
            finish(last, u)
            for t in range(NT):
                u = ("hr", l, t)
                ps = take(pe, u)
                for k in range(KD):
                    last = pe.transpose(ps[:, k * P:k * P + P], hT[:, k, t * P:t * P + P], ident)
                finish(last, u)
            late = range(12 + N_DIFF_MODS, 24) if l == 0 else []
            for i in late[:1]:
                mod_rows_pe(pe, i)
            pe.wait_ge(S("aff"), l + 1)
            u = ("affT", l)
            ps = take(pe, u)
            for t in range(NT):
                last = pe.transpose(ps[0:NE, t * P:t * P + P], lg[:, t, :], ident)
            finish(last, u)
            for i in late[1:]:
                mod_rows_pe(pe, i)
                mod_turn_pe(pe, i - 1)
            if l == 0:
                mod_turn_pe(pe, 23)
            pe.wait_ge(S("top"), l + 1)
            u = ("gi", l)
            ps = take(pe, u)
            pe.transpose(ps[0:CAP, 0:16], g16, ident[0:NE, 0:NE])
            finish(pe.transpose(ps[0:CAP, 16:32], i16f, ident[0:NE, 0:NE]), u)

        def route_act(act, step, l):
            for t in range(NT):
                u = ("hr", l, t)
                release(copy(act, hrow[:, t, :], filled(act, u)), u)
            act.wait_ge(S("lg_sub"), l + 1)
            act.activation(lg, lg, ACT.Exp).then_inc(S("lg_exp"), 1)
            if l == 0:
                for i in range(12 + N_DIFF_MODS, 24):
                    mod_act(act, i)

        def route_dve(v, step, l):
            u = ("logit", l)
            ps = filled(v, u)[:, 0:80].rearrange("p (t e) -> p t e", e=NE)
            step(v.tensor_reduce(smx[:, 0:5], ps, AX_X, ALU.max))
            release(v.tensor_tensor(lg, ps, smx[:, 0:5].unsqueeze(2).broadcast_to((P, NT, NE)), ALU.subtract), u)
            emptied(v, u)
            v.memset(sm[:, 251:252], 0.0).then_inc(S("lg_sub"), 1)
            v.wait_ge(S("lg_exp"), l + 1)
            step(v.tensor_reduce(smx[:, 5:10], lg, AX_X, ALU.add))
            step(v.reciprocal(smx[:, 5:10], smx[:, 5:10]))
            v.tensor_tensor(lg, lg, smx[:, 5:10].unsqueeze(2).broadcast_to((P, NT, NE)), ALU.mult)\
                .then_inc(S("aff"), 1)
            u = ("affT", l)
            release(v.tensor_copy(affT, filled(v, u)[0:NE, 0:T]), u)
            emptied(v, u)
            late = range(12 + N_DIFF_MODS, 24) if l == 0 else []
            for (a, b), c0, rounds in ((seg[0], 0, CAPS // 8), (seg[1], CAPS, CAPP // 8)):
                for r in range(rounds):
                    c = slice(c0 + 8 * r, c0 + 8 * r + 8)
                    step(v.max(g16[:, c], affT[:, a:b]))
                    step(v.max_index(i16[:, c], g16[:, c], affT[:, a:b]))
                    step(v.match_replace(affT[:, a:b], g16[:, c], affT[:, a:b], -1.0))
                    if l == 0 and c0 == 0 and r in (2, 5):
                        mod_dve(v, step, late[r // 3])
            step(v.tensor_copy(i16f, i16))
            v.tensor_scalar(i16f[:, CAPS:CAP], i16f[:, CAPS:CAP], float(NS), None, ALU.add).then_inc(S("top"), 1)
            for i in late[2:]:
                mod_dve(v, step, i)
            u = ("gi", l)
            ps = filled(v, u)
            step(v.tensor_copy(gateT, ps[0:CAP, 0:16]))
            release(v.tensor_copy(idxT, ps[0:CAP, 16:32]), u)

        def route_pool(g, l):
            for t in range(NT):
                emptied(g, ("hr", l, t))
            g.dma_start(DR["h", l].rearrange("(t p) d -> p t d", p=P), hrow).then_inc(S("h_stored"), 16)

        xe = [hflat[0:CAP, 1024 * i:1024 * i + 1024] for i in range(2)]
        ye = [hflat[0:CAP, 2048 + 1024 * i:3072 + 1024 * i] for i in range(2)]
        xeT = [ar(20000 + 640 * i, 2, 4 * CAP) for i in range(2)]
        hid = [ar(21280 + 320 * i, FT, CAP) for i in range(2)]
        slu = [hflat[:, 4096 + 80 * i:4176 + 80 * i] for i in range(2)]
        PER = (1, 2, 2, 1)

        def moe_pe(pe, l):
            while units.next % 4:
                u = ("skip", l, units.next)
                take(pe, u)
                units.uses[units.of[u][0]] -= 1
            base = list(units.uses)
            moe_base[l] = base

            def take_at(pair, i, n):
                pe.wait_ge(pair_free[pair], i * PER[pair] + (base[pair] + n))

            def gather_T(i, par):
                pe.wait_ge(S(f"gathered{par}"), (i - par) * 8 + (16 + 128 * l))
                take_at(0, i, 0)
                ps = PSUM[:, 0, :]
                for k in range(KD):
                    o = 512 * (k // 4) + CAP * (k % 4)
                    last = pe.transpose(ps[:, o:o + CAP], xe[par][:, k * P:k * P + P], ident[0:CAP, 0:CAP])
                last.then_inc(pair_full[0], 1)

            def expert(i, par, nxt):
                s = 3 - 3 * par
                w1, w3 = (slots[s + j].rearrange("p (k n) -> p k n", n=FF) for j in range(2))
                w2 = slots[s + 2].rearrange("p (k n) -> p k n", n=D)
                pe.wait_ge(pair_free[0], i + (base[0] + 1))
                for j in range(2):
                    pe.wait_ge(w_here[s + j], (i - par) * 8 + 16 * (slot_of["exp", l, s + j] + 1))
                for f in range(FT):
                    pair = 1 + f % 2
                    take_at(pair, i, f // 2)
                    ps = PSUM[:, pair, :]
                    for w, o in ((w1, 0), (w3, 512)):
                        last = mmk(pe, ps[:, o:o + CAP], lambda k: w[:, k, f * P:f * P + P],
                                   lambda k: xeT[par][:, k // 4, CAP * (k % 4):CAP * (k % 4) + CAP])
                    last.then_inc(pair_full[pair], 1)
                if nxt is not None:
                    gather_T(nxt, 1 - par)
                pe.wait_ge(w_here[s + 2], (i - par) * 8 + 16 * (slot_of["exp", l, s + 2] + 1))
                take_at(3, i, 0)
                for f0, f1 in ((0, FT - 1), (FT - 1, FT)):
                    if f0 == 0:
                        pe.wait_ge(pair_free[1], i * 2 + (base[1] + 2))
                        pe.wait_ge(pair_free[2], i * 2 + (base[2] + 1))
                    else:
                        pe.wait_ge(pair_free[2], i * 2 + (base[2] + 2))
                    for half in range(2):
                        for f in range(f0, f1):
                            last = pe.matmul(PSUM[0:CAP, 3, 512 * half:512 * half + 512], hid[par][:, f, :],
                                             w2[:, f, 512 * half:512 * half + 512], start=(f == 0), stop=(f == FT - 1))
                last.then_inc(pair_full[3], 1)

            gather_T(0, 0)
            with pe.Fori(0, NE // 2 - 1) as i:
                expert(i * 2, 0, i * 2 + 1)
                expert(i * 2 + 1, 1, i * 2 + 2)
            expert(NE - 2, 0, NE - 1)
            expert(NE - 1, 1, None)
            for pair in range(4):
                units.uses[pair] = base[pair] + NE * PER[pair]

        def moe_act_run(act, l):
            base = moe_base[l]

            def xt(i, par):
                act.wait_ge(pair_full[0], i + (base[0] + 1))
                ps = PSUM[:, 0, :].rearrange("p (a b) -> p a b", a=2)[:, :, 0:4 * CAP]
                act.activation(xeT[par], ps, ACT.Copy).then_inc(pair_free[0], 1)

            def expert(i, par, nxt):
                for f in range(FT):
                    pair = 1 + f % 2
                    act.wait_ge(pair_full[pair], i * 2 + (base[pair] + f // 2 + 1))
                    act.wait_ge(pair_free[pair], i * 2 + (base[pair] + f // 2))
                    act.activation(slu[f % 2], PSUM[:, pair, 0:CAP], ACT.Silu).then_inc(S("silu"), 1)
                if nxt is not None:
                    xt(nxt, 1 - par)
                act.wait_ge(pair_full[3], i + (base[3] + 1))
                act.wait_ge(S(f"y_room{par}"), (i - par) * 8 + (16 + 128 * l))
                act.activation(ye[par][:, 0:512], PSUM[0:CAP, 3, 0:512], ACT.Copy, scale=gateT[:, bass.ds(i, 1)])\
                    .then_inc(S("y_low"), 1)

            emptied(act, ("gi", l))
            xt(0, 0)
            with act.Fori(0, NE // 2 - 1) as i:
                expert(i * 2, 0, i * 2 + 1)
                expert(i * 2 + 1, 1, i * 2 + 2)
            expert(NE - 2, 0, NE - 1)
            expert(NE - 1, 1, None)

        def moe_dve(v, l):
            base = moe_base[l]

            def expert(i, par):
                for f in range(FT):
                    pair = 1 + f % 2
                    v.wait_ge(S("silu"), i * 4 + (64 * l + f + 1))
                    v.tensor_tensor(hid[par][:, f, :], slu[f % 2], PSUM[:, pair, 512:512 + CAP], ALU.mult)\
                        .then_inc(pair_free[pair], 1)
                v.wait_ge(pair_full[3], i + (base[3] + 1))
                v.wait_ge(S("y_low"), i + (16 * l + 1))
                v.tensor_scalar(ye[par][:, 512:1024], PSUM[0:CAP, 3, 512:1024], gateT[:, bass.ds(i, 1)], None,
                                ALU.mult).then_inc(pair_free[3], 1)

            emptied(v, ("gi", l))
            with v.Fori(0, NE // 2) as i:
                expert(i * 2, 0)
                expert(i * 2 + 1, 1)

        def moe_pool(g, l):
            base = moe_base[l]
            emptied(g, ("gi", l))
            g.wait_ge(S("h_stored"), 16 * (l + 1))
            off = lambda e: bass.IndirectOffsetOnAxis(ap=idxT[:, e:e + 1], axis=0)

            def gather(e):
                if e >= 2:
                    g.wait_ge(pair_full[0], base[0] + e - 1)
                g.indirect_dma_start(xe[e % 2], None, DR["h", l], off(e)).then_inc(S(f"gathered{e % 2}"), 16)

            gather(0)
            for e in range(NE):
                if e + 1 < NE:
                    gather(e + 1)
                g.wait_ge(pair_free[3], base[3] + e + 1)
                if e:
                    g.wait_ge(S(f"y_room{(e - 1) % 2}"), 16 * ((e - 1) // 2 + 1) + 16 + 128 * l)
                g.indirect_dma_start(DR["m", l], off(e), ye[e % 2], None, compute_op=ALU.add)\
                    .then_inc(S(f"y_room{e % 2}"), 16)

        def load_stream(sp):
            for c, s, prev in loads:
                if c[0] != "experts":
                    if prev is not None:
                        if prev[0] == "experts":
                            l = prev[1]
                            pair, n = (2, 2 * NE) if s < 2 else (3, NE)
                            sp.wait_ge(pair_full[pair], moe_base[l][pair] + n)
                        else:
                            filled(sp, chunk_last[prev])
                    src, n = chunk_src(c)
                    sp.dma_start(chunk(c), src.rearrange("(k p) n -> p k n", p=P)).then_inc(w_here[s], 16)
                    if c == wouts[c[1]][1]:
                        filled(sp, ("dyT", 3) if c[1] == 0 else ("cyT", 3))
                        sp.wait_ge(S("caches"), (48, 96)[c[1]])
                        for j in range(3):
                            load_expert(sp, c[1], 0, 0, j, False)
                else:
                    experts_stream(sp, c[1], prev)

        def load_expert(sp, l, i, par, j, wait):
            base = moe_base[l]
            if True:
                s = 3 - 3 * par + j
                if wait:
                    pair = 3 if j == 2 else 2
                    sp.wait_ge(pair_full[pair], i * PER[pair] + (base[pair] - PER[pair]))
                w = (W1, W3, W2)[j][l]
                kk = FT if j == 2 else KD
                n = D if j == 2 else FF
                src = w[:, bass.ds(i * kk, kk), :]
                sp.dma_start(slots[s].rearrange("p (k n) -> p k n", n=n), src).then_inc(w_here[s], 16)

        def experts_stream(sp, l, prev):
            load = lambda *a: load_expert(sp, l, *a)

            for j in range(3):
                filled(sp, chunk_last[prev[j]])
                load(1, 1, j, False)
            with sp.Fori(1, NE // 2) as i:
                for par in range(2):
                    for j in range(3):
                        load(i * 2 + par, par, j, True)

        def gather_sum_act(act, l):
            for par in range(2):
                act.wait_ge(S(f"y_room{par}"), 16 + 128 + 128 * l)
            for pair in range(4):
                act.wait_ge(pair_free[pair], moe_base[l][pair] + NE * PER[pair])
            act.dma_start(rows_m, DR["m", l].rearrange("(t p) d -> p t d", p=P)).then_inc(S("m_rows"), 16)

        def sum_pe(pe, l):
            pe.wait_ge(S("m_rows"), 16 * (l + 1))
            for k in range(KD):
                u = ("ms", l, k)
                ps = take(pe, u)
                for t in range(NT):
                    last = pe.transpose(ps[:, t * P:t * P + P], rows_m[:, t, k * P:k * P + P], ident)
                finish(last, u)

        def store_pe(pe):
            for k in range(KD):
                emptied(pe, ("ms", 1, k))
            pe.wait_ge(S("x_half"), 32)
            for t in range(NT):
                u = ("xr", t)
                ps = take(pe, u)
                for k in range(KD):
                    last = pe.transpose(ps[:, k * P:k * P + P], xT[:, k, t * P:t * P + P], ident)
                finish(last, u)

        def store_read(eng, part):
            for t in range(part, NT, 2):
                u = ("xr", t)
                release(copy(eng, rows[:, t, :], filled(eng, u)), u)

        def store_sp(sp, n_out):
            for t in range(NT):
                emptied(sp, ("xr", t))
                dst = outs["y_sample"][0, t * P:t * P + P, :] if t < ST else outs["y_prompt"][0]
                sp.dma_start(dst, rows[:, t, :]).then_inc(S("outputs"), 16)
            sp.wait_ge(S("outputs"), 16 * NT)
            sp.wait_ge(S("caches"), 16 * n_out)

        pad = ar(0, 12, PADW)
        gate = ar(7752, NT, 512)
        z2 = ar(10312, NT, 784)
        zq = z2[:, :, 16:528].rearrange("p t (h d) -> p t h d", d=HD)
        zk = z2[:, :, 528:656].rearrange("p t (h d) -> p t h d", d=HD)
        zo = z2[:, :, 16:528]
        gqT = ar(14232, 4, T)
        gkT = ar(16792, 2, 768)
        gp = [ar(18328 + 640 * i, T) for i in range(2)]
        gaT = [ar(19608 + 640 * i, T) for i in range(2)]
        gscr = ar(18328, NT * 8, HD)
        kdup = ar(20888, NT, 256)
        cdup = ar(22168, 256)
        GI = [(t, h) for t in range(NT) for h in range(8)]
        beta = sm[:, 256:296]
        gdec = sm[:, 296:336]
        gsm = sm[:, 336:496]
        eG = sm[:, 496:536]
        eGL = sm[:, 536:576]
        bG = sm[:, 576:616]
        dx, de, dz, dz2, do_ = (ar(22700 + 40 * i, 40) for i in range(5))
        t8 = lambda x: x.rearrange("p (t q) -> p t q", q=8)

        def gqa_act(act, step):
            for c in (4, 5):
                for tp in range(3):
                    emptied(act, ("pR", 1, c, tp))
            act.activation(t8(beta), z2[:, :, 0:8], ACT.Tanh, scale=0.5).then_inc(S("dl_tanh"), 1)
            act.activation(anl, alog, ACT.Exp).then_inc(S("dl_tanh"), 1)
            act.wait_ge(S("dl_x"), 1)
            softplus_act(act, step, dx, de).then_inc(S("sp_exp"), 1)
            hn_act(act, zq, 0, gscr.rearrange("p (t h) d -> p t h d", h=8), 1.0 / HD, ssq)
            act.wait_ge(S("gq_done"), 1)
            hn_act(act, zk, 0, gscr[:, 0:10, :].rearrange("p (t h) d -> p t h d", h=2), 1.0 / HD, ssq[:, 0:10])
            for g in range(4):
                release(copy(act, gqT[:, g, :], filled(act, ("gqT", g))[:, 0:T]), ("gqT", g))
            for n in range(2):
                release(copy(act, gkT[:, n, :], filled(act, ("gkT", n))[:, 0:768]), ("gkT", n))

            for i in range(len(GI)):
                n = T if GI[i][0] < ST else P
                act.wait_ge(S("g_max"), i + 1)
                if i >= 2:
                    filled(act, ("gaT", i - 2))
                if i >= 4:
                    emptied(act, ("go", i - 4))
                u = ("gs", i)
                release(act.activation(gp[i % 2][:, 0:n], filled(act, u)[:, 0:n], ACT.Exp, bias=nmax(i),
                                       accum_out=psum_of(i)), u)
            for b in range(4):
                release(copy(act, hT[:, 4 + b, :], filled(act, ("gyT", b))[:, 0:T]), ("gyT", b))

        def gqa_dve(v, step):
            for c in (4, 5):
                for tp in range(3):
                    emptied(v, ("pR", 1, c, tp))
            v.tensor_tensor(t8(dx), z2[:, :, 8:16], dtb.unsqueeze(1).broadcast_to((P, NT, 8)), ALU.add)\
                .then_inc(S("dl_x"), 1)
            v.wait_ge(S("dl_x"), 1)
            v.wait_ge(S("dl_tanh"), 2)
            step(v.tensor_scalar(beta, beta, 0.5, 0.5, ALU.mult, ALU.add))
            v.wait_ge(S("sp_exp"), 2)
            softplus_dve(v, step, dx, de, dz, dz2, do_)
            step(v.scalar_tensor_tensor(out=t8(gdec), in0=t8(do_), scalar=-1.0,
                                        in1=anl.unsqueeze(1).broadcast_to((P, NT, 8)), op0=ALU.mult, op1=ALU.mult))
            hn_dve(v, step, 4, zq, gscr, ssq, 8, HD, gqg)
            v.memset(smx[:, 36:37], 0.0).then_inc(S("gq_done"), 1)
            hn_dve(v, step, 5, zk, gscr[:, 0:10, :], ssq[:, 0:10], 2, HD, gkg)
            v.memset(smx[:, 36:37], 0.0).then_inc(S("cache_k_ready"), 1)
            rs = ar(18328, 4096)
            rope_dve(v, step, zq[:, 0:ST], 8, rs)
            rope_dve(v, step, zk[:, 0:ST], 2, rs)
            for r in range(2):
                step(v.tensor_copy(kdup.rearrange("p t (n r d) -> p t n r d", n=2, r=2)[:, :, :, r, :], zk))
                step(v.tensor_copy(cdup.rearrange("p (n r d) -> p n r d", n=2, r=2)[:, :, r, :],
                                   gk_c[:, :].rearrange("p (n d) -> p n d", n=2)))
            v.memset(smx[:, 36:37], 0.0).then_inc(S("qk_rows"), 1)

            def maxes(i):
                n = T if GI[i][0] < ST else P
                if i >= 4:
                    emptied(v, ("gs", i - 4))
                v.tensor_reduce(nmax(i), filled(v, ("gs", i))[:, 0:n], AX_X, ALU.max, negate=True)\
                    .then_inc(S("g_max"), 1)

            def turned(i):
                n = T if GI[i][0] < ST else P
                if i >= 2:
                    filled(v, ("go", i - 2))
                release(v.tensor_copy(gaT[i % 2][:, 0:n], filled(v, ("gaT", i))[:, 0:n]), ("gaT", i))

            def rows_out(i):
                t, h = GI[i]
                emptied(v, ("gs", i))
                step(v.reciprocal(rsum(i), psum_of(i)))
                release(v.tensor_scalar(zo[:, t, h * HD:h * HD + HD], filled(v, ("go", i))[:, 0:HD], rsum(i), None,
                                        ALU.mult), ("go", i))

            for i in range(-2, len(GI)):
                if i + 2 < len(GI):
                    maxes(i + 2)
                if 0 <= i + 1 < len(GI):
                    turned(i + 1)
                if i >= 0:
                    rows_out(i)

        def gqa_pe(pe):
            pe.wait_ge(S("qk_rows"), 2)
            for g in range(4):
                u = ("gqT", g)
                ps = take(pe, u)
                for t in range(NT):
                    last = pe.transpose(ps[:, t * P:t * P + P], zo[:, t, g * P:g * P + P], ident)
                finish(last, u)
            for n in range(2):
                u = ("gkT", n)
                ps = take(pe, u)
                pe.transpose(ps[:, 0:P], cdup[:, n * P:n * P + P], ident)
                for t in range(NT):
                    last = pe.transpose(ps[:, (t + 1) * P:(t + 2) * P], kdup[:, t, n * P:n * P + P], ident)
                finish(last, u)
            for g in range(4):
                emptied(pe, ("gqT", g))
            emptied(pe, ("gkT", 0))
            emptied(pe, ("gkT", 1))

            def scores(i):
                t, h = GI[i]
                r = slice(64 * (h % 2), 64 * (h % 2) + 64)
                u = ("gs", i)
                ps = take(pe, u, i % 2)
                q = gqT[r, h // 2, t * P:t * P + P]
                k = gkT[r, h // 4, :]
                if t < ST:
                    pe.matmul(ps[:, 0:512], q, k[:, 0:512], start=True, stop=True)
                    last = pe.matmul(ps[:, 512:T], q, k[:, 512:T], start=True, stop=True)
                else:
                    last = pe.matmul(ps[:, 0:P], q, k[:, T:768], start=True, stop=True)
                finish(last, u)

            def turn(i):
                emptied(pe, ("gs", i))
                u = ("gaT", i)
                ps = take(pe, u, 2)
                for j in range(NT if GI[i][0] < ST else 1):
                    last = pe.transpose(ps[:, j * P:j * P + P], gp[i % 2][:, j * P:j * P + P], ident)
                finish(last, u)

            def rows(i):
                t, h = GI[i]
                nk = NT if t < ST else 1
                u = ("go", i)
                ps = take(pe, u, 3)
                emptied(pe, ("gaT", i))
                o = 64 * (h // 4)
                for j in range(nk):
                    vals = z2[:, ST, 656 + o:720 + o] if t == ST else \
                        gv_c[:, o:o + HD] if j == 0 else z2[:, j - 1, 656 + o:720 + o]
                    last = pe.matmul(ps[:, 0:HD], gaT[i % 2][:, j * P:j * P + P], vals, start=(j == 0),
                                     stop=(j == nk - 1))
                finish(last, u)

            for i in range(-2, len(GI)):
                if i + 2 < len(GI):
                    scores(i + 2)
                if 0 <= i + 1 < len(GI):
                    turn(i + 1)
                if i >= 0:
                    rows(i)
            for i in range(len(GI) - 3, len(GI)):
                emptied(pe, ("go", i))
            for b in range(4):
                u = ("gyT", b)
                ps = take(pe, u)
                for t in range(NT):
                    last = pe.transpose(ps[:, t * P:t * P + P], zo[:, t, b * P:b * P + P], ident)
                finish(last, u)

        cv = [ar(15432 + UW * i, UW) for i in range(3)]
        dq, dk, dv = ar(10312, NT, 512), ar(12872, NT, 512), ar(0, NT, 512)
        dqkv = (dq, dk, dv)
        oacc = ar(15432, NT, 512)
        dscr2 = ar(18040, NT * 4, P)
        dbase = (18040, 2560)
        slot = lambda d, i, n=1: ar(dbase[d] + 512 * i, 4 * n, P)
        KT_U, QT_W, DA_KB, DB_QK, A_VB, AM_KT, X_, XT_, WT_VN, QD_ = range(10)
        sdec = [hflat[:, 512 * d:512 * d + 512].rearrange("p (h v) -> p h v", h=4) for d in range(2)]
        tile_of = lambda n, d: 4 if n == 4 else n if d == 0 else 3 - n
        chunk_at = lambda ci, d: ci if d == 0 else 1 - ci
        DIRS = "fb"

        def over_heads(x):
            return x.unsqueeze(1).broadcast_to((P, 4, P))

        def per_head(x, t, d):
            return x[:, 8 * t + 4 * d:8 * t + 4 * d + 4].unsqueeze(2).broadcast_to((P, 4, P))

        def conv_pe(pe):
            for ct in range(12):
                pe.wait_ge(S("cv_silu"), ct + 1)
                u = ("cvT", ct)
                ps = take(pe, u)
                c = cv[ct % 3]
                for t in range(NT):
                    o = t * P if t < ST else UP0
                    last = pe.transpose(ps[:, t * P:t * P + P], c[:, o:o + P], ident)
                finish(last, u)

        def conv_read(eng, ct):
            u = ("cvT", ct)
            dst = dqkv[ct // 4][:, :, (ct % 4) * P:(ct % 4) * P + P]
            release(copy(eng, dst, filled(eng, u)[:, 0:T].rearrange("p (t c) -> p t c", c=P)), u)

        def heads4(x):
            return x.rearrange("p t (h d) -> p t h d", d=P)

        def delta_pe(pe):
            pe.wait_ge(S("dl_g"), 1)
            ps = take(pe, "G")
            gv = gdec.rearrange("p (t d h) -> p t d h", d=2, h=4)
            pv = ps[:, 0:40].rearrange("p (t d h) -> p t d h", d=2, h=4)
            for d in range(2):
                pe.matmul(pv[:, :, d, :], C[("up_one", "lo_one")[d]], gv[:, :, d, :], start=True, stop=True)
            pe.matmul(ps[:, 40:80], C["block"], gdec, start=True, stop=True)
            for c in range(2):
                last = pe.matmul(ps[:, 80 + 512 * c:120 + 512 * c], ones[64 * c:64 * c + 64, :], gdec[64 * c:64 * c + 64, :],
                                 start=True, stop=True)
            finish(last, "G")
            conv_pe(pe)
            pe.wait_ge(S("dn_rows"), 1)
            for n in range(5):
                for d in range(2):
                    t = tile_of(n, d)
                    u = ("kq", n, d)
                    ps = take(pe, u)
                    for h in range(4):
                        pe.transpose(ps[:, h * P:h * P + P], dk[:, t, h * P:h * P + P], ident)
                        last = pe.transpose(ps[:, 512 + h * P:640 + h * P], dq[:, t, h * P:h * P + P], ident)
                    finish(last, u)
                for d in range(2):
                    pe.wait_ge(S("dl_diag"), 2 * n + d + 1)
                    u = ("dec", n, d)
                    ps = take(pe, u)
                    pe.matmul(ps[:, 0:512], ones, slot(d, XT_), start=True, stop=False)
                    for h in range(4):
                        last = pe.matmul(ps[:, h * P:h * P + P], slot(d, X_)[:, h, :], ones, start=False, stop=(h == 3))
                    finish(last, u)
                for d in range(2):
                    u = ("kk", n, d)
                    emptied(pe, ("kq", n, d))
                    ps = take(pe, u)
                    for h in range(4):
                        k = slot(d, KT_U)[:, h, :]
                        pe.matmul(ps[:, h * P:h * P + P], k, k, start=True, stop=True)
                        last = pe.matmul(ps[:, 512 + h * P:640 + h * P], k, slot(d, QT_W)[:, h, :], start=True, stop=True)
                    finish(last, u)
                for d in range(2):
                    pe.wait_ge(S("dl_qd"), 2 * n + d + 1)
                    u = ("qd", n, d)
                    ps = take(pe, u)
                    for h in range(4):
                        last = pe.transpose(ps[:, h * P:h * P + P], slot(d, WT_VN)[:, h, :], ident)
                    finish(last, u)
                for d in range(2):
                    pe.wait_ge(S(f"dl_am{d}"), 6 * n + 1)
                    u = ("am", n, d)
                    ps = take(pe, u)
                    for h in range(4):
                        last = pe.transpose(ps[:, h * P:h * P + P], slot(d, AM_KT)[:, h, :], ident)
                    finish(last, u)
                for s in range(1, 6):
                    for d in range(2):
                        pe.wait_ge(S(f"dl_am{d}"), 6 * n + s + 1)
                        if s == 1:
                            pe.wait_ge(S(f"dl_x0{d}"), n + 1)
                        else:
                            emptied(pe, ("x", n, d, s - 1))
                        u = ("w", n, d, s)
                        ps = take(pe, u)
                        for h in range(4):
                            last = pe.matmul(ps[:, h * P:h * P + P], slot(d, AM_KT)[:, h, :], slot(d, XT_)[:, h, :],
                                             start=True, stop=True)
                        finish(last, u)
                    for d in range(2):
                        emptied(pe, ("w", n, d, s))
                        u = ("x", n, d, s)
                        ps = take(pe, u)
                        for h in range(4):
                            if s < 5:
                                pe.matmul(ps[:, h * P:h * P + P], slot(d, WT_VN)[:, h, :], slot(d, X_)[:, h, :],
                                          start=True, stop=True)
                            last = pe.matmul(ps[:, 512 + h * P:640 + h * P], slot(d, X_)[:, h, :],
                                             slot(d, WT_VN)[:, h, :], start=True, stop=True)
                        finish(last, u)
                for d in range(2):
                    emptied(pe, ("x", n, d, 5))
                    pe.wait_ge(S(f"dl_kv{d}"), n + 1)
                    u = ("wu", n, d)
                    ps = take(pe, u)
                    for h in range(4):
                        xt = slot(d, XT_)[:, h, :]
                        pe.matmul(ps[:, h * P:h * P + P], xt, slot(d, A_VB)[:, h, :], start=True, stop=True)
                        last = pe.matmul(ps[:, 512 + h * P:640 + h * P], slot(d, DA_KB)[:, h, :], xt,
                                         start=True, stop=True)
                    finish(last, u)
                for ci in range(2):
                    for d in range(2):
                        c = chunk_at(ci, d)
                        r = slice(64 * c, 64 * c + 64)
                        if ci == 0:
                            emptied(pe, ("wu", n, d))
                            if n == 4:
                                pe.wait_ge(S("dl_zero"), 2)
                            elif n:
                                emptied(pe, ("os", n - 1, d, 1))
                        else:
                            emptied(pe, ("os", n, d, 0))
                        u = ("vs", n, d, ci)
                        ps = take(pe, u)
                        for h in range(4):
                            last = pe.matmul(ps[r, h * P:h * P + P], slot(d, QT_W)[:, h, r], sdel[:, 4 * d + h, :],
                                             start=True, stop=True)
                        finish(last, u)
                    for d in range(2):
                        c = chunk_at(ci, d)
                        r = slice(64 * c, 64 * c + 64)
                        emptied(pe, ("vs", n, d, ci))
                        u = ("os", n, d, ci)
                        ps = take(pe, u)
                        for h in range(4):
                            pe.matmul(ps[r, h * P:h * P + P], slot(d, QD_)[:, h, r], sdel[:, 4 * d + h, :],
                                      start=True, stop=False)
                            pe.matmul(ps[r, h * P:h * P + P], slot(d, DB_QK)[r, h, r], slot(d, WT_VN)[r, h, :],
                                      start=False, stop=True)
                        for h in range(4):
                            last = pe.matmul(ps[:, 512 + h * P:640 + h * P], slot(d, AM_KT)[r, h, :],
                                             slot(d, WT_VN)[r, h, :], start=True, stop=True)
                        finish(last, u)
            pe.wait_ge(S("dy_rows"), 2)
            for b in range(4):
                u = ("cyT", b)
                ps = take(pe, u)
                for t in range(NT):
                    last = pe.transpose(ps[:, t * P:t * P + P], oacc[:, t, b * P:b * P + P], ident)
                finish(last, u)

        def delta_act(act, step):
            act.wait_ge(S("dl_gsm"), 1)
            act.activation(eG, gsm[:, 0:40], ACT.Exp).then_inc(S("dl_eg"), 1)
            act.activation(eGL, eGL, ACT.Exp).then_inc(S("dl_eg"), 1)
            act.activation(gsm[:, 80:160], gsm[:, 80:160], ACT.Exp).then_inc(S("dl_eg"), 1)
            for tp in range(3):
                emptied(act, ("pR", 1, 3, tp))
            act.activation(gate, gate, ACT.Silu).then_inc(S("gate_silu"), 1)
            for ct in range(12):
                act.wait_ge(S("cv_done"), ct + 1)
                act.activation(cv[ct % 3], cv[ct % 3], ACT.Silu).then_inc(S("cv_silu"), 1)
                if ct >= 1 and (ct - 1) % 2 == 0:
                    conv_read(act, ct - 1)
            scr = dscr2.rearrange("p (t h) d -> p t h d", h=4)
            for c in range(8):
                emptied(act, ("cvT", c))
            hn_act(act, heads4(dq), 0, scr, 1.0, ssq[:, 0:20])
            act.wait_ge(S("dq2_done"), 1)
            hn_act(act, heads4(dk), 0, scr, 1.0, ssq[:, 0:20])
            for n in range(5):
                for d in range(2):
                    if n:
                        emptied(act, ("vs", n - 1, d, 1))
                    if n == 0:
                        act.wait_ge(S("dn_rows"), 1)
                    u = ("kq", n, d)
                    release(copy(act, slot(d, KT_U, 2), filled(act, u).rearrange("p (h c) -> p h c", c=P)), u)
                for d in range(2):
                    emptied(act, ("dec", n, d))
                    act.activation(slot(d, DA_KB, 2), slot(d, DA_KB, 2), ACT.Exp).then_inc(S("dl_exp"), 1)
                for d in range(2):
                    if n:
                        filled(act, ("os", n - 1, d, 1))
                    u = ("qd", n, d)
                    release(copy(act, slot(d, QD_), filled(act, u)[:, 0:512].rearrange("p (h c) -> p h c", c=P)), u)
                for s in range(1, 6):
                    for d in range(2):
                        if s > 1:
                            filled(act, ("x", n, d, s - 1))
                        u = ("w", n, d, s)
                        release(copy(act, slot(d, WT_VN), filled(act, u)[:, 0:512].rearrange("p (h c) -> p h c", c=P)), u)
                for d in range(2):
                    u = ("wu", n, d)
                    release(copy(act, slot(d, KT_U, 2), filled(act, u).rearrange("p (h c) -> p h c", c=P)), u)
            act.wait_ge(S("d_rows"), 2)
            hn_act(act, heads4(oacc), 0, scr, 1.0 / P, ssq[:, 0:20])
            for b in range(4):
                release(copy(act, hT[:, b, :], filled(act, ("cyT", b))[:, 0:T]), ("cyT", b))

        def delta_dve(v, step):
            v.memset(smx[:, 36:37], 0.0).then_inc(S("dl_g"), 1)
            ps = filled(v, "G")
            step(v.tensor_copy(gsm[:, 0:120], ps[:, 0:120]))
            release(v.tensor_copy(gsm[:, 120:160], ps[:, 592:632]), "G")
            emptied(v, "G")
            v.tensor_tensor(eGL, gsm[:, 40:80], gsm[:, 0:40], ALU.subtract).then_inc(S("dl_gsm"), 1)
            v.wait_ge(S("dl_eg"), 3)
            step(v.tensor_tensor(bG, beta, eG, ALU.mult))
            for b in range(4):
                filled(v, ("gyT", b))
            v.wait_ge(S("pad_evac0"), 8)
            v.wait_ge(S("pad_evac1"), 8)
            v.wait_ge(S("caches"), 80)
            for ct in range(12):
                emptied(v, ("pT", 1, ct // 4, ct % 4))
                if ct >= 3:
                    filled(v, ("cvT", ct - 3))
                conv_dve(v, step, cv[ct % 3], pad[:, ct, :],
                         lambda tap: cB[:, dw_col + 12 * tap + ct:dw_col + 12 * tap + ct + 1], None)\
                    .then_inc(S("cv_done"), 1)
                if ct >= 2 and ct % 2 == 0:
                    conv_read(v, ct - 1)
            conv_read(v, 11)
            for c in range(12):
                emptied(v, ("cvT", c))
            hn_dve(v, step, 6, heads4(dq), dscr2, ssq[:, 0:20], 4, P, None, mul=P ** -0.5)
            v.memset(smx[:, 36:37], 0.0).then_inc(S("dq2_done"), 1)
            hn_dve(v, step, 7, heads4(dk), dscr2, ssq[:, 0:20], 4, P, None)
            v.memset(smx[:, 36:37], 0.0).then_inc(S("dn_rows"), 1)
            neg = ("lo_neg", "up_neg")
            for n in range(5):
                for d in range(2):
                    t = tile_of(n, d)
                    step(v.tensor_tensor(slot(d, X_), over_heads(ident), per_head(gsm, t, d), ALU.mult))
                    v.tensor_scalar(slot(d, XT_), slot(d, X_), -1.0, None, ALU.mult).then_inc(S("dl_diag"), 1)
                for d in range(2):
                    u = ("dec", n, d)
                    ps = filled(v, u)[:, 0:512].rearrange("p (h c) -> p h c", c=P)
                    step(v.tensor_tensor(slot(d, DA_KB), ps, over_heads(C[neg[d]]), ALU.add))
                    release(v.tensor_tensor(slot(d, DB_QK), over_heads(C[neg[1 - d]]), ps, ALU.subtract), u)
                for d in range(2):
                    t = tile_of(n, d)
                    v.wait_ge(S("dl_exp"), 2 * n + d + 1)
                    u = ("kk", n, d)
                    ps = filled(v, u).rearrange("p (h c) -> p h c", c=P)
                    step(v.tensor_tensor(slot(d, A_VB), ps[:, 0:4], slot(d, DA_KB), ALU.mult))
                    release(v.tensor_tensor(slot(d, DB_QK), ps[:, 4:8], slot(d, DB_QK), ALU.mult), u)
                    v.tensor_tensor(slot(d, A_VB), slot(d, A_VB), per_head(beta, t, d), ALU.mult)\
                        .then_inc(S(f"dl_A{d}"), 1)
                for d in range(2):
                    v.wait_ge(S(f"dl_am{d}"), 6 * n + 1)
                    u = ("am", n, d)
                    ps = filled(v, u)[:, 0:512].rearrange("p (h c) -> p h c", c=P)
                    release(v.tensor_tensor(slot(d, XT_), over_heads(ident), ps, ALU.subtract), u)
                    emptied(v, u)
                    v.tensor_tensor(slot(d, X_), over_heads(ident), slot(d, AM_KT), ALU.subtract)\
                        .then_inc(S(f"dl_x0{d}"), 1)
                    v.wait_ge(S(f"dl_x0{d}"), n + 1)
                for s in range(1, 6):
                    for d in range(2):
                        u = ("x", n, d, s)
                        ps = filled(v, u).rearrange("p (h c) -> p h c", c=P)
                        if s < 5:
                            release(v.tensor_tensor(slot(d, X_, 2), slot(d, X_, 2), ps, ALU.subtract), u)
                        else:
                            release(v.tensor_tensor(slot(d, XT_), slot(d, XT_), ps[:, 4:8], ALU.subtract), u)
                        emptied(v, u)
                for ci in range(2):
                    for d in range(2):
                        c = chunk_at(ci, d)
                        r = slice(64 * c, 64 * c + 64)
                        emptied(v, ("wu", n, d))
                        u = ("vs", n, d, ci)
                        ps = filled(v, u)[r, 0:512].rearrange("p (h c) -> p h c", c=P)
                        release(v.tensor_tensor(slot(d, WT_VN)[r], slot(d, KT_U)[r], ps, ALU.subtract), u)
                    for d in range(2):
                        c = chunk_at(ci, d)
                        r = slice(64 * c, 64 * c + 64)
                        t = tile_of(n, d)
                        u = ("os", n, d, ci)
                        ps = filled(v, u)
                        first = n < 2 if n < 4 else ci == 0
                        if first:
                            step(v.tensor_copy(oacc[r, t, :], ps[r, 0:512]))
                        else:
                            step(v.tensor_tensor(oacc[r, t, :], oacc[r, t, :], ps[r, 0:512], ALU.add))
                        v.wait_ge(S(f"dl_sd{d}"), 2 * n + ci + 1)
                        release(v.tensor_tensor(sdel[:, 4 * d:4 * d + 4, :], sdec[d],
                                                ps[:, 512:1024].rearrange("p (h c) -> p h c", c=P), ALU.add), u)
                        emptied(v, u)
                        if n == 3 and ci == 1:
                            v.memset(sdel[:, 4 * d:4 * d + 4, :], 0.0).then_inc(S("dl_zero"), 1)
            v.memset(smx[:, 36:37], 0.0).then_inc(S("d_rows"), 1)
            hn_dve(v, step, 8, heads4(oacc), dscr2, ssq[:, 0:20], 4, P, dng)
            v.wait_ge(S("gate_silu"), 1)
            v.tensor_tensor(oacc, oacc, gate, ALU.mult).then_inc(S("dy_rows"), 1)

        def delta_pool(g, step):
            g.wait_ge(S("dn_rows"), 1)
            r4 = lambda x: x.rearrange("p (h d) -> p h d", d=P)
            for n in range(5):
                for d in range(2):
                    t = tile_of(n, d)
                    if n:
                        filled(g, ("os", n - 1, d, 1))
                    g.tensor_tensor(slot(d, WT_VN), r4(dq[:, t, :]), per_head(eG, t, d), ALU.mult)\
                        .then_inc(S("dl_qd"), 1)
                for s in range(6):
                    for d in range(2):
                        if s == 0:
                            g.wait_ge(S(f"dl_A{d}"), n + 1)
                        elif s == 1:
                            g.wait_ge(S(f"dl_x0{d}"), n + 1)
                        else:
                            filled(g, ("w", n, d, s - 1))
                        g.tensor_tensor(slot(d, AM_KT), slot(d, A_VB), over_heads(C[f"{DIRS[d]}{s}"]), ALU.mult)\
                            .then_inc(S(f"dl_am{d}"), 1)
                for d in range(2):
                    t = tile_of(n, d)
                    filled(g, ("w", n, d, 5))
                    g.wait_ge(S(f"dl_am{d}"), 6 * n + 6)
                    step(g.tensor_tensor(slot(d, DA_KB), r4(dk[:, t, :]), per_head(bG, t, d), ALU.mult))
                    step(g.tensor_tensor(slot(d, A_VB), r4(dv[:, t, :]), per_head(beta, t, d), ALU.mult))
                    g.tensor_tensor(slot(d, AM_KT), r4(dk[:, t, :]), per_head(eGL, t, d), ALU.mult)\
                        .then_inc(S(f"dl_kv{d}"), 1)
                for ci in range(2):
                    for d in range(2):
                        t = tile_of(n, d)
                        if ci:
                            emptied(g, ("os", n, d, 0))
                        elif n == 4:
                            g.wait_ge(S("dl_zero"), 2)
                        elif n:
                            emptied(g, ("os", n - 1, d, 1))
                        cd = gsm[:, 80 + 40 * chunk_at(ci, d):]
                        g.tensor_tensor(sdec[d], sdel[:, 4 * d:4 * d + 4, :], per_head(cd, t, d), ALU.mult)\
                            .then_inc(S(f"dl_sd{d}"), 1)
            for d in range(2):
                emptied(g, ("os", 4, d, 1))
            g.dma_start(outs["new_state_delta"][0, 0].rearrange("r h k v -> k (r h) v"), sdel[:, :, :])\
                .then_inc(S("caches"), 16)

        def layer1_outputs(g):
            g.wait_ge(S("cache_k_ready"), 2)
            g.dma_start(outs["new_cache_gqa_k"].rearrange("a b t h d -> t (a b h d)"), z2[:, ST, 528:656])\
                .then_inc(S("caches"), 16)
            g.dma_start(outs["new_cache_gqa_v"].rearrange("a b t h d -> t (a b h d)"), z2[:, ST, 656:784])\
                .then_inc(S("caches"), 16)

        def layer1_ready(pe):
            for b in range(4):
                emptied(pe, ("gyT", b))
                emptied(pe, ("cyT", b))

        ctx.enter_context(nc.allow_non_contiguous_dma(reason="weights' column chunks"))
        block = ctx.enter_context(nc.Block())

        @block.tensor
        def _(pe):
            setup_pe(pe)
            for l in range(2):
                if l == 0:
                    mod_rows_pe(pe, 0)
                norm_pe(pe, l, 0)
                if l == 0:
                    for i in range(1, 4):
                        mod_rows_pe(pe, i)
                        mod_turn_pe(pe, i - 1)
                    mod_turn_pe(pe, 3)
                for c in range(2 + l):
                    proj_T_pe(pe, l, c)
                for c in range(2 + l, 5 + l):
                    proj_R_pe(pe, l, c)
                if l == 0:
                    lru_pe(pe)
                    diff_pe(pe)
                else:
                    gqa_pe(pe)
                    delta_pe(pe)
                out_pe(pe, l)
                norm_pe(pe, l, 1)
                route_pe(pe, l)
                moe_pe(pe, l)
                sum_pe(pe, l)
            store_pe(pe)

        @block.scalar
        def _(act):
            step = Steps(act, S("act_step"))
            setup_act(act, step)
            for l in range(2):
                norm_squares_act(act, l, 0)
                if l == 0:
                    mod_act(act, 0)
                norm_root_act(act, l, 0)
                if l == 0:
                    for i in range(1, 4):
                        mod_act(act, i)
                norm_shift_act(act, l, 0)
                if l == 0:
                    read_T(act, 0, 0, xap, 0, True)
                    read_T(act, 0, 1, ga, 0, False)
                    for c in (2, 3, 4):
                        read_R(act, 0, c, qkv[:, :, 512 * (c - 2):512 * (c - 1)], 0)
                    lru_act(act, step)
                    diff_act(act, step)
                else:
                    for c in range(3):
                        read_T(act, 1, c, pad[:, 4 * c:4 * c + 4, :], 0, True)
                    read_R(act, 1, 3, gate, 0)
                    read_R(act, 1, 4, z2[:, :, 0:512], 0)
                    read_R(act, 1, 5, z2[:, :, 512:784], 0)
                    filled(act, ("pR", 1, 5, 2))
                    gqa_act(act, step)
                    delta_act(act, step)
                norm_squares_act(act, l, 1)
                norm_root_act(act, l, 1)
                norm_shift_act(act, l, 1)
                route_act(act, step, l)
                moe_act_run(act, l)
                gather_sum_act(act, l)
            store_read(act, 0)

        @block.vector
        def _(v):
            step = Steps(v, S("dve_step"))
            setup_dve(v, step)
            for l in range(2):
                if l == 0:
                    for k in range(1, KD):
                        norm_add_dve(v, 0, 0, k)
                    for i in range(4):
                        mod_dve(v, step, i)
                    mods_done(v, 3)
                norm_dve(v, step, l, 0)
                if l == 0:
                    pads_dve(v, step, xap)
                    read_T(v, 0, 0, xap, 1, True)
                    read_T(v, 0, 1, ga, 1, False)
                    for c in (2, 3, 4):
                        read_R(v, 0, c, qkv[:, :, 512 * (c - 2):512 * (c - 1)], 1)
                else:
                    pads_dve(v, step, pad)
                    for c in range(3):
                        read_T(v, 1, c, pad[:, 4 * c:4 * c + 4, :], 1, True)
                    read_R(v, 1, 3, gate, 1)
                    read_R(v, 1, 4, z2[:, :, 0:512], 1)
                    read_R(v, 1, 5, z2[:, :, 512:784], 1)
                if l == 0:
                    lru_dve(v, step)
                    diff_dve(v, step)
                else:
                    gqa_dve(v, step)
                    delta_dve(v, step)
                if l == 0:
                    mods_done(v, 11)
                residual_dve(v, step, l, "out")
                norm_dve(v, step, l, 1)
                route_dve(v, step, l)
                moe_dve(v, l)
                residual_dve(v, step, l, "ms")
            store_read(v, 1)

        @block.gpsimd
        def _(g):
            step = Steps(g, S("pool_step"))
            setup_pool(g)
            layer0_outputs(g)
            route_pool(g, 0)
            moe_pool(g, 0)
            layer1_outputs(g)
            delta_pool(g, step)
            route_pool(g, 1)
            moe_pool(g, 1)

        @block.sync
        def _(sp):
            load_stream(sp)
            store_sp(sp, 6)


_PLAIN = ["x_prompt", "x_sample", "cache_diff_k", "cache_diff_v", "state_delta", "cache_gqa_k", "cache_gqa_v",
          "w_mod", "w_in_ab", "lru_wa", "lru_wi", "w_in_cd", "w_out", "router_w", "exp_w1", "exp_w3", "exp_w2"]
_OUTS = {"y_prompt": (1, 128, 1024), "y_sample": (1, 512, 1024), "new_state_lru": (1, 1, 2, 512),
         "new_cache_diff_k": (1, 1, 128, 4, 2, 64), "new_cache_diff_v": (1, 1, 128, 4, 128),
         "new_state_delta": (1, 1, 2, 4, 128, 128), "new_cache_gqa_k": (1, 1, 128, 2, 64),
         "new_cache_gqa_v": (1, 1, 128, 2, 64)}


def layout(inputs):
    import numpy as np
    a = {k: np.ascontiguousarray(inputs[k]) for k in _PLAIN}
    r = lambda k: np.asarray(inputs[k]).reshape(-1, P)
    a["colsA"] = np.concatenate([r(k) for k in ("norm1_g", "norm2_g", "b_mod")])
    a["colsB"] = np.concatenate([r(k) for k in ("c", "c_ctx", "lru_conv_b", "lru_ba", "lru_bi", "lru_lam", "state_lru",
                                                "lru_conv_w", "delta_conv_w")])
    a["params"] = np.concatenate([np.asarray(inputs[k]).reshape(1, -1) for k in
                                  ("diff_q_gain", "diff_k_gain", "gqa_q_gain", "gqa_k_gain", "diff_sub_gain",
                                   "delta_norm_g", "delta_a_log", "delta_dt_bias", "diff_lam")], axis=1)
    t = np.arange(NS)
    inv = (10000.0 ** (-np.arange(16, dtype=np.float32) / 16)).astype(np.float32)
    ang = np.concatenate([(t // 64).astype(np.float32)[:, None] * inv, (t % 64).astype(np.float32)[:, None] * inv], 1)
    a["rope"] = np.concatenate([np.cos(ang), np.sin(ang)], 1).astype(np.float32)
    i, j = np.arange(P)[:, None], np.arange(P)[None, :]
    same = i // CK == j // CK
    lo, up = same & (j <= i), same & (j >= i)
    c = [i == j, i >= 0 * j, np.where(lo, 0.0, NEG), np.where(up, 0.0, NEG), lo, up, same]
    lev = [(i // (2 << s) == j // (2 << s)) & (i // (1 << s) > j // (1 << s)) for s in range(6)]
    c += lev + [m.T for m in lev]
    a["consts"] = np.stack([np.broadcast_to(m, (P, P)).astype(np.float32) for m in c])
    return a


def program(nc, arrays):
    io = {k: nc.dram_tensor("in_" + k, v.shape, F32, kind="ExternalInput").ap() for k, v in arrays.items()}
    outs = {k: nc.dram_tensor("out_" + k, s, F32, kind="ExternalOutput").ap() for k, s in _OUTS.items()}
    build(nc, io, outs)


def kernel(**inputs):
    import concourse.bacc as _bacc
    from concourse.bass_utils import run_bass_kernel_spmd as _run
    arrays = layout(inputs)
    nc = _bacc.Bacc("TRN2", target_bir_lowering=False, num_devices=1)
    program(nc, arrays)
    r = _run(nc, [{"in_" + k: v for k, v in arrays.items()}], core_ids=[0])
    return tuple(r.results[0]["out_" + k] for k in _OUTS)
```

```python
from contextlib import ExitStack

import concourse.bass as bass
from concourse import mybir

F32 = mybir.dt.float32
U32 = mybir.dt.uint32
ACT = mybir.ActivationFunctionType
ALU = mybir.AluOpType
AX_X = mybir.AxisListType.X

P = 128
D = 1024
KD = D // P
NS, NP = 512, 128
T = NS + NP
NT = T // P
ST = NS // P
HD = 64
PADW = NS + NP + 6
PS0, PP0 = 2, NS + 5
UW = PADW - 3
UP0 = NS + 3
NE, CAPS, CAPP = 16, 64, 16
CAP = CAPS + CAPP
FF = 512
FT = FF // P
NIN_AB, NIN_CD = 2560, 2832
CK = 64
NEG = -1.0e30
LAM_INIT = 0.2
CONSTS = ["ident", "ones", "lo_neg", "up_neg", "lo_one", "up_one", "block"] + [f"f{s}" for s in range(6)] + \
         [f"b{s}" for s in range(6)]


class Units:

    def __init__(self):
        self.uses = [0] * 4
        self.of = {}
        self.next = 0

    def add(self, name, pair=None):
        if pair is None:
            pair = self.next % 4
            self.next += 1
        self.uses[pair] += 1
        self.of[name] = (pair, self.uses[pair])
        return self.of[name]


class Steps:

    def __init__(self, eng, sem):
        self.eng, self.sem, self.n = eng, sem, 0

    def __call__(self, ins):
        self.n += 1
        ins.then_inc(self.sem, 1)
        self.eng.wait_ge(self.sem, self.n)


def build(nc, io, outs):
    with ExitStack() as ctx:
        def sb(name, shape, dt=F32):
            return ctx.enter_context(nc.sbuf_tensor(name, shape, dt))

        sems = {}

        def S(name):
            if name not in sems:
                sems[name] = ctx.enter_context(nc.semaphore("s_" + name))
            return sems[name]

        PSUM = ctx.enter_context(nc.psum_tensor("pairs", [P, 4, 1024], F32))
        pair_full = [S(f"pair_full{i}") for i in range(4)]
        pair_free = [S(f"pair_free{i}") for i in range(4)]
        units = Units()

        xT = sb("xT", [P, KD, T])
        hT = sb("hT", [P, KD, T])
        ring = sb("ring", [P, 3, 4096])
        cst = sb("cst", [P, len(CONSTS), P])
        rope = sb("rope", [P, ST, HD])
        cA = sb("cA", [P, P])
        cB = sb("cB", [P, P])
        par = sb("par", [P, 784])
        modt = sb("modt", [P, 2, 48, 2])
        gsc = sb("gsc", [P, 2, 2, KD, 2])
        csil = sb("csil", [P, KD, 2])
        dk_c = sb("dk_c", [P, 512])
        dv_c = sb("dv_c", [P, 512])
        gk_c = sb("gk_c", [P, 128])
        gv_c = sb("gv_c", [P, 128])
        sdel = sb("sdel", [P, 8, P])
        wr = sb("wr", [P, 2, KD, NE])
        sm = sb("sm", [P, 640])
        AR = 23400
        arena = sb("arena", [P, AR])

        C = {n: cst[:, i, :] for i, n in enumerate(CONSTS)}
        ident, ones = C["ident"], C["ones"]

        def ar(off, *shape):
            n = 1
            for x in shape:
                n *= x
            assert off + n <= AR, (off, n)
            v = arena[:, off:off + n]
            if len(shape) == 2:
                v = v.rearrange("p (a b) -> p a b", b=shape[1])
            elif len(shape) == 3:
                v = v.rearrange("p (a b c) -> p a b c", b=shape[1], c=shape[2])
            return v

        hflat = hT[:, :, :].rearrange("p k t -> p (k t)")
        rows = ar(0, NT, D)
        c_cols, cb_col, ba_col, bi_col, lam_col, st_col, lw_col, dw_col = \
            cB[:, 0:16], 16, 20, 28, 36, 44, 52, 68
        dqg, dkg, gqg, gkg = (par[:, 64 * i:64 * i + 64] for i in range(4))
        dsg, dng = par[:, 256:384], par[:, 384:512]
        alog, dtb = par[:, 512:520], par[:, 520:528]
        dlam = par[:, 528:784]
        hs = sm[:, 0:8]
        nlam = sm[:, 8:9]
        hba, hbi = sm[:, 16:24], sm[:, 24:32]
        spt = sm[:, 32:112]
        stl = sm[:, 112:120]
        smx = sm[:, 120:160]
        nmax = lambda i, c=0: smx[:, 2 * (i % 4) + c:2 * (i % 4) + c + 1]
        psum_of = lambda i, c=0, n=1: smx[:, 8 + 2 * (i % 4) + c:8 + 2 * (i % 4) + c + n]
        rsum = lambda i, c=0, n=1: smx[:, 16 + 2 * (i % 4) + c:16 + 2 * (i % 4) + c + n]
        ratio = lambda i: smx[:, 24 + i % 4:25 + i % 4]
        ssq = sm[:, 160:200]
        sps = sm[:, 200:208]
        anl = sm[:, 208:216]

        DR = {}
        for l in range(2):
            DR["h", l] = nc.dram_tensor(f"h_rows{l}", (T, D), F32, kind="Internal").ap()
            DR["m", l] = nc.dram_tensor(f"moe_rows{l}", (T, D), F32, kind="Internal").ap()

        def take(pe, name, pair=None):
            pair, n = units.add(name, pair)
            if n > 1:
                pe.wait_ge(pair_free[pair], n - 1)
            return PSUM[:, pair, :]

        def finish(ins, name):
            ins.then_inc(pair_full[units.of[name][0]], 1)

        def filled(eng, name):
            pair, n = units.of[name]
            eng.wait_ge(pair_full[pair], n)
            return PSUM[:, pair, :]

        def release(ins, name):
            ins.then_inc(pair_free[units.of[name][0]], 1)

        def emptied(eng, name):
            pair, n = units.of[name]
            eng.wait_ge(pair_free[pair], n)

        def mmk(pe, out, lhs, rhs):
            for k in range(KD):
                last = pe.matmul(out, lhs(k), rhs(k), start=(k == 0), stop=(k == KD - 1))
            return last

        mods = [[("mod", l, m, h) for m in range(6) for h in range(2)] for l in range(2)]
        ins = [[("in", l, c, 0) for c in order] for l, order in enumerate(((0, 1, 2, 3, 4), (4, 5, 0, 1, 2, 3)))]
        wouts = [[("out", l, h, 0) for h in range(2)] for l in range(2)]
        N_DIFF_MODS = 8
        chunks = [mods[0][:4] + ins[0] + mods[0][4:] + mods[1][:N_DIFF_MODS] + wouts[0] + mods[1][N_DIFF_MODS:],
                  ins[1] + wouts[1]]
        slot_of, slot_uses = {}, [0] * 6
        last_in_slot = {}
        loads = []
        for l in range(2):
            for i, c in enumerate(chunks[l]):
                s = i % 3
                slot_uses[s] += 1
                slot_of[c] = (s, slot_uses[s])
                loads.append((c, s, last_in_slot.get(s)))
                last_in_slot[s] = c
            base = list(slot_uses)
            for s in range(6):
                slot_uses[s] += NE // 2
                slot_of["exp", l, s] = base[s]
            loads.append((("experts", l), None, dict(last_in_slot)))
            for s in range(3):
                last_in_slot[s] = ("experts", l)
        slots = [ring[:, s, :] for s in range(3)] + [ar(4096 * s, 4096) for s in range(3)]
        w_here = [S(f"w_here{s}") for s in range(6)]

        def chunk_src(c):
            kind, l, a, b = c
            if kind == "mod":
                return io["w_mod"][l][:, 1024 * a + 512 * b:1024 * a + 512 * b + 512], 512
            if kind == "in":
                w = io["w_in_ab" if l == 0 else "w_in_cd"][0]
                n = min(512, w.shape[1] - 512 * a)
                return w[:, 512 * a:512 * a + n], n
            return io["w_out"][l][:, 512 * a:512 * a + 512], 512

        def chunk(c):
            n = chunk_src(c)[1]
            return slots[slot_of[c][0]][:, 0:KD * n].rearrange("p (k n) -> p k n", n=n)

        def arrived(pe, c):
            s, n = slot_of[c]
            pe.wait_ge(w_here[s], 16 * n)
            return chunk(c)

        chunk_last = {}

        W1 = [io["exp_w1"][l].rearrange("e (k p) f -> p (e k) f", p=P) for l in range(2)]
        W3 = [io["exp_w3"][l].rearrange("e (k p) f -> p (e k) f", p=P) for l in range(2)]
        W2 = [io["exp_w2"][l].rearrange("e (k p) d -> p (e k) d", p=P) for l in range(2)]
        moe_base = {}

        def setup_dma(act):
            q = S("cols_here")
            act.dma_start(ar(6000, 128), io["colsA"]).then_inc(q, 16)
            act.dma_start(ar(6200, 128)[0:116, :], io["colsB"]).then_inc(q, 16)
            act.dma_start(cst[:, 0:2, :], io["consts"][0:2].rearrange("n p m -> p n m")).then_inc(q, 16)
            q = S("x_here")
            for t in range(ST):
                act.dma_start(rows[:, t, :], io["x_sample"][0, t * P:t * P + P, :]).then_inc(q, 16)
            act.dma_start(rows[:, ST, :], io["x_prompt"][0]).then_inc(q, 16)
            act.dma_start(par[:, :], io["params"].to_broadcast((P, 784))).then_inc(S("par_here"), 16)

        def setup_late_dma(act):
            q = S("late_here")
            act.dma_start(rope[:, :, :], io["rope"].rearrange("(t p) n -> p t n", p=P)).then_inc(q, 16)
            act.dma_start(cst[:, 2:, :], io["consts"][2:].rearrange("n p m -> p n m")).then_inc(q, 16)
            act.dma_start(dk_c[:, :], io["cache_diff_k"][0, 0].rearrange("t h c d -> t (h c d)")).then_inc(q, 16)
            act.dma_start(dv_c[:, :], io["cache_diff_v"][0, 0].rearrange("t h d -> t (h d)")).then_inc(q, 16)
            act.dma_start(gk_c[:, :], io["cache_gqa_k"][0, 0].rearrange("t h d -> t (h d)")).then_inc(q, 16)
            act.dma_start(gv_c[:, :], io["cache_gqa_v"][0, 0].rearrange("t h d -> t (h d)")).then_inc(q, 16)
            act.dma_start(sdel[:, :, :], io["state_delta"][0, 0].rearrange("r h k v -> k (r h) v")).then_inc(q, 16)
            for l in range(2):
                act.dma_start(wr[:, l, :, :], io["router_w"][l].rearrange("(k p) e -> p k e", p=P)).then_inc(q, 16)

        wg = ar(10000, 16, P).rearrange("p (q c) m -> p q c m", c=4)

        def setup_gates_dma(act):
            q = S("late_here")
            for r in range(2):
                for i, w in enumerate(("lru_wa", "lru_wi")):
                    for half in range(2):
                        src = io[w][0, r].rearrange("(t h) c d -> h c t d", h=2)[half]
                        act.dma_start(wg[64 * half:64 * half + 64, 2 * r + i, :, 64 * half:64 * half + 64],
                                      src).then_inc(q, 16)
        LATE_ALL = 16 * (9 + 8)

        def setup_pe(pe):
            pe.wait_ge(S("cols_here"), 16 * 3)
            ps = take(pe, "cols")
            pe.transpose(ps[:, 0:P], ar(6000, 128), ident)
            finish(pe.transpose(ps[:, 512:628], ar(6200, 128)[0:116, :], ident[0:116, 0:116]), "cols")
            mod_rows_pe(pe, 0)
            pe.wait_ge(S("x_here"), 16 * NT)
            flip_in_pe(pe, "x_in")

        def flip_in_pe(pe, tag):
            for k in range(KD):
                ps = take(pe, (tag, k))
                for t in range(NT):
                    last = pe.transpose(ps[:, t * P:t * P + P], rows[:, t, k * P:k * P + P], ident)
                finish(last, (tag, k))

        def mark(v):
            return v.memset(smx[:, 36:37], 0.0)

        def copy(eng, dst, src):
            return eng.activation(dst, src, ACT.Copy) if eng is nc.scalar else eng.tensor_copy(dst, src)

        def flip_in_read(eng, tag, part):
            for k in range(part, KD, 2):
                release(copy(eng, xT[:, k, :], filled(eng, (tag, k))[:, 0:T]), (tag, k))

        def softplus_act(act, step, x, e):
            step(act.activation(e, x, ACT.Abs))
            return act.activation(e, e, ACT.Exp, scale=-1.0)

        def softplus_dve(v, step, x, e, z, z2, out):
            step(v.tensor_scalar(z, e, 2.0, None, ALU.add))
            step(v.reciprocal(z, z))
            step(v.tensor_tensor(z, e, z, ALU.mult))
            step(v.tensor_tensor(z2, z, z, ALU.mult))
            step(v.tensor_scalar(e, z2, 1.0 / 17, 1.0 / 15, ALU.mult, ALU.add))
            for n in (13, 11, 9, 7, 5, 3, 1):
                step(v.tensor_tensor(e, e, z2, ALU.mult))
                step(v.tensor_scalar(e, e, 1.0 / n, None, ALU.add))
            step(v.tensor_tensor(e, e, z, ALU.mult))
            step(v.tensor_scalar(z, x, 0.0, None, ALU.max))
            step(v.scalar_tensor_tensor(out=out, in0=e, scalar=2.0, in1=z, op0=ALU.mult, op1=ALU.add))

        negl = sm[:, 216:224]
        zeros = ar(12288, D)

        def setup_act(act, step):
            setup_dma(act)
            act.wait_ge(S("cB"), 1)
            act.activation(csil[:, :, :].rearrange("p k g -> p g k"), c_cols.rearrange("p (g k) -> p g k", g=2),
                           ACT.Silu).then_inc(S("csil"), 1)
            mod_act(act, 0)
            flip_in_read(act, "x_in", 0)

        def setup_late_act(act, step):
            act.wait_ge(S("negl"), 1)
            softplus_act(act, step, negl, spt[:, 0:8]).then_inc(S("sp_exp"), 1)
            act.wait_ge(S("lam_dot"), 1)
            act.activation(sps[:, 2:4], sps[:, 0:2], ACT.Exp).then_inc(S("lam_exp"), 1)

        def setup_dve(v, step):
            v.memset(zeros, 0.0).then_inc(S("zeroed"), 1)
            v.memset(ar(10000, 2048), 0.0).then_inc(S("zeroed"), 1)
            ps = filled(v, "cols")
            v.tensor_copy(cB[:, 0:116], ps[:, 512:628]).then_inc(S("cB"), 1)
            release(v.tensor_copy(cA[:, :], ps[:, 0:P]), "cols")
            flip_in_read(v, "x_in", 1)

        def setup_late_dve(v, step):
            v.wait_ge(S("cB"), 1)
            v.tensor_scalar(negl, cB[:, lam_col:lam_col + 8], -1.0, None, ALU.mult).then_inc(S("negl"), 1)
            v.wait_ge(S("negl"), 1)
            v.wait_ge(S("sp_exp"), 1)
            softplus_dve(v, step, negl, spt[:, 0:8], spt[:, 8:16], spt[:, 16:24], spt[:, 24:32])
            step(v.tensor_scalar(hs, spt[:, 24:32], -4.0, None, ALU.mult))
            step(v.tensor_scalar(hba, cB[:, ba_col:ba_col + 8], 0.5, None, ALU.mult))
            step(v.tensor_scalar(hbi, cB[:, bi_col:bi_col + 8], 0.5, None, ALU.mult))
            v.wait_ge(S("par_here"), 16)
            dl = dlam.rearrange("p (a b d) -> p a b d", a=2, b=2)
            step(v.tensor_tensor(ar(6400, 2, 64), dl[:, :, 0, :], dl[:, :, 1, :], ALU.mult))
            v.tensor_reduce(sps[:, 0:2], ar(6400, 2, 64), AX_X, ALU.add).then_inc(S("lam_dot"), 1)
            v.wait_ge(S("lam_exp"), 1)
            step(v.tensor_tensor(sps[:, 4:5], sps[:, 3:4], sps[:, 2:3], ALU.subtract))
            step(v.tensor_scalar(nlam, sps[:, 4:5], -LAM_INIT, None, ALU.add))
            step(v.tensor_scalar(dsg, dsg, 1.0 - LAM_INIT, None, ALU.mult))
            step(v.tensor_scalar(dqg, dqg, HD ** -0.5, None, ALU.mult))
            step(v.tensor_scalar(gqg, gqg, HD ** -0.5, None, ALU.mult))

        def setup_pool(g):
            g.wait_ge(S("zeroed"), 1)
            filled(g, ("mod_rows", 3))
            for l in range(2):
                g.dma_start(DR["m", l].rearrange("(t p) d -> p t d", p=P),
                            zeros.unsqueeze(1).broadcast_to((P, NT, D))).then_inc(S(f"y_room{l}"), 16)

        mrow = [ar(22360 + 512 * i, 512)[0:2, :] for i in range(2)]
        all_mods = mods[0] + mods[1]

        def mod_rows_pe(pe, i, pair=None):
            c = all_mods[i]
            if i == 0:
                pe.wait_ge(S("csil"), 1)
            w = arrived(pe, c)
            u = ("mod_rows", i)
            ps = take(pe, u, pair)
            finish(mmk(pe, ps[0:2, 0:512], lambda k: csil[:, k, :], lambda k: w[:, k, :]), u)
            chunk_last[c] = u

        def mod_turn_pe(pe, i, pair=None):
            emptied(pe, ("mod_rows", i))
            u = ("mod", i)
            ps = take(pe, u, pair)
            for f in range(4):
                last = pe.transpose(ps[:, 2 * f:2 * f + 2], mrow[i % 2][:, f * P:f * P + P], ident[0:2, 0:2])
            finish(last, u)

        def mod_act(act, i):
            if i >= 2:
                filled(act, ("mod", i - 2))
            u = ("mod_rows", i)
            release(copy(act, mrow[i % 2], filled(act, u)[0:2, 0:512]), u)

        def mod_dve(v, step, i):
            _, l, m, h = all_mods[i]
            u = ("mod", i)
            c0 = 8 * m + 4 * h
            ps = filled(v, u)[:, 0:8].rearrange("p (f g) -> p f g", g=2)
            b = cA[:, 32 + 48 * l + c0:32 + 48 * l + c0 + 4].unsqueeze(2).broadcast_to((P, 4, 2))
            if i == 0:
                emptied(v, "cols")
            release(v.tensor_tensor(modt[:, l, c0:c0 + 4, :], ps, b, ALU.add), u)
            if m in (1, 4) and h == 1:
                emptied(v, u)
                emptied(v, ("mod", i - 1))
                n = m // 4
                g = cA[:, 16 * n + 8 * l:16 * n + 8 * l + 8].unsqueeze(2).broadcast_to((P, KD, 2))
                step(v.scalar_tensor_tensor(out=gsc[:, l, n, :, :], in0=modt[:, l, 8 * m:8 * m + 8, :], scalar=1.0,
                                            in1=g, op0=ALU.add, op1=ALU.mult))

        def mods_done(eng, i):
            for j in range(max(0, i - 3), i + 1):
                emptied(eng, ("mod", j))

        sq = ar(20000, 2, T)
        ssum = ar(21280, T)
        rstd = ar(19300, T)
        seg = ((0, NS), (NS, T))

        ADDS = {(0, 0): 0, (0, 1): KD - 1, (1, 1): 2 * (KD - 1)}
        sq_all = ar(0, KD, T)

        def norm_pe(pe, l, n):
            u = ("nrm", l, n)
            pe.wait_ge(S("sq_add"), ADDS[l, n] + KD - 1)
            ps = take(pe, u)
            pe.matmul(ps[:, 0:NS], ones, ssum[:, 0:NS], start=True, stop=True)
            finish(pe.matmul(ps[:, NS:T], ones, ssum[:, NS:T], start=True, stop=True), u)

        def x_unit(l, n, k):
            return ("x_in", k) if (l, n) == (0, 0) else ("out", l, k) if n else ("ms", l - 1, k)

        def norm_squares_act(act, l, n):
            i = 2 * l + n
            if n == 1:
                act.wait_ge(S("caches"), (48, 96)[l])
            for k in range(KD):
                emptied(act, x_unit(l, n, k))
                if i:
                    act.wait_ge(S("x_half"), 8 * (i - 1) + k + 1)
                if k >= 2 and (l, n) != (1, 0):
                    act.wait_ge(S("sq_add"), ADDS[l, n] + max(1, k - 2))
                act.activation(sq_all[:, k, :] if (l, n) == (1, 0) else sq[:, k % 2, :], xT[:, k, :], ACT.Square).then_inc(S("sq"), 1)

        def norm_root_act(act, l, n):
            ps = filled(act, ("nrm", l, n))
            release(act.activation(rstd, ps[:, 0:T], ACT.Sqrt, scale=1.0 / D, bias=1e-6), ("nrm", l, n))

        def norm_shift_act(act, l, n):
            i = 2 * l + n
            for k in range(KD):
                for g in range(2):
                    a, b = seg[g]
                    act.wait_ge(S("h_scaled"), i * 16 + 2 * k + g + 1)
                    act.activation(hT[:, k, a:b], hT[:, k, a:b], ACT.Identity,
                                   bias=modt[:, l, 24 * n + k, g:g + 1]).then_inc(S("h_ready"), 1)

        def norm_add(v, l, n, k):
            i = 2 * l + n
            v.wait_ge(S("sq"), 8 * i + k + 1)
            if k > 1:
                v.wait_ge(S("sq_add"), ADDS[l, n] + k - 1)
            v.tensor_tensor(ssum, sq[:, 0, :] if k == 1 else ssum, sq[:, k % 2, :], ALU.add).then_inc(S("sq_add"), 1)

        def norm_rstd_dve(v, step, l, n):
            emptied(v, ("nrm", l, n))
            step(v.reciprocal(rstd, rstd))

        def norm_scale_dve(v, l, n):
            for k in range(KD):
                emptied(v, x_unit(l, n, k))
                for g in range(2):
                    a, b = seg[g]
                    v.scalar_tensor_tensor(out=hT[:, k, a:b], in0=xT[:, k, a:b], scalar=gsc[:, l, n, k, g:g + 1],
                                           in1=rstd[:, a:b], op0=ALU.mult, op1=ALU.mult)\
                        .then_inc(S("h_scaled"), 1)

        def proj_T_pe(pe, l, c):
            w = arrived(pe, ("in", l, c, 0))
            for f in range(4):
                u = ("pT", l, c, f)
                ps = take(pe, u)
                lhs = lambda k: w[:, k, f * P:f * P + P]
                if l == 0 and c == 0 and f == 0:
                    for k in range(KD):
                        pe.wait_ge(S("h_ready"), 32 * l + 2 * k + 2)
                        pe.matmul(ps[:, 0:NS], lhs(k), hT[:, k, 0:NS], start=(k == 0), stop=(k == KD - 1))
                        last = pe.matmul(ps[:, NS:T], lhs(k), hT[:, k, NS:T], start=(k == 0), stop=(k == KD - 1))
                    finish(last, u)
                    continue
                mmk(pe, ps[:, 0:NS], lhs, lambda k: hT[:, k, 0:NS])
                finish(mmk(pe, ps[:, NS:T], lhs, lambda k: hT[:, k, NS:T]), u)
            chunk_last["in", l, c, 0] = u

        def proj_R_pe(pe, l, c):
            w = arrived(pe, ("in", l, c, 0))
            n = chunk_src(("in", l, c, 0))[1]
            for tp in range(3):
                u = ("pR", l, c, tp)
                ps = take(pe, u)
                if l == 1 and c == 4 and tp == 0:
                    for k in range(KD):
                        pe.wait_ge(S("h_ready"), 32 * l + 2 * k + 2)
                        for t in range(2):
                            last = pe.matmul(ps[:, 512 * t:512 * t + n], hT[:, k, t * P:t * P + P], w[:, k, 0:n],
                                             start=(k == 0), stop=(k == KD - 1))
                    finish(last, u)
                    continue
                for t in range(2 * tp, min(2 * tp + 2, NT)):
                    o = 512 * (t % 2)
                    last = mmk(pe, ps[:, o:o + n], lambda k: hT[:, k, t * P:t * P + P], lambda k: w[:, k, 0:n])
                finish(last, u)
            chunk_last["in", l, c, 0] = u

        def read_T(eng, l, c, dst, part, padded):
            for f in range(part, 4, 2):
                u = ("pT", l, c, f)
                ps = filled(eng, u)
                if padded:
                    copy(eng, dst[:, f, PS0:PS0 + NS], ps[:, 0:NS]).then_inc(S("pad_evac" + str(part)), 1)
                    release(copy(eng, dst[:, f, PP0:PP0 + NP], ps[:, NS:T]), u)
                else:
                    release(copy(eng, dst[:, f, :], ps[:, 0:T]), u)

        def read_R(eng, l, c, dst, part):
            n = chunk_src(("in", l, c, 0))[1]
            if l == 0 and c == 2:
                eng.wait_ge(S("y_room0"), 16)
                eng.wait_ge(S("y_room1"), 16)
            for tp in range(3):
                if (tp + c) % 2 == part:
                    u = ("pR", l, c, tp)
                    ps = filled(eng, u)
                    m = 2 if tp < 2 else 1
                    release(copy(eng, dst[:, 2 * tp:2 * tp + m, :],
                                 ps.rearrange("p (a b) -> p a b", a=2)[:, 0:m, 0:n]), u)

        xap = ar(0, 4, PADW)
        ga = ar(2584, 4, T)
        qkv = ar(12048, NT, 1536)
        uT = ar(5144, 4, UW)
        lb = [[hflat[:, 2560 + 0 * UW:2560 + UW], hflat[:, 2560 + UW:2560 + 2 * UW],
               hflat[:, 2560 + 2 * UW:2560 + 3 * UW], ar(7716, UW)],
              [ar(7716 + UW, UW), ar(7716 + 2 * UW, UW), ar(19728 + 0 * UW, UW), ar(19728 + UW, UW)]]
        hfb = [ar(19728 + 2 * UW, UW), ar(19728 + 3 * UW, UW)]

        def pads_dve(v, step, pad):
            step(v.memset(pad[:, :, 0:2], 0.0))
            step(v.memset(pad[:, :, PS0 + NS:PP0], 0.0))
            step(v.memset(pad[:, :, PADW - 1:PADW], 0.0))

        def conv_dve(v, step, out, src, w, b):
            if b is None:
                step(v.tensor_scalar(out, src[:, 0:UW], w(0), None, ALU.mult))
            else:
                step(v.tensor_scalar(out, src[:, 0:UW], w(0), b, ALU.mult, ALU.add))
            for tap in range(1, 4):
                ins = v.scalar_tensor_tensor(out=out, in0=src[:, tap:tap + UW], scalar=w(tap), in1=out,
                                             op0=ALU.mult, op1=ALU.add)
                if tap < 3:
                    step(ins)
            return ins

        def lru_pe(pe):
            pe.wait_ge(S("late_here"), LATE_ALL)
            for ct in range(4):
                pe.wait_ge(S("u_ready"), ct + 1)
                for q in range(4):
                    u = ("gate", ct, q)
                    ps = take(pe, u)
                    pe.matmul(ps[:, 0:NS], wg[:, q, ct, :], uT[:, ct, 0:NS], start=True, stop=True)
                    finish(pe.matmul(ps[:, NS:UW], wg[:, q, ct, :], uT[:, ct, NS:UW], start=True, stop=True), u)
                    if q % 2 == 1:
                        i = 2 * ct + q // 2
                        mod_rows_pe(pe, 4 + i)
                        if i:
                            mod_turn_pe(pe, 3 + i)
            mod_turn_pe(pe, 11)

        def lru_act(act, step):
            act.wait_ge(S("qk_rows"), 1)
            for i in range(9):
                if i < 8:
                    ct, d = i // 2, i % 2
                    tr, ti, a, _ = lb[i % 2]
                    c8 = 4 * d + ct
                    if i == 0:
                        filled(act, ("pR", 0, 4, 2))
                    if i >= 2:
                        act.wait_ge(S("lru_scan"), i - 1)
                    release(act.activation(tr, filled(act, ("gate", ct, 2 * d))[:, 0:UW], ACT.Tanh, scale=0.5,
                                           bias=hba[:, c8:c8 + 1]), ("gate", ct, 2 * d))
                    release(act.activation(ti, filled(act, ("gate", ct, 2 * d + 1))[:, 0:UW], ACT.Tanh, scale=0.5,
                                           bias=hbi[:, c8:c8 + 1]), ("gate", ct, 2 * d + 1))
                    emptied(act, ("gate", ct, 2 * d))
                    step(act.activation(a, tr, ACT.Exp, scale=hs[:, c8:c8 + 1], bias=hs[:, c8:c8 + 1]))
                    act.activation(tr, tr, ACT.Tanh, scale=hs[:, c8:c8 + 1], bias=hs[:, c8:c8 + 1])\
                        .then_inc(S("lru_tanh"), 1)
                if i >= 1:
                    act.wait_ge(S("lru_q"), i)
                    tr = lb[(i - 1) % 2][0]
                    act.activation(tr, tr, ACT.Sqrt, scale=-0.25).then_inc(S("lru_root"), 1)
                if i < 8:
                    mod_act(act, 4 + i)

        def gelu_act(act):
            for f in range(4):
                emptied(act, ("pT", 0, 1, f))
            act.activation(ga, ga, ACT.Gelu_apprx_tanh).then_inc(S("gelu"), 1)

        def lru_conv_dve(v, step):
            for part in range(2):
                v.wait_ge(S("pad_evac" + str(part)), 2)
            for ct in range(4):
                emptied(v, ("pT", 0, 0, ct))
                conv_dve(v, step, uT[:, ct, :], xap[:, ct, :], lambda tap: cB[:, lw_col + 4 * tap + ct:lw_col + 4 * tap + ct + 1],
                         cB[:, cb_col + ct:cb_col + ct + 1]).then_inc(S("u_ready"), 1)

        def lru_dve(v, step):
            filled(v, ("pR", 0, 4, 2))
            v.wait_ge(S("u_ready"), 4)
            for i in range(9):
                if i < 8:
                    tr, ti, a, w = lb[i % 2]
                    v.wait_ge(S("lru_tanh"), i + 1)
                    step(v.tensor_tensor(w, a, a, ALU.mult))
                    v.scalar_tensor_tensor(out=tr, in0=w, scalar=1.0, in1=tr, op0=ALU.add, op1=ALU.mult)\
                        .then_inc(S("lru_q"), 1)
                    step(v.scalar_tensor_tensor(out=ti, in0=ti, scalar=1.0, in1=uT[:, i // 2, :], op0=ALU.add,
                                                op1=ALU.mult))
                if i >= 1:
                    j = i - 1
                    ct, d = j // 2, j % 2
                    tr, ti, a, w = lb[j % 2]
                    c8 = 4 * d + ct
                    v.wait_ge(S("lru_root"), j + 1)
                    step(v.tensor_tensor(ti, ti, tr, ALU.mult))
                    h = hfb[d]
                    r = slice(None, None, 1 if d == 0 else -1)
                    step(v.tensor_tensor_scan(h[:, 0:NS][:, r], a[:, 0:NS][:, r], ti[:, 0:NS][:, r],
                                              cB[:, st_col + c8:st_col + c8 + 1], ALU.mult, ALU.add))
                    v.tensor_tensor_scan(h[:, UP0:UW][:, r], a[:, UP0:UW][:, r], ti[:, UP0:UW][:, r], 0.0,
                                         ALU.mult, ALU.add).then_inc(S("lru_scan"), 1)
                    v.wait_ge(S("lru_scan"), j + 1)
                    e = UW - 1 if d == 0 else UP0
                    step(v.tensor_copy(stl[:, c8:c8 + 1], h[:, e:e + 1]))
                    if d == 1:
                        step(v.tensor_tensor(hT[:, ct, 0:NS], hfb[0][:, 0:NS], hfb[1][:, 0:NS], ALU.add))
                        step(v.tensor_tensor(hT[:, ct, NS:T], hfb[0][:, UP0:UW], hfb[1][:, UP0:UW], ALU.add))
                        if ct == 0:
                            v.wait_ge(S("gelu"), 1)
                        ins = v.tensor_tensor(hT[:, ct, :], hT[:, ct, :], ga[:, ct, :], ALU.mult)
                        ins.then_inc(S("y_first"), 1)
                    mod_dve(v, step, 4 + j)

        pscr = ar(19728, NT * 8, HD)
        oscr = ar(19728, 512)

        def rope_dve(v, step, x, nh, scr):
            cos = rope[:, :, 0:32].unsqueeze(2).broadcast_to((P, ST, nh, 32))
            sin = rope[:, :, 32:64].unsqueeze(2).broadcast_to((P, ST, nh, 32))
            x1, x2 = x[:, :, :, 0:32], x[:, :, :, 32:64]
            n = nh * 32
            for t in range(ST):
                a, b, c, d = (scr[:, (4 * (t % 2) + i) * n:(4 * (t % 2) + i + 1) * n]
                              .rearrange("p (h d) -> p h d", d=32) for i in range(4))
                v.tensor_tensor(a, x1[:, t], cos[:, t], ALU.mult)
                v.tensor_tensor(b, x2[:, t], sin[:, t], ALU.mult)
                v.tensor_tensor(c, x2[:, t], cos[:, t], ALU.mult)
                step(v.tensor_tensor(d, x1[:, t], sin[:, t], ALU.mult))
                v.tensor_tensor(x1[:, t], a, b, ALU.subtract)
                step(v.tensor_tensor(x2[:, t], c, d, ALU.add))

        qr = qkv[:, :, 0:512]
        kr = qkv[:, :, 512:1024]
        vr = qkv[:, :, 1024:1536]
        kT = ar(0, 4, 768)
        qT = ar(3072, 4, T)
        pb = [ar(5632 + 1280 * i, 2, T) for i in range(2)]
        aT = [ar(8192 + 640 * i, T) for i in range(2)]
        osb = qkv[:, :, 0:512]
        ITS = [(t, h) for t in range(NT) for h in range(4)]
        MOD_AT = {2 * j + 1: 12 + j for j in range(N_DIFF_MODS)}
        hn_count = [0]

        def hn_act(act, src, scr, eps_scale, ss):
            hn_count[0] += 1
            k = hn_count[0]
            act.activation(scr, src, ACT.Square).then_inc(S("hn_sq"), 1)
            act.wait_ge(S("hn_sum"), k)
            act.activation(ss, ss, ACT.Sqrt, scale=eps_scale, bias=1e-6).then_inc(S("hn_root"), 1)

        def hn_dve(v, step, k, x, scr, ss, nh, w, gain):
            v.wait_ge(S("hn_sq"), k)
            v.tensor_reduce(ss, scr, AX_X, ALU.add).then_inc(S("hn_sum"), 1)
            v.wait_ge(S("hn_root"), k)
            step(v.reciprocal(ss, ss))
            s4 = ss.rearrange("p (t h) -> p t h", h=nh).unsqueeze(3).broadcast_to((P, NT, nh, w))
            for t in range(NT):
                step(v.tensor_tensor(x[:, t], x[:, t], s4[:, t], ALU.mult))
                step(v.tensor_tensor(x[:, t], x[:, t], gain.unsqueeze(1).broadcast_to((P, nh, w)), ALU.mult))


        def o_square(act, x, scr):
            act.activation(scr, x, ACT.Square).then_inc(S("o_sq"), 1)

        def o_sum(v, m, scr, j):
            v.wait_ge(S("o_sq"), m)
            v.tensor_reduce(ssq[:, 4 * j:4 * j + 4], scr.rearrange("p (h d) -> p h d", d=P), AX_X, ALU.add)\
                .then_inc(S("o_sum"), 1)

        def o_root(act, m, ss):
            act.wait_ge(S("o_sum"), m)
            act.activation(ss, ss, ACT.Sqrt, scale=1.0 / P, bias=1e-6).then_inc(S("o_root"), 1)

        def o_apply(v, step, x, rs, gain, gate_rows=None):
            x4 = x.rearrange("p (h d) -> p h d", d=P)
            step(v.tensor_tensor(x4, x4, rs.unsqueeze(2).broadcast_to((P, 4, P)), ALU.mult))
            ins = v.tensor_tensor(x4, x4, gain.unsqueeze(1).broadcast_to((P, 4, P)), ALU.mult)
            if gate_rows is not None:
                step(ins)
                ins = v.tensor_tensor(x, x, gate_rows, ALU.mult)
            ins.then_inc(S("o_done"), 1)

        def diff_rows_act(act, j):
            for tp in range(3):
                emptied(act, ("pR", 0, 2 + j, tp))
            if j:
                act.wait_ge(S("dq_done"), 1)
            x = (qr, kr)[j].rearrange("p t (h d) -> p t h d", d=HD)
            hn_act(act, x, pscr.rearrange("p (t h) d -> p t h d", h=8), 1.0 / HD, ssq)

        def diff_act(act, step):
            act.wait_ge(S("y_first"), 4)
            for h in range(4):
                release(copy(act, kT[:, h, :], filled(act, ("kT", h))[:, 0:768]), ("kT", h))

            def exps(i):
                n = T if ITS[i][0] < ST else P
                for c in range(2):
                    act.wait_ge(S("d_max"), 2 * i + c + 1)
                    if i >= 2:
                        filled(act, ("daT", i - 2))
                    u = ("ds", i, c)
                    release(act.activation(pb[i % 2][:, c, 0:n], filled(act, u)[:, 0:n], ACT.Exp,
                                           bias=nmax(i, c), accum_out=psum_of(i, c)), u)

            def dy_read(t):
                u = ("dyT", t)
                release(copy(act, hT[:, 4:8, t * P:t * P + P],
                             filled(act, u)[:, 0:512].rearrange("p (h c) -> p h c", c=P)), u)

            exps(0)
            for i in range(len(ITS)):
                if i + 1 < len(ITS):
                    exps(i + 1)
                if i - 1 in MOD_AT:
                    mod_act(act, MOD_AT[i - 1])
                n = T if ITS[i][0] < ST else P
                u = ("daT", i)
                if i >= 2:
                    filled(act, ("do", i - 2))
                release(copy(act, aT[i % 2][:, 0:n], filled(act, u)[:, 0:n]), u)
                if i >= 5 and i % 4 == 1:
                    emptied(act, ("do", i - 2))
                    if i // 4 > 1:
                        act.wait_ge(S("o_sum"), i // 4 - 1)
                    o_square(act, osb[:, i // 4 - 1, :], oscr)
                if i == 17:
                    o_root(act, ST, ssq[:, 0:16])
            emptied(act, ("do", len(ITS) - 1))
            act.wait_ge(S("o_sum"), ST)
            o_square(act, osb[:, ST, :], oscr)
            o_root(act, NT, ssq[:, 16:20])
            for t in range(NT):
                dy_read(t)

        def diff_rows_dve(v, step, j):
            for tp in range(3):
                emptied(v, ("pR", 0, 2 + j, tp))
            v.wait_ge(S("late_here"), LATE_ALL)
            x = (qr, kr)[j].rearrange("p t (h d) -> p t h d", d=HD)
            hn_dve(v, step, 1 + j, x, pscr, ssq, 8, HD, (dqg, dkg)[j])
            mark(v).then_inc(S(("dq_done", "cache_k_ready")[j]), 1)
            rope_dve(v, step, x[:, 0:ST], 8, ar(7716, 2048))
            if j:
                mark(v).then_inc(S("qk_rows"), 1)

        def diff_dve(v, step):
            v.wait_ge(S("y_first"), 4)
            for tp in range(3):
                emptied(v, ("pR", 0, 4, tp))
            for h in range(4):
                release(v.tensor_copy(qT[:, h, :], filled(v, ("qT", h))[:, 0:T]), ("qT", h))

            def maxes(i, c):
                n = T if ITS[i][0] < ST else P
                if i >= 4:
                    emptied(v, ("ds", i - 4, 1))
                v.tensor_reduce(nmax(i, c), filled(v, ("ds", i, c))[:, 0:n], AX_X, ALU.max, negate=True)\
                    .then_inc(S("d_max"), 1)

            def combine(i):
                n = T if ITS[i][0] < ST else P
                emptied(v, ("ds", i, 0))
                emptied(v, ("ds", i, 1))
                step(v.reciprocal(rsum(i, 0, 2), psum_of(i, 0, 2)))
                step(v.scalar_tensor_tensor(out=ratio(i), in0=rsum(i, 1), scalar=nlam, in1=psum_of(i),
                                            op0=ALU.mult, op1=ALU.mult))
                v.scalar_tensor_tensor(out=pb[i % 2][:, 0, 0:n], in0=pb[i % 2][:, 1, 0:n], scalar=ratio(i),
                                       in1=pb[i % 2][:, 0, 0:n], op0=ALU.mult, op1=ALU.add).then_inc(S("d_comb"), 1)

            def rows_out(i):
                t, h = ITS[i]
                release(v.tensor_scalar(osb[:, t, h * P:h * P + P], filled(v, ("do", i))[:, 0:P], rsum(i), None,
                                        ALU.mult), ("do", i))

            maxes(0, 0)
            maxes(0, 1)
            for i in range(len(ITS)):
                if i + 1 < len(ITS):
                    maxes(i + 1, 0)
                if i - 2 in MOD_AT:
                    mod_dve(v, step, MOD_AT[i - 2])
                combine(i)
                if i + 1 < len(ITS):
                    maxes(i + 1, 1)
                if i >= 1:
                    rows_out(i - 1)
                if i >= 5 and i % 4 == 1:
                    o_sum(v, i // 4, oscr, i // 4 - 1)
                if i >= 18:
                    if i == 18:
                        v.wait_ge(S("o_root"), 1)
                        step(v.reciprocal(ssq[:, 0:16], ssq[:, 0:16]))
                    for t in (0, 1) if i == 18 else (2, 3):
                        o_apply(v, step, osb[:, t, :], ssq[:, 4 * t:4 * t + 4], dsg)
            rows_out(len(ITS) - 1)
            o_sum(v, NT, oscr, ST)
            v.wait_ge(S("o_root"), 2)
            step(v.reciprocal(ssq[:, 16:20], ssq[:, 16:20]))
            o_apply(v, step, osb[:, ST, :], ssq[:, 16:20], dsg)

        def diff_pe(pe):
            for tp in range(3):
                emptied(pe, ("pR", 0, 4, tp))
            pe.wait_ge(S("qk_rows"), 1)
            pe.wait_ge(S("late_here"), LATE_ALL)
            for h in range(4):
                u = ("kT", h)
                ps = take(pe, u)
                c = slice(h * P, h * P + P)
                pe.transpose(ps[:, 0:P], dk_c[:, c], ident)
                for t in range(NT):
                    last = pe.transpose(ps[:, (t + 1) * P:(t + 2) * P], kr[:, t, c], ident)
                finish(last, u)
                u = ("qT", h)
                ps = take(pe, u)
                for t in range(NT):
                    last = pe.transpose(ps[:, t * P:t * P + P], qr[:, t, c], ident)
                finish(last, u)
            for h in range(4):
                emptied(pe, ("kT", h))
                emptied(pe, ("qT", h))

            def scores(i, c):
                t, h = ITS[i]
                u = ("ds", i, c)
                ps = take(pe, u, c)
                q = qT[64 * c:64 * c + 64, h, t * P:t * P + P]
                k = kT[64 * c:64 * c + 64, h, :]
                if t < ST:
                    pe.matmul(ps[:, 0:512], q, k[:, 0:512], start=True, stop=True)
                    last = pe.matmul(ps[:, 512:T], q, k[:, 512:T], start=True, stop=True)
                else:
                    last = pe.matmul(ps[:, 0:P], q, k[:, T:768], start=True, stop=True)
                finish(last, u)

            def rows(i):
                t, h = ITS[i]
                nk = NT if t < ST else 1
                u = ("do", i)
                ps = take(pe, u, 3)
                emptied(pe, ("daT", i))
                for j in range(nk):
                    vals = vr[:, ST, h * P:h * P + P] if t == ST else \
                        dv_c[:, h * P:h * P + P] if j == 0 else vr[:, j - 1, h * P:h * P + P]
                    last = pe.matmul(ps[:, 0:P], aT[i % 2][:, j * P:j * P + P], vals, start=(j == 0), stop=(j == nk - 1))
                finish(last, u)

            def dy_turn(t):
                pe.wait_ge(S("o_done"), t + 1)
                u = ("dyT", t)
                ps = take(pe, u, t % 4)
                for h in range(4):
                    last = pe.transpose(ps[:, h * P:h * P + P], osb[:, t, h * P:h * P + P], ident)
                finish(last, u)

            scores(0, 0)
            scores(0, 1)
            for i, (t, h) in enumerate(ITS):
                if i + 1 < len(ITS):
                    scores(i + 1, 0)
                if i - 2 in MOD_AT:
                    mod_turn_pe(pe, MOD_AT[i - 2], 2)
                if i + 1 < len(ITS):
                    scores(i + 1, 1)
                if i - 1 in MOD_AT:
                    mod_rows_pe(pe, MOD_AT[i - 1], 2)
                if i >= 1:
                    rows(i - 1)
                pe.wait_ge(S("d_comb"), i + 1)
                u = ("daT", i)
                ps = take(pe, u, 2)
                for j in range(NT if t < ST else 1):
                    last = pe.transpose(ps[:, j * P:j * P + P], pb[i % 2][:, 0, j * P:j * P + P], ident)
                finish(last, u)
            rows(len(ITS) - 1)
            for t in range(NT):
                dy_turn(t)

        def layer0_outputs(g):
            g.wait_ge(S("cache_k_ready"), 1)
            g.dma_start(outs["new_cache_diff_k"].rearrange("a b t h c d -> t (a b h c d)"), kr[:, ST, :])\
                .then_inc(S("caches"), 16)
            for tp in range(3):
                emptied(g, ("pR", 0, 4, tp))
            g.dma_start(outs["new_cache_diff_v"].rearrange("a b t h d -> t (a b h d)"), vr[:, ST, :])\
                .then_inc(S("caches"), 16)
            g.wait_ge(S("y_first"), 4)
            with nc.allow_non_contiguous_dma(reason="a small state"):
                g.dma_start(outs["new_state_lru"][0, 0].rearrange("r (c p) -> p (r c)", p=P), stl)\
                    .then_inc(S("caches"), 16)

        def out_pe(pe, l):
            if l == 0:
                pe.wait_ge(S("y_first"), 4)
                for t in range(NT):
                    emptied(pe, ("dyT", t))
            else:
                layer1_ready(pe)
            for c in range(2):
                w = arrived(pe, ("out", l, c, 0))
                for f in range(4):
                    u = ("out", l, 4 * c + f)
                    ps = take(pe, u)
                    lhs = lambda k: w[:, k, f * P:f * P + P]
                    mmk(pe, ps[:, 0:NS], lhs, lambda k: hT[:, k, 0:NS])
                    finish(mmk(pe, ps[:, NS:T], lhs, lambda k: hT[:, k, NS:T]), u)
                chunk_last["out", l, c, 0] = u

        def add_gated(v, l, m, k, ps, u):
            a, b = seg[0]
            v.scalar_tensor_tensor(out=xT[:, k, a:b], in0=ps[:, a:b], scalar=modt[:, l, 8 * m + k, 0:1],
                                   in1=xT[:, k, a:b], op0=ALU.mult, op1=ALU.add).then_inc(S("x_half"), 1)
            a, b = seg[1]
            release(v.scalar_tensor_tensor(out=xT[:, k, a:b], in0=ps[:, a:b], scalar=modt[:, l, 8 * m + k, 1:2],
                                           in1=xT[:, k, a:b], op0=ALU.mult, op1=ALU.add), u)

        def residual_dve(v, step, l, kind):
            nl, nn = (l, 1) if kind == "out" else (l + 1, 0)
            for k in range(KD):
                u = (kind, l, k)
                add_gated(v, l, 2 if kind == "out" else 5, k, filled(v, u), u)
                if k >= 2 and kind == "out":
                    norm_add(v, nl, nn, k - 1)
            if kind == "out":
                norm_add(v, nl, nn, KD - 1)
            v.wait_ge(S("x_half"), 8 * (2 * l + (1 if kind == "out" else 2)))

        lg = ar(18700, NT, NE)
        affT = ar(18800, T)[0:NE, :]
        g16 = ar(19500, CAP)[0:NE, :]
        i16 = ar(19600, CAP)[0:NE, :].bitcast(U32)
        i16f = ar(19700, CAP)[0:NE, :]
        gateT = ar(19968, NE)[0:CAP, :]
        idxT = ar(19984, NE)[0:CAP, :].bitcast(U32)
        hrow = ar(12800, NT, D)
        rows_m = ar(12800, NT, D)
        xrow = ar(12800, NT, D)
        grow = ar(17920, 2, D)

        def route_pe(pe, l):
            late = range(12 + N_DIFF_MODS, 24) if l == 0 else []
            for i in late[:1]:
                mod_rows_pe(pe, i)
            u = ("logit", l)
            ps = take(pe, u)
            for k in range(KD):
                pe.wait_ge(S("h_ready"), 16 * (2 * l + 1) + 2 * k + 2)
                pe.matmul(ps[0:NE, 0:NS], wr[:, l, k, :], hT[:, k, 0:NS], start=(k == 0), stop=(k == KD - 1))
                last = pe.matmul(ps[0:NE, NS:T], wr[:, l, k, :], hT[:, k, NS:T], start=(k == 0), stop=(k == KD - 1))
            finish(last, u)
            for t in range(NT):
                u = ("hr", l, t)
                ps = take(pe, u)
                for k in range(KD):
                    last = pe.transpose(ps[:, k * P:k * P + P], hT[:, k, t * P:t * P + P], ident)
                finish(last, u)
                if t == 0:
                    emptied(pe, ("logit", l))
                    u = ("lrow", l)
                    ps = take(pe, u)
                    for j in range(NT):
                        last = pe.transpose(ps[:, NE * j:NE * j + NE], affT[:, j * P:j * P + P], ident[0:NE, 0:NE])
                    finish(last, u)
            pe.wait_ge(S("aff"), l + 1)
            u = ("affT", l)
            ps = take(pe, u)
            for t in range(NT):
                last = pe.transpose(ps[0:NE, t * P:t * P + P], lg[:, t, :], ident)
            finish(last, u)

            def residual_rows(tiles):
                for t in tiles:
                    u = ("xr", t)
                    ps = take(pe, u)
                    for k in range(KD):
                        last = pe.transpose(ps[:, k * P:k * P + P], xT[:, k, t * P:t * P + P], ident)
                    finish(last, u)

            if l == 0:
                mod_rows_pe(pe, late[1])
                mod_turn_pe(pe, late[0])
                mod_rows_pe(pe, late[2])
                mod_turn_pe(pe, late[1])
                mod_turn_pe(pe, late[2])
            else:
                pe.wait_ge(S("x_half"), 24)
                for k in range(4, KD):
                    emptied(pe, ("out", 1, k))
                residual_rows((0, 1, 2))
            pe.wait_ge(S("top"), l + 1)
            u = ("gi", l)
            ps = take(pe, u)
            pe.transpose(ps[0:CAP, 0:16], g16, ident[0:NE, 0:NE])
            finish(pe.transpose(ps[0:CAP, 16:32], i16f, ident[0:NE, 0:NE]), u)
            if l == 1:
                residual_rows((3, 4))

        def beside_first_pe(pe, l):
            if l == 0:
                mod_rows_pe(pe, 23, 1)
                return
            for g in range(2):
                u = ("grow", g)
                ps = take(pe, u, 1 + g)
                for k in range(KD):
                    col = modt[:, 1, 40 + k, g:g + 1].broadcast_to((P, P))
                    last = pe.matmul(ps[:, k * P:k * P + P], col, ident, start=True, stop=True)
                finish(last, u)

        def beside_first_act(act, l):
            if l == 0:
                mod_act(act, 23)
                return
            for g in range(2):
                u = ("grow", g)
                release(copy(act, grow[:, g, :], filled(act, u)), u)

        def route_act(act, step, l):
            for t in range(NT):
                u = ("hr", l, t)
                release(copy(act, hrow[:, t, :], filled(act, u)), u)
                if t == 0:
                    act.wait_ge(S("lg_sub"), l + 1)
                    act.activation(lg, lg, ACT.Exp).then_inc(S("lg_exp"), 1)
            if l == 0:
                for i in range(13 + N_DIFF_MODS, 23):
                    mod_act(act, i)
            if l == 1:
                act.wait_ge(S("h_stored"), 32)
                for t in range(NT):
                    u = ("xr", t)
                    release(copy(act, xrow[:, t, :], filled(act, u)), u)

        def route_dve(v, step, l):
            u = ("logit", l)
            release(v.tensor_copy(affT, filled(v, u)[0:NE, 0:T]), u)
            u = ("lrow", l)
            ps = filled(v, u)[:, 0:80].rearrange("p (t e) -> p t e", e=NE)
            step(v.tensor_reduce(smx[:, 0:5], ps, AX_X, ALU.max))
            release(v.tensor_tensor(lg, ps, smx[:, 0:5].unsqueeze(2).broadcast_to((P, NT, NE)), ALU.subtract), u)
            emptied(v, u)
            mark(v).then_inc(S("lg_sub"), 1)
            v.wait_ge(S("lg_exp"), l + 1)
            step(v.tensor_reduce(smx[:, 5:10], lg, AX_X, ALU.add))
            step(v.reciprocal(smx[:, 5:10], smx[:, 5:10]))
            v.tensor_tensor(lg, lg, smx[:, 5:10].unsqueeze(2).broadcast_to((P, NT, NE)), ALU.mult)\
                .then_inc(S("aff"), 1)
            u = ("affT", l)
            release(v.tensor_copy(affT, filled(v, u)[0:NE, 0:T]), u)
            emptied(v, u)
            late = range(12 + N_DIFF_MODS, 24) if l == 0 else []
            for (a, b), c0, rounds in ((seg[0], 0, CAPS // 8), (seg[1], CAPS, CAPP // 8)):
                for r in range(rounds):
                    c = slice(c0 + 8 * r, c0 + 8 * r + 8)
                    step(v.max(g16[:, c], affT[:, a:b]))
                    step(v.max_index(i16[:, c], g16[:, c], affT[:, a:b]))
                    step(v.match_replace(affT[:, a:b], g16[:, c], affT[:, a:b], -1.0))
                    if l == 0 and c0 == 0 and r in (2, 5):
                        mod_dve(v, step, late[r // 3])
            step(v.tensor_copy(i16f, i16))
            v.tensor_scalar(i16f[:, CAPS:CAP], i16f[:, CAPS:CAP], float(NS), None, ALU.add).then_inc(S("top"), 1)
            u = ("gi", l)
            ps = filled(v, u)
            step(v.tensor_copy(gateT, ps[0:CAP, 0:16]))
            release(v.tensor_copy(idxT, ps[0:CAP, 16:32]), u)
            for i in late[2:3]:
                mod_dve(v, step, i)

        def route_pool(g, l):
            for t in range(NT):
                emptied(g, ("hr", l, t))
            g.dma_start(DR["h", l].rearrange("(t p) d -> p t d", p=P), hrow).then_inc(S("h_stored"), 16)

        xe = [hflat[0:CAP, 1024 * i:1024 * i + 1024] for i in range(2)]
        ye = [hflat[0:CAP, 2048 + 1024 * i:3072 + 1024 * i] for i in range(2)]
        xeT = [ar(20000 + 640 * i, 2, 4 * CAP) for i in range(2)]
        hid = [ar(21280 + 320 * i, FT, CAP) for i in range(2)]
        slu = [hflat[:, 4096 + 80 * i:4176 + 80 * i] for i in range(2)]
        PER = (1, 2, 2, 1)

        def moe_pe(pe, l):
            while units.next % 4:
                u = ("skip", l, units.next)
                take(pe, u)
                units.uses[units.of[u][0]] -= 1
            base = list(units.uses)
            moe_base[l] = base

            def take_at(pair, i, n):
                pe.wait_ge(pair_free[pair], i * PER[pair] + (base[pair] + n))

            def gather_T(i, par):
                pe.wait_ge(S(f"gathered{par}"), (i - par) * 8 + (16 + 128 * l))
                take_at(0, i, 0)
                ps = PSUM[:, 0, :]
                for k in range(KD):
                    o = 512 * (k // 4) + CAP * (k % 4)
                    last = pe.transpose(ps[:, o:o + CAP], xe[par][:, k * P:k * P + P], ident[0:CAP, 0:CAP])
                last.then_inc(pair_full[0], 1)

            def expert(i, par, nxt):
                s = 3 - 3 * par
                w1, w3 = (slots[s + j].rearrange("p (k n) -> p k n", n=FF) for j in range(2))
                w2 = slots[s + 2].rearrange("p (k n) -> p k n", n=D)
                pe.wait_ge(pair_free[0], i + (base[0] + 1))
                for j in range(2):
                    pe.wait_ge(w_here[s + j], (i - par) * 8 + 16 * (slot_of["exp", l, s + j] + 1))
                for f in range(FT):
                    pair = 1 + f % 2
                    take_at(pair, i, f // 2)
                    ps = PSUM[:, pair, :]
                    for w, o in ((w1, 0), (w3, 512)):
                        last = mmk(pe, ps[:, o:o + CAP], lambda k: w[:, k, f * P:f * P + P],
                                   lambda k: xeT[par][:, k // 4, CAP * (k % 4):CAP * (k % 4) + CAP])
                    last.then_inc(pair_full[pair], 1)
                if nxt is not None:
                    gather_T(nxt, 1 - par)
                pe.wait_ge(w_here[s + 2], (i - par) * 8 + 16 * (slot_of["exp", l, s + 2] + 1))
                take_at(3, i, 0)
                for f0, f1 in ((0, FT - 1), (FT - 1, FT)):
                    if f0 == 0:
                        pe.wait_ge(pair_free[1], i * 2 + (base[1] + 2))
                        pe.wait_ge(pair_free[2], i * 2 + (base[2] + 1))
                    else:
                        pe.wait_ge(pair_free[2], i * 2 + (base[2] + 2))
                    for half in range(2):
                        for f in range(f0, f1):
                            last = pe.matmul(PSUM[0:CAP, 3, 512 * half:512 * half + 512], hid[par][:, f, :],
                                             w2[:, f, 512 * half:512 * half + 512], start=(f == 0), stop=(f == FT - 1))
                last.then_inc(pair_full[3], 1)

            gather_T(0, 0)
            beside_first_pe(pe, l)
            base[1:] = units.uses[1:]
            with pe.Fori(0, NE // 2 - 1) as i:
                expert(i * 2, 0, i * 2 + 1)
                expert(i * 2 + 1, 1, i * 2 + 2)
            expert(NE - 2, 0, NE - 1)
            expert(NE - 1, 1, None)
            for pair in range(4):
                units.uses[pair] = base[pair] + NE * PER[pair]

        def moe_act_run(act, l):
            base = moe_base[l]

            def xt(i, par):
                act.wait_ge(pair_full[0], i + (base[0] + 1))
                ps = PSUM[:, 0, :].rearrange("p (a b) -> p a b", a=2)[:, :, 0:4 * CAP]
                act.activation(xeT[par], ps, ACT.Copy).then_inc(pair_free[0], 1)

            def expert(i, par, nxt):
                for f in range(FT):
                    pair = 1 + f % 2
                    act.wait_ge(pair_full[pair], i * 2 + (base[pair] + f // 2 + 1))
                    act.wait_ge(pair_free[pair], i * 2 + (base[pair] + f // 2))
                    act.activation(slu[f % 2], PSUM[:, pair, 0:CAP], ACT.Silu).then_inc(S("silu"), 1)
                if nxt is not None:
                    xt(nxt, 1 - par)
                act.wait_ge(pair_full[3], i + (base[3] + 1))
                act.wait_ge(S(f"y_room{par}"), (i - par) * 8 + (16 + 128 * l))
                act.activation(ye[par][:, 0:512], PSUM[0:CAP, 3, 0:512], ACT.Copy, scale=gateT[:, bass.ds(i, 1)])\
                    .then_inc(S("y_low"), 1)

            emptied(act, ("gi", l))
            xt(0, 0)
            beside_first_act(act, l)
            with act.Fori(0, NE // 2 - 1) as i:
                expert(i * 2, 0, i * 2 + 1)
                expert(i * 2 + 1, 1, i * 2 + 2)
            expert(NE - 2, 0, NE - 1)
            expert(NE - 1, 1, None)

        def moe_dve(v, l):
            base = moe_base[l]

            def expert(i, par):
                for f in range(FT):
                    pair = 1 + f % 2
                    v.wait_ge(S("silu"), i * 4 + (64 * l + f + 1))
                    v.tensor_tensor(hid[par][:, f, :], slu[f % 2], PSUM[:, pair, 512:512 + CAP], ALU.mult)\
                        .then_inc(pair_free[pair], 1)
                v.wait_ge(pair_full[3], i + (base[3] + 1))
                v.wait_ge(S("y_low"), i + (16 * l + 1))
                v.tensor_scalar(ye[par][:, 512:1024], PSUM[0:CAP, 3, 512:1024], gateT[:, bass.ds(i, 1)], None,
                                ALU.mult).then_inc(pair_free[3], 1)

            emptied(v, ("gi", l))
            with v.Fori(0, NE // 2) as i:
                expert(i * 2, 0)
                expert(i * 2 + 1, 1)

        def moe_pool(g, l):
            base = moe_base[l]
            emptied(g, ("gi", l))
            g.wait_ge(S("h_stored"), 16 * (l + 1))
            off = lambda e: bass.IndirectOffsetOnAxis(ap=idxT[:, e:e + 1], axis=0)

            def gather(e):
                if e >= 2:
                    g.wait_ge(pair_full[0], base[0] + e - 1)
                g.indirect_dma_start(xe[e % 2], None, DR["h", l], off(e)).then_inc(S(f"gathered{e % 2}"), 16)

            gather(0)
            for e in range(NE):
                if e + 1 < NE:
                    gather(e + 1)
                g.wait_ge(pair_free[3], base[3] + e + 1)
                if e:
                    g.wait_ge(S(f"y_room{(e - 1) % 2}"), 16 * ((e - 1) // 2 + 1) + 16 + 128 * l)
                g.indirect_dma_start(DR["m", l], off(e), ye[e % 2], None, compute_op=ALU.add)\
                    .then_inc(S(f"y_room{e % 2}"), 16)

        def load_stream(sp):
            for c, s, prev in loads:
                if c[0] != "experts":
                    if prev is not None:
                        if prev[0] == "experts":
                            l = prev[1]
                            pair, n = (2, 2 * NE) if s < 2 else (3, NE)
                            sp.wait_ge(pair_full[pair], moe_base[l][pair] + n)
                        else:
                            filled(sp, chunk_last[prev])
                    if c == chunks[0][1]:
                        sp.wait_ge(S("x_here"), 16 * NT)
                    if c == chunks[1][1]:
                        sp.wait_ge(S("m_quarter3"), 16)
                    src, n = chunk_src(c)
                    sp.dma_start(chunk(c), src.rearrange("(k p) n -> p k n", p=P)).then_inc(w_here[s], 16)
                    if c == wouts[c[1]][1]:
                        filled(sp, ("dyT", ST) if c[1] == 0 else ("cyT", 3))
                        sp.wait_ge(S("caches"), (48, 96)[c[1]])
                        for j in range(3):
                            load_expert(sp, c[1], 0, 0, j, False)
                else:
                    experts_stream(sp, c[1], prev)

        def load_expert(sp, l, i, par, j, wait):
            base = moe_base[l]
            s = 3 - 3 * par + j
            if wait:
                pair = 3 if j == 2 else 2
                sp.wait_ge(pair_full[pair], i * PER[pair] + (base[pair] - PER[pair]))
            w = (W1, W3, W2)[j][l]
            kk = FT if j == 2 else KD
            n = D if j == 2 else FF
            src = w[:, bass.ds(i * kk, kk), :]
            sp.dma_start(slots[s].rearrange("p (k n) -> p k n", n=n), src).then_inc(w_here[s], 16)

        def experts_stream(sp, l, prev):
            load = lambda *a: load_expert(sp, l, *a)
            sp.wait_ge(S("gathered0"), 16 + 128 * l)
            for j in (1, 2, 0):
                filled(sp, chunk_last[prev[j]])
                load(1, 1, j, False)
            with sp.Fori(1, NE // 2) as i:
                for par in range(2):
                    for j in range(3):
                        load(i * 2 + par, par, j, True)

        def gather_sum_act(act, l):
            for par in range(2):
                act.wait_ge(S(f"y_room{par}"), 16 + 128 + 128 * l)
            for pair in range(4):
                act.wait_ge(pair_free[pair], moe_base[l][pair] + NE * PER[pair])
            for q in range(4):
                act.dma_start(rows_m[:, :, 256 * q:256 * q + 256],
                              DR["m", l][:, 256 * q:256 * q + 256].rearrange("(t p) d -> p t d", p=P))\
                    .then_inc(S(f"m_quarter{q}"), 16)

        def sum_pe(pe, l):
            mod_turn_pe(pe, 23, 0)
            un = ("nrm", 1, 0)
            acc = take(pe, un, 3)
            for k in range(KD + 3):
                if k < KD:
                    if k % 2 == 0:
                        pe.wait_ge(S(f"m_quarter{k // 2}"), 16)
                    u = ("ms", l, k)
                    ps = take(pe, u, k % 3)
                    for t in range(NT):
                        last = pe.transpose(ps[:, t * P:t * P + P], rows_m[:, t, k * P:k * P + P], ident)
                    finish(last, u)
                j = k - 3
                if j >= 0:
                    pe.wait_ge(S("sq"), 16 + j + 1)
                    for a, b in seg:
                        last = pe.matmul(acc[:, a:b], ones, sq_all[:, j, a:b], start=(j == 0), stop=(j == KD - 1))
            finish(last, un)

        mrow_out = xT[:, :, :].rearrange("p k t -> p (k t)").rearrange("p (t d) -> p t d", d=D)
        Y_TILES = {"dve": (0, 1, 4), "pool": (2, 3)}

        def y_load(act):
            for par in range(2):
                act.wait_ge(S(f"y_room{par}"), 16 + 128 + 128)
            for t in (0, 2, 1, 3, 4):
                act.dma_start(mrow_out[:, t, :], DR["m", 1][t * P:t * P + P, :]).then_inc(S(f"m_tile{t}"), 16)

        def y_rows(eng, step, tiles):
            for g in range(2):
                emptied(eng, ("grow", g))
            for t in tiles:
                eng.wait_ge(S(f"m_tile{t}"), 16)
                m = mrow_out[:, t, :]
                step(eng.tensor_tensor(m, m, grow[:, 0 if t < ST else 1, :], ALU.mult))
                eng.tensor_tensor(xrow[:, t, :], xrow[:, t, :], m, ALU.add).then_inc(S(f"y_tile{t}"), 1)

        def store_sp(sp, n_out):
            for t in (0, 2, 1, 3, 4):
                sp.wait_ge(S(f"y_tile{t}"), 1)
                dst = outs["y_sample"][0, t * P:t * P + P, :] if t < ST else outs["y_prompt"][0]
                sp.dma_start(dst, xrow[:, t, :]).then_inc(S("outputs"), 16)
            sp.wait_ge(S("outputs"), 16 * NT)
            sp.wait_ge(S("caches"), 16 * n_out)

        pad = ar(0, 12, PADW)
        gate = ar(7752, NT, 512)
        z2 = ar(10312, NT, 784)
        zq = z2[:, :, 16:528].rearrange("p t (h d) -> p t h d", d=HD)
        zk = z2[:, :, 528:656].rearrange("p t (h d) -> p t h d", d=HD)
        gqT = ar(14232, 4, T)
        gkT = ar(16792, 2, 768)
        gp = [ar(18328 + 640 * i, T) for i in range(2)]
        gaT = [ar(19608 + 640 * i, T) for i in range(2)]
        gscr = ar(18328, NT * 8, HD)
        kdup = ar(20888, NT, 256)
        cdup = ar(22168, 256)
        GI = [(t, h) for t in range(NT) for h in range(8)]
        TAPS = [(ct, tap) for ct in range(12) for tap in range(4)]
        cv = [hflat[:, UW * i:UW * i + UW] for i in range(3)]
        beta = sm[:, 256:296]
        gdec = sm[:, 296:336]
        gsm = sm[:, 336:496]
        eG = sm[:, 496:536]
        eGL = sm[:, 536:576]
        bG = sm[:, 576:616]
        dx, de, dz, dz2, do_ = (ar(22700 + 40 * i, 40) for i in range(5))
        t8 = lambda x: x.rearrange("p (t q) -> p t q", q=8)

        def gqa_rows_act(act, step, j):
            if j == 0:
                for c in (4, 5):
                    for tp in range(3):
                        emptied(act, ("pR", 1, c, tp))
                act.activation(t8(beta), z2[:, :, 0:8], ACT.Tanh, scale=0.5).then_inc(S("dl_tanh"), 1)
                act.activation(anl, alog, ACT.Exp).then_inc(S("dl_tanh"), 1)
                act.wait_ge(S("dl_x"), 1)
                softplus_act(act, step, dx, de).then_inc(S("sp_exp"), 1)
            elif j == 1:
                hn_act(act, zq, gscr.rearrange("p (t h) d -> p t h d", h=8), 1.0 / HD, ssq)
            else:
                act.wait_ge(S("gq_done"), 1)
                hn_act(act, zk, gscr[:, 0:10, :].rearrange("p (t h) d -> p t h d", h=2), 1.0 / HD, ssq[:, 0:10])

        def gqa_act(act, step):
            for g in range(4):
                release(copy(act, gqT[:, g, :], filled(act, ("gqT", g))[:, 0:T]), ("gqT", g))

            def exps(i):
                n = T if GI[i][0] < ST else P
                act.wait_ge(S("g_max"), i + 1)
                if i >= 2:
                    filled(act, ("gaT", i - 2))
                if i >= 4:
                    act.wait_ge(S("g_norm"), i - 3)
                u = ("gs", i)
                release(act.activation(gp[i % 2][:, 0:n], filled(act, u)[:, 0:n], ACT.Exp, bias=nmax(i),
                                       accum_out=psum_of(i)), u)

            def turned(i):
                n = T if GI[i][0] < ST else P
                if i >= 2:
                    filled(act, ("go", i - 2))
                release(copy(act, gaT[i % 2][:, 0:n], filled(act, ("gaT", i))[:, 0:n]), ("gaT", i))

            for i in range(-2, len(GI)):
                if i + 2 < len(GI):
                    exps(i + 2)
                if 0 <= i + 1 < len(GI):
                    turned(i + 1)

        def decay_dve(v, step):
            for c in (4, 5):
                for tp in range(3):
                    emptied(v, ("pR", 1, c, tp))
            v.tensor_tensor(t8(dx), z2[:, :, 8:16], dtb.unsqueeze(1).broadcast_to((P, NT, 8)), ALU.add)\
                .then_inc(S("dl_x"), 1)
            v.wait_ge(S("dl_x"), 1)
            v.wait_ge(S("dl_tanh"), 2)
            step(v.tensor_scalar(beta, beta, 0.5, 0.5, ALU.mult, ALU.add))
            v.wait_ge(S("sp_exp"), 2)
            softplus_dve(v, step, dx, de, dz, dz2, do_)
            step(v.scalar_tensor_tensor(out=t8(gdec), in0=t8(do_), scalar=-1.0,
                                        in1=anl.unsqueeze(1).broadcast_to((P, NT, 8)), op0=ALU.mult, op1=ALU.mult))

        def gqa_rows_dve(v, step, j):
            rs = ar(20888, 2048)
            if j == 1:
                hn_dve(v, step, 3, zq, gscr, ssq, 8, HD, gqg)
                mark(v).then_inc(S("gq_done"), 1)
                rope_dve(v, step, zq[:, 0:ST], 8, rs)
                return
            hn_dve(v, step, 4, zk, gscr[:, 0:10, :], ssq[:, 0:10], 2, HD, gkg)
            mark(v).then_inc(S("cache_k_ready"), 1)
            rope_dve(v, step, zk[:, 0:ST], 2, rs)
            for r in range(2):
                step(v.tensor_copy(kdup.rearrange("p t (n r d) -> p t n r d", n=2, r=2)[:, :, :, r, :], zk))
                step(v.tensor_copy(cdup.rearrange("p (n r d) -> p n r d", n=2, r=2)[:, :, r, :],
                                   gk_c[:, :].rearrange("p (n d) -> p n d", n=2)))
            mark(v).then_inc(S("qk_rows"), 1)

        def gqa_dve(v, step):
            filled(v, ("pR", 1, 3, 2))
            v.wait_ge(S("pad_evac0"), 8)
            v.wait_ge(S("pad_evac1"), 8)
            for c in range(3):
                for f in range(4):
                    emptied(v, ("pT", 1, c, f))
            for n in range(2):
                release(v.tensor_copy(gkT[:, n, :], filled(v, ("gkT", n))[:, 0:768]), ("gkT", n))

            def maxes(i):
                n = T if GI[i][0] < ST else P
                if i >= 4:
                    emptied(v, ("gs", i - 4))
                v.tensor_reduce(nmax(i), filled(v, ("gs", i))[:, 0:n], AX_X, ALU.max, negate=True)\
                    .then_inc(S("g_max"), 1)

            def scaled(i):
                emptied(v, ("gs", i))
                n = T if GI[i][0] < ST else P
                step(v.reciprocal(rsum(i), psum_of(i)))
                v.tensor_scalar(gp[i % 2][:, 0:n], gp[i % 2][:, 0:n], rsum(i), None, ALU.mult)\
                    .then_inc(S("g_norm"), 1)

            def result(i):
                t, h = GI[i]
                r = slice(64 * (h % 2), 64 * (h % 2) + 64)
                release(v.tensor_copy(hT[r, 4 + h // 2, t * P:t * P + P], filled(v, ("go", i))[r, 0:P]), ("go", i))

            for i in range(-2, len(GI)):
                if 0 <= i + 1 < len(GI):
                    scaled(i + 1)
                if i + 2 < len(GI):
                    maxes(i + 2)
                for ct, tap in TAPS[(i + 2) * len(TAPS) // 42:(i + 3) * len(TAPS) // 42]:
                    w = cB[:, dw_col + 12 * tap + ct:dw_col + 12 * tap + ct + 1]
                    n_tap = 4 * ct + tap
                    if n_tap:
                        v.wait_ge(S("cv_tap"), n_tap)
                    c, x = cv[ct % 2], pad[:, ct, tap:tap + UW]
                    if tap == 0:
                        v.tensor_scalar(c, x, w, None, ALU.mult).then_inc(S("cv_tap"), 1)
                    else:
                        v.scalar_tensor_tensor(out=c if tap < 3 else pad[:, ct, 0:UW], in0=x, scalar=w, in1=c,
                                               op0=ALU.mult, op1=ALU.add).then_inc(S("cv_tap"), 1)
                if i >= 0:
                    result(i)

        def gqa_pe(pe):
            pe.wait_ge(S("qk_rows"), 2)
            for g in range(4):
                u = ("gqT", g)
                ps = take(pe, u)
                for t in range(NT):
                    last = pe.transpose(ps[:, t * P:t * P + P], z2[:, t, 16 + g * P:16 + g * P + P], ident)
                finish(last, u)
            for n in range(2):
                u = ("gkT", n)
                ps = take(pe, u)
                pe.transpose(ps[:, 0:P], cdup[:, n * P:n * P + P], ident)
                for t in range(NT):
                    last = pe.transpose(ps[:, (t + 1) * P:(t + 2) * P], kdup[:, t, n * P:n * P + P], ident)
                finish(last, u)
            for g in range(4):
                emptied(pe, ("gqT", g))
            emptied(pe, ("gkT", 0))
            emptied(pe, ("gkT", 1))

            def scores(i):
                t, h = GI[i]
                r = slice(64 * (h % 2), 64 * (h % 2) + 64)
                u = ("gs", i)
                ps = take(pe, u, i % 2)
                q = gqT[r, h // 2, t * P:t * P + P]
                k = gkT[r, h // 4, :]
                if t < ST:
                    pe.matmul(ps[:, 0:512], q, k[:, 0:512], start=True, stop=True)
                    last = pe.matmul(ps[:, 512:T], q, k[:, 512:T], start=True, stop=True)
                else:
                    last = pe.matmul(ps[:, 0:P], q, k[:, T:768], start=True, stop=True)
                finish(last, u)

            def turn(i):
                pe.wait_ge(S("g_norm"), i + 1)
                u = ("gaT", i)
                ps = take(pe, u, 2)
                for j in range(NT if GI[i][0] < ST else 1):
                    last = pe.transpose(ps[:, j * P:j * P + P], gp[i % 2][:, j * P:j * P + P], ident)
                finish(last, u)

            def rows(i):
                t, h = GI[i]
                nk = NT if t < ST else 1
                r = slice(64 * (h % 2), 64 * (h % 2) + 64)
                u = ("go", i)
                ps = take(pe, u, 3)
                emptied(pe, ("gaT", i))
                o = 64 * (h // 4)
                for j in range(nk):
                    vals = z2[:, ST, 656 + o:720 + o] if t == ST else \
                        gv_c[:, o:o + HD] if j == 0 else z2[:, j - 1, 656 + o:720 + o]
                    last = pe.matmul(ps[r, 0:P], vals, gaT[i % 2][:, j * P:j * P + P], start=(j == 0),
                                     stop=(j == nk - 1))
                finish(last, u)

            for i in range(-2, len(GI)):
                if i + 2 < len(GI):
                    scores(i + 2)
                if 0 <= i + 1 < len(GI):
                    turn(i + 1)
                if i >= 0:
                    rows(i)
        dq, dk, dv = ar(10312, NT, 512), ar(12872, NT, 512), ar(0, NT, 512)
        dqkv = (dq, dk, dv)
        oacc = ar(15432, NT, 512)
        dscr2 = ar(18040, NT * 4, P)
        dbase = (18040, 2560)
        KT_U, QT_W, DA_KB, DB_QK, VB_QE, AM_, X_, XT_, WT_VN, QD_ = range(10)
        heads = lambda x: x.rearrange("p (h c) -> p h c", c=P)
        slot = lambda d, i, n=1: ar(dbase[d] + 512 * i, 4 * n, P)
        odd = lambda d, i, n=1: heads(ring[:, 2, 2048 * d + 512 * i:2048 * d + 512 * (i + n)])
        buf = lambda step_n, d, i, n=1: (odd, slot)[step_n % 2](d, i, n)
        KX = [heads(hflat[:, 1024 + 512 * d:1536 + 512 * d]) for d in range(2)]
        sdec = [heads(hflat[:, 512 * d:512 * d + 512]) for d in range(2)]
        dscr3 = hflat[:, 2048:2560]
        minus_ones = ar(23160, P)
        DONE = {2: (2, 1), 3: (3, 0), 4: (4,)}
        tile_of = lambda n, d: 4 if n == 4 else n if d == 0 else 3 - n
        chunk_at = lambda ci, d: ci if d == 0 else 1 - ci
        DIRS = "fb"

        def over_heads(x):
            return x.unsqueeze(1).broadcast_to((P, 4, P))

        def per_head(x, t, d):
            return x[:, 8 * t + 4 * d:8 * t + 4 * d + 4].unsqueeze(2).broadcast_to((P, 4, P))

        def conv_pe(pe):
            for ct in range(12):
                pe.wait_ge(S("cv_silu"), ct + 1)
                u = ("cvT", ct)
                ps = take(pe, u)
                c = pad[:, ct, 0:UW]
                for t in range(NT):
                    o = t * P if t < ST else UP0
                    last = pe.transpose(ps[:, t * P:t * P + P], c[:, o:o + P], ident)
                finish(last, u)

        def conv_read(eng, ct):
            u = ("cvT", ct)
            filled(eng, ("go", len(GI) - 1))
            eng.wait_ge(S("caches"), 80)
            dst = dqkv[ct // 4][:, :, (ct % 4) * P:(ct % 4) * P + P]
            release(copy(eng, dst, filled(eng, u)[:, 0:T].rearrange("p (t c) -> p t c", c=P)), u)

        def heads4(x):
            return x.rearrange("p t (h d) -> p t h d", d=P)

        def dec_pe(pe, n):
            for d in range(2):
                pe.wait_ge(S("dl_diag"), 2 * n + d + 1)
                u = ("dec", n, d)
                ps = take(pe, u, 2 + d)
                diag = buf(n, d, DA_KB)
                pe.matmul(ps[:, 0:512], ones, diag, start=True, stop=False)
                for h in range(4):
                    last = pe.matmul(ps[:, h * P:h * P + P], diag[:, h, :], minus_ones, start=False, stop=(h == 3))
                finish(last, u)

        def decay_pe(pe):
            pe.wait_ge(S("dl_g"), 1)
            ps = take(pe, "G")
            gv = gdec.rearrange("p (t d h) -> p t d h", d=2, h=4)
            pv = ps[:, 0:40].rearrange("p (t d h) -> p t d h", d=2, h=4)
            for d in range(2):
                pe.matmul(pv[:, :, d, :], C[("up_one", "lo_one")[d]], gv[:, :, d, :], start=True, stop=True)
            pe.matmul(ps[:, 40:80], C["block"], gdec, start=True, stop=True)
            for c in range(2):
                last = pe.matmul(ps[:, 80 + 512 * c:120 + 512 * c], ones[64 * c:64 * c + 64, :], gdec[64 * c:64 * c + 64, :],
                                 start=True, stop=True)
            finish(last, "G")
            dec_pe(pe, 0)

        def delta_pe(pe):
            conv_pe(pe)
            pe.wait_ge(S("dn_rows"), 1)

            def kq(n):
                pe.wait_ge(S("dn_rows"), min(n, 1) + 1)
                for d in range(2):
                    t = tile_of(n, d)
                    u = ("kq", n, d)
                    ps = take(pe, u, 2 + d)
                    for h in range(4):
                        pe.transpose(ps[:, h * P:h * P + P], dk[:, t, h * P:h * P + P], ident)
                        last = pe.transpose(ps[:, 512 + h * P:640 + h * P], dq[:, t, h * P:h * P + P], ident)
                    finish(last, u)

            def kk(n):
                for d in range(2):
                    u = ("kk", n, d)
                    emptied(pe, ("kq", n, d))
                    ps = take(pe, u, 2 + d)
                    for h in range(4):
                        k = buf(n, d, KT_U)[:, h, :]
                        pe.matmul(ps[:, h * P:h * P + P], k, k, start=True, stop=True)
                        last = pe.matmul(ps[:, 512 + h * P:640 + h * P], k, buf(n, d, QT_W)[:, h, :], start=True,
                                         stop=True)
                    finish(last, u)

            def turn4(u, src, pair):
                ps = take(pe, u, pair)
                for h in range(4):
                    last = pe.transpose(ps[:, h * P:h * P + P], src[:, h, :], ident)
                finish(last, u)

            def qd(n):
                for d in range(2):
                    pe.wait_ge(S("dl_qd"), 2 * n + d + 1)
                    turn4(("qd", n, d), slot(d, VB_QE), 2 + d)

            def am(n):
                for d in range(2):
                    pe.wait_ge(S(f"dl_am{d}"), 6 * n + 1)
                    turn4(("am", n, d), slot(d, AM_), d)

            kq(0)
            kk(0)
            am(0)
            for n in range(5):
                for s in range(1, 6):
                    for d in range(2):
                        pe.wait_ge(S(f"dl_am{d}"), 6 * n + s + 1)
                        if s == 1:
                            pe.wait_ge(S(f"dl_x0{d}"), n + 1)
                        else:
                            emptied(pe, ("x", n, d, s - 1))
                        u = ("w", n, d, s)
                        ps = take(pe, u, d)
                        for h in range(4):
                            last = pe.matmul(ps[:, h * P:h * P + P], slot(d, AM_)[:, h, :], slot(d, XT_)[:, h, :],
                                             start=True, stop=True)
                        finish(last, u)
                    if n < 4 and s == 1:
                        kq(n + 1)
                    if n < 4 and s == 2:
                        dec_pe(pe, n + 1)
                    if s == 3:
                        qd(n)
                    if n < 4 and s == 4:
                        kk(n + 1)
                    for d in range(2):
                        emptied(pe, ("w", n, d, s))
                        u = ("x", n, d, s)
                        ps = take(pe, u, d)
                        for h in range(4):
                            if s < 5:
                                pe.matmul(ps[:, h * P:h * P + P], slot(d, WT_VN)[:, h, :], slot(d, X_)[:, h, :],
                                          start=True, stop=True)
                            last = pe.matmul(ps[:, 512 + h * P:640 + h * P], slot(d, X_)[:, h, :],
                                             slot(d, WT_VN)[:, h, :], start=True, stop=True)
                        finish(last, u)
                for d in range(2):
                    emptied(pe, ("x", n, d, 5))
                    pe.wait_ge(S(f"dl_kv{d}"), n + 1)
                    u = ("wu", n, d)
                    ps = take(pe, u, 2 + d)
                    for h in range(4):
                        xt = slot(d, XT_)[:, h, :]
                        pe.matmul(ps[:, h * P:h * P + P], xt, slot(d, VB_QE)[:, h, :], start=True, stop=True)
                        last = pe.matmul(ps[:, 512 + h * P:640 + h * P], buf(n, d, DA_KB)[:, h, :], xt,
                                         start=True, stop=True)
                    finish(last, u)
                for ci in range(2):
                    for d in range(2):
                        c = chunk_at(ci, d)
                        r = slice(64 * c, 64 * c + 64)
                        if ci == 0:
                            emptied(pe, ("wu", n, d))
                            if n == 4:
                                pe.wait_ge(S("dl_zero"), 2)
                            elif n:
                                emptied(pe, ("os", n - 1, d, 1))
                        else:
                            emptied(pe, ("os", n, d, 0))
                        u = ("vs", n, d, ci)
                        ps = take(pe, u, d)
                        for h in range(4):
                            last = pe.matmul(ps[r, h * P:h * P + P], buf(n, d, QT_W)[:, h, r], sdel[:, 4 * d + h, :],
                                             start=True, stop=True)
                        finish(last, u)
                    if n < 4 and ci == 1:
                        am(n + 1)
                    for d in range(2):
                        c = chunk_at(ci, d)
                        r = slice(64 * c, 64 * c + 64)
                        emptied(pe, ("qd", n, d))
                        ps = take(pe, ("os", n, d, ci), 2 + d)
                        for h in range(4):
                            pe.matmul(ps[r, h * P:h * P + P], slot(d, QD_)[:, h, r], sdel[:, 4 * d + h, :],
                                      start=(h == 0), stop=False)
                    for d in range(2):
                        c = chunk_at(ci, d)
                        r = slice(64 * c, 64 * c + 64)
                        emptied(pe, ("vs", n, d, ci))
                        pe.wait_ge(S("dl_kx"), 2 * n + d + 1)
                        u = ("os", n, d, ci)
                        ps = PSUM[:, units.of[u][0], :]
                        for h in range(4):
                            pe.matmul(ps[r, h * P:h * P + P], buf(n, d, DB_QK)[r, h, r], slot(d, WT_VN)[r, h, :],
                                      start=False, stop=(h == 3))
                        for h in range(4):
                            last = pe.matmul(ps[:, 512 + h * P:640 + h * P], KX[d][r, h, :],
                                             slot(d, WT_VN)[r, h, :], start=True, stop=True)
                        finish(last, u)
            pe.wait_ge(S("o_done"), 10)
            for b in range(4):
                u = ("cyT", b)
                ps = take(pe, u)
                for t in range(NT):
                    last = pe.transpose(ps[:, t * P:t * P + P], oacc[:, t, b * P:b * P + P], ident)
                finish(last, u)

        qsq, ksq = ar(18040, NT * 4, P), ar(2560, NT * 4, P)
        heads5 = lambda x: x.rearrange("p (t h) d -> p t h d", h=4)

        def decay_exp(act, n):
            for d in range(2):
                emptied(act, ("dec", n, d))
                act.activation(buf(n, d, DA_KB, 2), buf(n, d, DA_KB, 2), ACT.Exp).then_inc(S("dl_exp"), 1)

        def decay_act(act):
            act.wait_ge(S("dl_gsm"), 1)
            act.activation(eG, gsm[:, 0:40], ACT.Exp).then_inc(S("dl_eg"), 1)
            act.activation(eGL, eGL, ACT.Exp).then_inc(S("dl_eg"), 1)
            act.activation(gsm[:, 80:160], gsm[:, 80:160], ACT.Exp).then_inc(S("dl_eg"), 1)
            decay_exp(act, 0)

        def delta_act(act, step):
            def silu(ct):
                act.wait_ge(S("cv_tap"), 4 * ct + 4)
                act.activation(pad[:, ct, 0:UW], pad[:, ct, 0:UW], ACT.Silu).then_inc(S("cv_silu"), 1)

            for ct in range(8):
                silu(ct)
            for c in range(4):
                emptied(act, ("cvT", c))
            act.activation(heads5(qsq), heads4(dq), ACT.Square).then_inc(S("qk_sq"), 1)
            for ct in range(8, 12):
                silu(ct)
            for c in range(4, 8):
                emptied(act, ("cvT", c))
            act.activation(heads5(ksq), heads4(dk), ACT.Square).then_inc(S("qk_sq"), 1)
            for ct in range(8, 12):
                conv_read(act, ct)
            act.wait_ge(S("qk_sum"), 2)
            act.activation(ssq, ssq, ACT.Sqrt, bias=1e-6).then_inc(S("qk_root"), 1)
            for tp in range(3):
                emptied(act, ("pR", 1, 3, tp))

            def kq_read(n):
                for d in range(2):
                    if n >= 2:
                        emptied(act, ("vs", n - 2, d, 1))
                    u = ("kq", n, d)
                    release(copy(act, buf(n, d, KT_U, 2), heads(filled(act, u))), u)

            act.wait_ge(S("dn_rows"), 1)
            kq_read(0)
            act.activation(gate, gate, ACT.Silu).then_inc(S("gate_silu"), 1)
            for n in range(5):
                for s in range(1, 6):
                    for d in range(2):
                        if s > 1:
                            filled(act, ("x", n, d, s - 1))
                        u = ("w", n, d, s)
                        release(copy(act, slot(d, WT_VN), heads(filled(act, u)[:, 0:512])), u)
                    if s == 3:
                        for d in range(2):
                            if n:
                                filled(act, ("os", n - 1, d, 1))
                            u = ("qd", n, d)
                            release(copy(act, slot(d, QD_), heads(filled(act, u)[:, 0:512])), u)
                    if n < 4 and s == 1:
                        kq_read(n + 1)
                    if n < 4 and s == 3:
                        decay_exp(act, n + 1)
                    if n >= 3 and s in (3, 4):
                        m = 2 * (n - 3) + s - 3
                        if s == 4:
                            o_root(act, 5 + m, ssq[:, 0:4])
                        o_square(act, oacc[:, DONE[n - 1][s - 3], :], dscr3)
                    if n >= 3 and s == 5:
                        o_root(act, 5 + 2 * (n - 3) + 2, ssq[:, 0:4])
                for d in range(2):
                    u = ("wu", n, d)
                    release(copy(act, buf(n, d, KT_U, 2), heads(filled(act, u))), u)
            for d in range(2):
                emptied(act, ("os", 4, d, 1))
            o_square(act, oacc[:, ST, :], dscr3)
            o_root(act, 10, ssq[:, 0:4])
            for b in range(4):
                release(copy(act, hT[:, b, :], filled(act, ("cyT", b))[:, 0:T]), ("cyT", b))

        neg = ("lo_neg", "up_neg")

        def diag(v, n, d):
            v.tensor_tensor(buf(n, d, DA_KB), over_heads(ident), per_head(gsm, tile_of(n, d), d), ALU.mult)\
                .then_inc(S("dl_diag"), 1)

        def dec_read(v, step, n, d):
            u = ("dec", n, d)
            ps = heads(filled(v, u)[:, 0:512])
            step(v.tensor_tensor(buf(n, d, DA_KB), over_heads(C[neg[d]]), ps, ALU.subtract))
            release(v.tensor_tensor(buf(n, d, DB_QK), ps, over_heads(C[neg[1 - d]]), ALU.add), u)

        def decay_sums_dve(v, step):
            mark(v).then_inc(S("dl_g"), 1)
            ps = filled(v, "G")
            step(v.tensor_copy(gsm[:, 0:120], ps[:, 0:120]))
            release(v.tensor_copy(gsm[:, 120:160], ps[:, 592:632]), "G")
            emptied(v, "G")
            v.tensor_tensor(eGL, gsm[:, 40:80], gsm[:, 0:40], ALU.subtract).then_inc(S("dl_gsm"), 1)
            step(v.memset(minus_ones, -1.0))
            for d in range(2):
                diag(v, 0, d)
            v.wait_ge(S("dl_eg"), 3)
            step(v.tensor_tensor(bG, beta, eG, ALU.mult))
            for d in range(2):
                dec_read(v, step, 0, d)

        def delta_dve(v, step):
            for ct in range(8):
                conv_read(v, ct)
            for j, x in enumerate((qsq, ksq)):
                v.wait_ge(S("qk_sq"), j + 1)
                v.tensor_reduce(ssq[:, 20 * j:20 * j + 20], x, AX_X, ALU.add).then_inc(S("qk_sum"), 1)
            for c in range(4):
                emptied(v, ("cvT", 8 + c))
            v.wait_ge(S("qk_root"), 1)
            step(v.reciprocal(ssq, ssq))
            step(v.tensor_scalar(ssq[:, 0:20], ssq[:, 0:20], P ** -0.5, None, ALU.mult))

            def unit_rows(tiles):
                for t in tiles:
                    for j, x in enumerate((dq, dk)):
                        x4 = x[:, t, :].rearrange("p (h d) -> p h d", d=P)
                        r = ssq[:, 20 * j + 4 * t:20 * j + 4 * t + 4].unsqueeze(2).broadcast_to((P, 4, P))
                        step(v.tensor_tensor(x4, x4, r, ALU.mult))
                mark(v).then_inc(S("dn_rows"), 1)

            unit_rows((0, 3))
            unit_rows((1, 2, 4))

            def o_scale(roots, t):
                v.wait_ge(S("gate_silu"), 1)
                v.wait_ge(S("o_root"), roots)
                step(v.reciprocal(ssq[:, 0:4], ssq[:, 0:4]))
                o_apply(v, step, oacc[:, t, :], ssq[:, 0:4], dng, gate[:, t, :])

            def kk_read(n, d):
                v.wait_ge(S("dl_exp"), 2 * n + d + 1)
                u = ("kk", n, d)
                ps = heads(filled(v, u))
                a = buf(n, d, DA_KB)
                step(v.tensor_tensor(a, ps[:, 0:4], a, ALU.mult))
                release(v.tensor_tensor(buf(n, d, DB_QK), ps[:, 4:8], buf(n, d, DB_QK), ALU.mult), u)
                v.tensor_tensor(a, a, per_head(beta, tile_of(n, d), d), ALU.mult).then_inc(S(f"dl_A{d}"), 1)

            def x_first(n, d):
                v.wait_ge(S(f"dl_am{d}"), 6 * n + 1)
                if n:
                    filled(v, ("wu", n - 1, d))
                u = ("am", n, d)
                ps = heads(filled(v, u)[:, 0:512])
                release(v.tensor_tensor(slot(d, XT_), over_heads(ident), ps, ALU.subtract), u)
                emptied(v, u)
                v.tensor_tensor(slot(d, X_), over_heads(ident), slot(d, AM_), ALU.subtract)\
                    .then_inc(S(f"dl_x0{d}"), 1)
                v.wait_ge(S(f"dl_x0{d}"), n + 1)

            for part in (kk_read, x_first):
                for d in range(2):
                    part(0, d)
            for n in range(5):
                for s in range(1, 6):
                    for d in range(2):
                        u = ("x", n, d, s)
                        ps = heads(filled(v, u))
                        if s < 5:
                            release(v.tensor_tensor(slot(d, X_, 2), slot(d, X_, 2), ps, ALU.subtract), u)
                        else:
                            release(v.tensor_tensor(slot(d, XT_), slot(d, XT_), ps[:, 4:8], ALU.subtract), u)
                        emptied(v, u)
                    if n < 4 and s in (1, 2, 4):
                        for d in range(2):
                            if s == 1:
                                diag(v, n + 1, d)
                            elif s == 2:
                                dec_read(v, step, n + 1, d)
                            else:
                                kk_read(n + 1, d)
                    if n >= 3 and s in (4, 5):
                        m = 2 * (n - 3) + s - 3
                        t = DONE[n - 1][s - 4]
                        o_scale(2 + m, t)
                    if n >= 3 and s in (3, 4):
                        o_sum(v, 5 + 2 * (n - 3) + s - 2, dscr3, 0)
                for ci in range(2):
                    for d in range(2):
                        c = chunk_at(ci, d)
                        r = slice(64 * c, 64 * c + 64)
                        emptied(v, ("wu", n, d))
                        u = ("vs", n, d, ci)
                        ps = heads(filled(v, u)[r, 0:512])
                        release(v.tensor_tensor(slot(d, WT_VN)[r], buf(n, d, KT_U)[r], ps, ALU.subtract), u)
                    if n < 4 and ci == 1:
                        for d in range(2):
                            x_first(n + 1, d)
                    for d in range(2):
                        c = chunk_at(ci, d)
                        r = slice(64 * c, 64 * c + 64)
                        t = tile_of(n, d)
                        u = ("os", n, d, ci)
                        ps = filled(v, u)
                        first = n < 2 if n < 4 else ci == 0
                        if first:
                            step(v.tensor_copy(oacc[r, t, :], ps[r, 0:512]))
                        else:
                            step(v.tensor_tensor(oacc[r, t, :], oacc[r, t, :], ps[r, 0:512], ALU.add))
                        v.wait_ge(S(f"dl_sd{d}"), 2 * n + ci + 1)
                        release(v.tensor_tensor(sdel[:, 4 * d:4 * d + 4, :], sdec[d], heads(ps[:, 512:1024]), ALU.add), u)
                        emptied(v, u)
                        if n == 3 and ci == 1:
                            v.memset(sdel[:, 4 * d:4 * d + 4, :], 0.0).then_inc(S("dl_zero"), 1)
            o_sum(v, 10, dscr3, 0)
            o_scale(7, ST)

        def delta_pool(g, step):
            g.wait_ge(S("dn_rows"), 1)
            r4 = lambda x: x.rearrange("p (h d) -> p h d", d=P)

            def q_decayed(n):
                g.wait_ge(S("dn_rows"), min(n, 1) + 1)
                for d in range(2):
                    t = tile_of(n, d)
                    if n:
                        filled(g, ("wu", n - 1, d))
                    g.tensor_tensor(slot(d, VB_QE), r4(dq[:, t, :]), per_head(eG, t, d), ALU.mult)\
                        .then_inc(S("dl_qd"), 1)

            def masked(n, s):
                for d in range(2):
                    if s == 0:
                        g.wait_ge(S(f"dl_A{d}"), n + 1)
                        if n:
                            filled(g, ("w", n - 1, d, 5))
                    elif s == 1:
                        g.wait_ge(S(f"dl_x0{d}"), n + 1)
                    else:
                        filled(g, ("w", n, d, s - 1))
                    g.tensor_tensor(slot(d, AM_), buf(n, d, DA_KB), over_heads(C[f"{DIRS[d]}{s}"]), ALU.mult)\
                        .then_inc(S(f"dl_am{d}"), 1)

            def state_decayed(n, ci):
                for d in range(2):
                    t = tile_of(n, d)
                    if ci:
                        emptied(g, ("os", n, d, 0))
                    elif n == 4:
                        g.wait_ge(S("dl_zero"), 2)
                    elif n:
                        emptied(g, ("os", n - 1, d, 1))
                    cd = gsm[:, 80 + 40 * chunk_at(ci, d):]
                    g.tensor_tensor(sdec[d], sdel[:, 4 * d:4 * d + 4, :], per_head(cd, t, d), ALU.mult)\
                        .then_inc(S(f"dl_sd{d}"), 1)

            q_decayed(0)
            masked(0, 0)
            for n in range(5):
                for s in range(1, 6):
                    masked(n, s)
                    for d in range(2):
                        t = tile_of(n, d)
                        if s == 1:
                            if n:
                                filled(g, ("os", n - 1, d, 1))
                            g.tensor_tensor(KX[d], r4(dk[:, t, :]), per_head(eGL, t, d), ALU.mult)\
                                .then_inc(S("dl_kx"), 1)
                        elif s == 4:
                            filled(g, ("qd", n, d))
                            step(g.tensor_tensor(slot(d, VB_QE), r4(dv[:, t, :]), per_head(beta, t, d), ALU.mult))
                for d in range(2):
                    t = tile_of(n, d)
                    g.wait_ge(S(f"dl_am{d}"), 6 * n + 6)
                    g.tensor_tensor(buf(n, d, DA_KB), r4(dk[:, t, :]), per_head(bG, t, d), ALU.mult)\
                        .then_inc(S(f"dl_kv{d}"), 1)
                if n < 4:
                    masked(n + 1, 0)
                state_decayed(n, 0)
                if n < 4:
                    q_decayed(n + 1)
                state_decayed(n, 1)
            for d in range(2):
                emptied(g, ("os", 4, d, 1))
            g.dma_start(outs["new_state_delta"][0, 0].rearrange("r h k v -> k (r h) v"), sdel[:, :, :])\
                .then_inc(S("caches"), 16)

        def layer1_outputs(g):
            g.wait_ge(S("cache_k_ready"), 2)
            g.dma_start(outs["new_cache_gqa_k"].rearrange("a b t h d -> t (a b h d)"), z2[:, ST, 528:656])\
                .then_inc(S("caches"), 16)
            g.dma_start(outs["new_cache_gqa_v"].rearrange("a b t h d -> t (a b h d)"), z2[:, ST, 656:784])\
                .then_inc(S("caches"), 16)

        def layer1_ready(pe):
            emptied(pe, ("go", len(GI) - 1))
            for b in range(4):
                emptied(pe, ("cyT", b))

        ctx.enter_context(nc.allow_non_contiguous_dma(reason="weights' column chunks"))
        block = ctx.enter_context(nc.Block())

        @block.tensor
        def _(pe):
            setup_pe(pe)
            for l in range(2):
                if l == 0:
                    mod_rows_pe(pe, 1)
                    mod_turn_pe(pe, 0)
                    norm_pe(pe, l, 0)
                    for i in range(2, 4):
                        mod_rows_pe(pe, i)
                        mod_turn_pe(pe, i - 1)
                    mod_turn_pe(pe, 3)
                for _, _, c, _ in ins[l]:
                    (proj_T_pe if c < 2 + l else proj_R_pe)(pe, l, c)
                if l == 0:
                    lru_pe(pe)
                    diff_pe(pe)
                else:
                    decay_pe(pe)
                    gqa_pe(pe)
                    delta_pe(pe)
                out_pe(pe, l)
                norm_pe(pe, l, 1)
                route_pe(pe, l)
                moe_pe(pe, l)
                if l == 0:
                    sum_pe(pe, l)

        @block.scalar
        def _(act):
            step = Steps(act, S("act_step"))
            setup_act(act, step)
            for l in range(2):
                norm_squares_act(act, l, 0)
                if l == 0:
                    mod_act(act, 1)
                norm_root_act(act, l, 0)
                if l == 0:
                    for i in range(2, 4):
                        mod_act(act, i)
                norm_shift_act(act, l, 0)
                if l == 0:
                    setup_late_dma(act)
                    act.wait_ge(S("zeroed"), 2)
                    setup_gates_dma(act)
                    setup_late_act(act, step)
                    read_T(act, 0, 0, xap, 0, True)
                    read_T(act, 0, 1, ga, 0, False)
                    gelu_act(act)
                    for c in (2, 3, 4):
                        read_R(act, 0, c, qkv[:, :, 512 * (c - 2):512 * (c - 1)], 0)
                        if c < 4:
                            diff_rows_act(act, c - 2)
                    lru_act(act, step)
                    diff_act(act, step)
                else:
                    read_R(act, 1, 4, z2[:, :, 0:512], 0)
                    read_R(act, 1, 5, z2[:, :, 512:784], 0)
                    for c in range(3):
                        gqa_rows_act(act, step, c)
                        read_T(act, 1, c, pad[:, 4 * c:4 * c + 4, :], 0, True)
                    read_R(act, 1, 3, gate, 0)
                    filled(act, ("pR", 1, 3, 2))
                    decay_act(act)
                    gqa_act(act, step)
                    delta_act(act, step)
                norm_squares_act(act, l, 1)
                norm_root_act(act, l, 1)
                if l == 0:
                    mod_act(act, 12 + N_DIFF_MODS)
                norm_shift_act(act, l, 1)
                route_act(act, step, l)
                moe_act_run(act, l)
                if l == 0:
                    gather_sum_act(act, l)
            y_load(act)

        @block.vector
        def _(v):
            step = Steps(v, S("dve_step"))
            setup_dve(v, step)
            for l in range(2):
                if l == 0:
                    for k in range(1, KD):
                        norm_add(v, 0, 0, k)
                    mod_dve(v, step, 0)
                norm_rstd_dve(v, step, l, 0)
                if l == 0:
                    for i in range(1, 4):
                        mod_dve(v, step, i)
                    mods_done(v, 3)
                norm_scale_dve(v, l, 0)
                if l == 0:
                    setup_late_dve(v, step)
                    pads_dve(v, step, xap)
                    read_T(v, 0, 0, xap, 1, True)
                    read_T(v, 0, 1, ga, 1, False)
                    lru_conv_dve(v, step)
                    for c in (2, 3, 4):
                        read_R(v, 0, c, qkv[:, :, 512 * (c - 2):512 * (c - 1)], 1)
                        if c < 4:
                            diff_rows_dve(v, step, c - 2)
                    lru_dve(v, step)
                    diff_dve(v, step)
                else:
                    pads_dve(v, step, pad)
                    read_R(v, 1, 4, z2[:, :, 0:512], 1)
                    read_R(v, 1, 5, z2[:, :, 512:784], 1)
                    for c in range(3):
                        if c == 0:
                            decay_dve(v, step)
                        else:
                            gqa_rows_dve(v, step, c)
                        read_T(v, 1, c, pad[:, 4 * c:4 * c + 4, :], 1, True)
                    read_R(v, 1, 3, gate, 1)
                    decay_sums_dve(v, step)
                    gqa_dve(v, step)
                    delta_dve(v, step)
                if l == 0:
                    mods_done(v, 11)
                residual_dve(v, step, l, "out")
                norm_rstd_dve(v, step, l, 1)
                norm_scale_dve(v, l, 1)
                route_dve(v, step, l)
                moe_dve(v, l)
                if l == 0:
                    mod_dve(v, step, 23)
                    residual_dve(v, step, l, "ms")
            y_rows(v, step, Y_TILES["dve"])

        @block.gpsimd
        def _(g):
            step = Steps(g, S("pool_step"))
            setup_pool(g)
            layer0_outputs(g)
            route_pool(g, 0)
            moe_pool(g, 0)
            layer1_outputs(g)
            delta_pool(g, step)
            route_pool(g, 1)
            moe_pool(g, 1)
            y_rows(g, step, Y_TILES["pool"])

        @block.sync
        def _(sp):
            load_stream(sp)
            store_sp(sp, 6)


_PLAIN = ["x_prompt", "x_sample", "cache_diff_k", "cache_diff_v", "state_delta", "cache_gqa_k", "cache_gqa_v",
          "w_mod", "w_in_ab", "lru_wa", "lru_wi", "w_in_cd", "w_out", "router_w", "exp_w1", "exp_w3", "exp_w2"]
_OUTS = {"y_prompt": (1, 128, 1024), "y_sample": (1, 512, 1024), "new_state_lru": (1, 1, 2, 512),
         "new_cache_diff_k": (1, 1, 128, 4, 2, 64), "new_cache_diff_v": (1, 1, 128, 4, 128),
         "new_state_delta": (1, 1, 2, 4, 128, 128), "new_cache_gqa_k": (1, 1, 128, 2, 64),
         "new_cache_gqa_v": (1, 1, 128, 2, 64)}


def layout(inputs):
    import numpy as np
    a = {k: np.ascontiguousarray(inputs[k]) for k in _PLAIN}
    r = lambda k: np.asarray(inputs[k]).reshape(-1, P)
    a["colsA"] = np.concatenate([r(k) for k in ("norm1_g", "norm2_g", "b_mod")])
    a["colsB"] = np.concatenate([r(k) for k in ("c", "c_ctx", "lru_conv_b", "lru_ba", "lru_bi", "lru_lam", "state_lru",
                                                "lru_conv_w", "delta_conv_w")])
    a["params"] = np.concatenate([np.asarray(inputs[k]).reshape(1, -1) for k in
                                  ("diff_q_gain", "diff_k_gain", "gqa_q_gain", "gqa_k_gain", "diff_sub_gain",
                                   "delta_norm_g", "delta_a_log", "delta_dt_bias", "diff_lam")], axis=1)
    t = np.arange(NS)
    inv = (10000.0 ** (-np.arange(16, dtype=np.float32) / 16)).astype(np.float32)
    ang = np.concatenate([(t // 64).astype(np.float32)[:, None] * inv, (t % 64).astype(np.float32)[:, None] * inv], 1)
    a["rope"] = np.concatenate([np.cos(ang), np.sin(ang)], 1).astype(np.float32)
    i, j = np.arange(P)[:, None], np.arange(P)[None, :]
    same = i // CK == j // CK
    lo, up = same & (j <= i), same & (j >= i)
    c = [i == j, i >= 0 * j, np.where(lo, 0.0, NEG), np.where(up, 0.0, NEG), lo, up, same]
    lev = [(i // (2 << s) == j // (2 << s)) & (i // (1 << s) > j // (1 << s)) for s in range(6)]
    c += lev + [m.T for m in lev]
    a["consts"] = np.stack([np.broadcast_to(m, (P, P)).astype(np.float32) for m in c])
    return a


def program(nc, arrays):
    io = {k: nc.dram_tensor("in_" + k, v.shape, F32, kind="ExternalInput").ap() for k, v in arrays.items()}
    outs = {k: nc.dram_tensor("out_" + k, s, F32, kind="ExternalOutput").ap() for k, s in _OUTS.items()}
    build(nc, io, outs)


def kernel(**inputs):
    import concourse.bacc as _bacc
    from concourse.bass_utils import run_bass_kernel_spmd as _run
    arrays = layout(inputs)
    nc = _bacc.Bacc("TRN2", target_bir_lowering=False, num_devices=1)
    program(nc, arrays)
    r = _run(nc, [{"in_" + k: v for k, v in arrays.items()}], core_ids=[0])
    return tuple(r.results[0]["out_" + k] for k in _OUTS)
```
